# Optimizing a Trainium2 kernel written in Bass

```python
import jax, jax.numpy as jnp
from jax import lax
import numpy as np

D_MODEL = 1024
BATCH = 1
SEQ = 512
DEPTH = 2
DEC_BATCH = 1
DEC_SEQ = 32
PAST_LEN = 256

CHUNK = 64
CONV_W = 4
N_A = (DEPTH + 1) // 2
N_C = DEPTH // 2
NORM_EPS = 1e-6
LRU_WIDTH = D_MODEL // 2
LRU_HEADS = 8
LRU_BLOCK = LRU_WIDTH // LRU_HEADS
LRU_C = 8.0
RET_HEADS = 4
RET_DK = D_MODEL // 8
RET_DV = D_MODEL // 8
ROPE_BASE = 10000.0
GLA_HEADS = 4
GLA_DK = D_MODEL // 16
GLA_DV = D_MODEL // 8
GLA_RANK = 16
GLA_TAU = 16.0
MLSTM_HEADS = 4
MLSTM_DH = D_MODEL // 8
MLSTM_WIDTH = MLSTM_HEADS * MLSTM_DH
D_FF = -(-8 * D_MODEL // (3 * 256)) * 256
EVEN_SPLITS = [LRU_WIDTH, LRU_WIDTH, RET_HEADS * RET_DK, RET_HEADS * RET_DK,
               RET_HEADS * RET_DV, RET_HEADS * RET_DV]
EVEN_IN = sum(EVEN_SPLITS)
EVEN_OUT = LRU_WIDTH + RET_HEADS * RET_DV
ODD_SPLITS = [GLA_HEADS * GLA_DK, GLA_HEADS * GLA_DK, GLA_HEADS * GLA_DV, GLA_RANK,
              GLA_HEADS * GLA_DV, MLSTM_WIDTH, MLSTM_WIDTH, MLSTM_HEADS, MLSTM_HEADS]
ODD_IN = sum(ODD_SPLITS)
ODD_OUT = GLA_HEADS * GLA_DV + MLSTM_WIDTH
STATE_KEYS = ('lru_h', 'lru_conv', 'ret', 'gla', 'mlstm_C', 'mlstm_n', 'mlstm_m', 'mlstm_conv')

kernel_name = 'hybrid_streaming_encoder_step'

def _rms_norm(x, g):
    xf = x.astype(jnp.float32)
    y = xf * lax.rsqrt(jnp.mean(xf * xf, axis=-1, keepdims=True) + NORM_EPS)
    return (y * g.astype(jnp.float32)).astype(x.dtype)

def _head_norm(x, g):
    xf = x.astype(jnp.float32)
    xc = xf - jnp.mean(xf, axis=-1, keepdims=True)
    y = xc * lax.rsqrt(jnp.mean(xc * xc, axis=-1, keepdims=True) + NORM_EPS)
    return y.reshape(x.shape[:2] + (-1,)) * g.astype(jnp.float32)

def _split(z, sizes):
    return jnp.split(z, np.cumsum(sizes)[:-1].tolist(), axis=-1)

def _to_chunks(t, L):
    b, T = t.shape[0], t.shape[1]
    return jnp.swapaxes(t.reshape((b, T // L, L) + t.shape[2:]), 0, 1)

def _from_chunks(t):
    t = jnp.swapaxes(t, 0, 1)
    return t.reshape((t.shape[0], t.shape[1] * t.shape[2]) + t.shape[3:])

def _causal_dwconv(u, buf, w, b):
    T = u.shape[1]
    up = jnp.concatenate([buf.astype(u.dtype), u], axis=1)
    out = b + w[0] * up[:, 0:T]
    for tap in range(1, CONV_W):
        out = out + w[tap] * up[:, tap:tap + T]
    return out, up[:, T:]

def _rotary(x, pos):
    half = x.shape[-1] // 2
    inv = ROPE_BASE ** (-jnp.arange(half, dtype=jnp.float32) / half)
    ang = pos.astype(jnp.float32)[:, None] * inv[None, :]
    cos = jnp.cos(ang)[None, :, None, :]
    sin = jnp.sin(ang)[None, :, None, :]
    x1, x2 = x[..., :half], x[..., half:]
    return jnp.concatenate([x1 * cos - x2 * sin, x1 * sin + x2 * cos], axis=-1)

def _rglru(xc, h0, gate_w, gate_b, lam):
    B, T, W = xc.shape
    gates = jnp.einsum('bthi,hij->bthj', xc.reshape(B, T, LRU_HEADS, LRU_BLOCK), gate_w) + gate_b
    r = jax.nn.sigmoid(gates[..., :LRU_BLOCK]).reshape(B, T, W)
    i = jax.nn.sigmoid(gates[..., LRU_BLOCK:]).reshape(B, T, W)
    log_a = -LRU_C * r * jax.nn.softplus(-lam)
    a = jnp.exp(log_a)
    b = jnp.sqrt(-jnp.expm1(2.0 * log_a)) * (i * xc)
    b = b.at[:, 0].add(a[:, 0] * h0)

    def combine(left, right):
        return left[0] * right[0], right[0] * left[1] + right[1]

    _, h = lax.associative_scan(combine, (a, b), axis=1)
    return h, h[:, -1]

def _retention(q, k, v, S0):
    B, T, H, _ = q.shape
    L = min(CHUNK, T)
    log_g = jnp.log1p(-jnp.exp2(-5.0 - jnp.arange(H, dtype=jnp.float32)))
    idx = jnp.arange(L, dtype=jnp.float32)
    diff = idx[:, None] - idx[None, :]
    decay = jnp.where(diff >= 0, jnp.exp(jnp.maximum(diff, 0.0)[None] * log_g[:, None, None]), 0.0)
    q_dec = jnp.exp((idx[:, None] + 1.0) * log_g[None, :])
    k_dec = jnp.exp((L - 1.0 - idx)[:, None] * log_g[None, :])
    s_dec = jnp.exp(L * log_g)

    def step(S, inp):
        qc, kc, vc = inp
        att = jnp.einsum('blhd,bshd->bhls', qc, kc) * decay
        o = (jnp.einsum('bhls,bshe->blhe', att, vc)
             + jnp.einsum('blhd,bhde->blhe', qc, S) * q_dec[None, :, :, None])
        S = s_dec[None, :, None, None] * S + jnp.einsum('bshd,bshe->bhde', kc * k_dec[None, :, :, None], vc)
        return S, o

    S, o = lax.scan(step, S0.astype(jnp.float32), (_to_chunks(q, L), _to_chunks(k, L), _to_chunks(v, L)))
    return _from_chunks(o), S

def _gla(q, k, v, log_alpha, S0):
    B, T, H, _ = q.shape
    L = min(CHUNK, T)
    causal = jnp.tril(jnp.ones((L, L), dtype=bool))

    def step(S, inp):
        qc, kc, vc, lac = inp
        cum = jnp.cumsum(lac, axis=1)
        last = cum[:, -1:]
        ref = 0.5 * last
        att = jnp.einsum('blhd,bshd->bhls', qc * jnp.exp(cum - ref), kc * jnp.exp(ref - cum))
        att = jnp.where(causal, att, 0.0)
        o = (jnp.einsum('bhls,bshe->blhe', att, vc)
             + jnp.einsum('blhd,bhde->blhe', qc * jnp.exp(cum), S))
        S = jnp.exp(last[:, 0])[..., None] * S + jnp.einsum('bshd,bshe->bhde', kc * jnp.exp(last - cum), vc)
        return S, o

    S, o = lax.scan(step, S0.astype(jnp.float32),
                    (_to_chunks(q, L), _to_chunks(k, L), _to_chunks(v, L), _to_chunks(log_alpha, L)))
    return _from_chunks(o), S

def _mlstm(q, k, v, log_i, log_f, C0, n0, m0):
    B, T, H, _ = q.shape
    L = min(CHUNK, T)
    causal = jnp.tril(jnp.ones((L, L), dtype=bool))

    def step(carry, inp):
        C, n, m = carry
        qc, kc, vc, ic, fc = inp
        b = jnp.cumsum(fc, axis=1)
        a = b + m[:, None, :]
        dlog = b[:, :, None, :] - b[:, None, :, :] + ic[:, None, :, :]
        dlog = jnp.where(causal[None, :, :, None], dlog, -jnp.inf)
        m_t = jnp.maximum(a, jnp.max(dlog, axis=2))
        w = jnp.exp(dlog - m_t[:, :, None, :])
        w_in = jnp.exp(a - m_t)
        qk = jnp.einsum('blhd,bshd->blsh', qc, kc) * w
        num = (jnp.einsum('blsh,bshe->blhe', qk, vc)
               + w_in[..., None] * jnp.einsum('blhd,bhde->blhe', qc, C))
        den = jnp.sum(qk, axis=2) + w_in * jnp.einsum('blhd,bhd->blh', qc, n)
        hc = num / jnp.maximum(jnp.abs(den), jnp.exp(-m_t))[..., None]
        w_last = w[:, -1]
        C = w_in[:, -1, :, None, None] * C + jnp.einsum('bsh,bshd,bshe->bhde', w_last, kc, vc)
        n = w_in[:, -1, :, None] * n + jnp.einsum('bsh,bshd->bhd', w_last, kc)
        return (C, n, m_t[:, -1]), hc

    xs = tuple(_to_chunks(t, L) for t in (q, k, v, log_i, log_f))
    (C, n, m), h = lax.scan(step, (C0.astype(jnp.float32), n0.astype(jnp.float32), m0.astype(jnp.float32)), xs)
    return _from_chunks(h), C, n, m

def _even_mixer(h, pos, P, j, h0, conv0, S0):
    B, T, _ = h.shape
    z = (h @ P['a_w_in'][j]).astype(jnp.float32)
    xb, gb, q, k, v, g = _split(z, EVEN_SPLITS)
    xc, conv_new = _causal_dwconv(xb, conv0, P['lru_conv_w'][j], P['lru_conv_b'][j])
    hs, h_last = _rglru(xc, h0.astype(jnp.float32), P['lru_gate_w'][j], P['lru_gate_b'][j], P['lru_lambda'][j])
    out_a = jax.nn.gelu(gb) * hs
    q = _rotary(q.reshape(B, T, RET_HEADS, RET_DK), pos)
    k = _rotary(k.reshape(B, T, RET_HEADS, RET_DK), pos) * (RET_DK ** -0.5)
    v = v.reshape(B, T, RET_HEADS, RET_DV)
    o, S_new = _retention(q, k, v, S0)
    out_b = jax.nn.silu(g) * _head_norm(o, P['ret_gn_g'][j])
    y = jnp.concatenate([out_a, out_b], axis=-1).astype(h.dtype) @ P['a_w_out'][j]
    return y, h_last, conv_new, S_new

def _odd_mixer(h, P, j, S0, C0, n0, m0, conv0):
    B, T, _ = h.shape
    z = (h @ P['c_w_in'][j]).astype(jnp.float32)
    gq, gk, gv, glr, gr, u, o_pre, i_pre, f_pre = _split(z, ODD_SPLITS)
    log_alpha = jax.nn.log_sigmoid(glr @ P['gla_w_gate'][j] + P['gla_b_gate'][j]) / GLA_TAU
    o_c, S_new = _gla(gq.reshape(B, T, GLA_HEADS, GLA_DK),
                      gk.reshape(B, T, GLA_HEADS, GLA_DK) * (GLA_DK ** -0.5),
                      gv.reshape(B, T, GLA_HEADS, GLA_DV),
                      log_alpha.reshape(B, T, GLA_HEADS, GLA_DK), S0)
    out_c = jax.nn.silu(gr) * _head_norm(o_c, P['gla_gn_g'][j])
    uc, conv_new = _causal_dwconv(u, conv0, P['mlstm_conv_w'][j], P['mlstm_conv_b'][j])
    uc = jax.nn.silu(uc)
    qk = jnp.einsum('bthi,hij->bthj', uc.reshape(B, T, MLSTM_HEADS, MLSTM_DH), P['mlstm_w_qk'][j])
    mv = jnp.einsum('bthi,hij->bthj', u.reshape(B, T, MLSTM_HEADS, MLSTM_DH), P['mlstm_w_v'][j])
    b_if = P['mlstm_b_if'][j]
    hm, C_new, n_new, m_new = _mlstm(qk[..., :MLSTM_DH], qk[..., MLSTM_DH:] * (MLSTM_DH ** -0.5), mv,
                                     i_pre + b_if[:MLSTM_HEADS],
                                     jax.nn.log_sigmoid(f_pre + b_if[MLSTM_HEADS:]), C0, n0, m0)
    out_d = jax.nn.sigmoid(o_pre) * _head_norm(hm, P['mlstm_gn_g'][j])
    y = jnp.concatenate([out_c, out_d], axis=-1).astype(h.dtype) @ P['c_w_out'][j]
    return y, S_new, C_new, n_new, m_new, conv_new

def _swiglu(h, w_in, w_out):
    gu = h @ w_in
    return (jax.nn.silu(gu[..., :D_FF]) * gu[..., D_FF:]) @ w_out

def _trunk(x, c, st, P, pos0):
    T = x.shape[1]
    pos = pos0 + jnp.arange(T, dtype=jnp.int32)
    cs = jax.nn.silu(c)
    new = {name: [] for name in STATE_KEYS}
    for l in range(DEPTH):
        mod = cs @ P['w_mod'][l] + P['b_mod'][l]
        sh1, sc1, g1, sh2, sc2, g2 = jnp.split(mod[:, None, :], 6, axis=-1)
        hn = _rms_norm(x, P['norm_mix_g'][l]) * (1.0 + sc1) + sh1
        j = l // 2
        if l % 2 == 0:
            y, h_new, lconv_new, ret_new = _even_mixer(hn, pos, P, j, st['lru_h'][j], st['lru_conv'][j], st['ret'][j])
            new['lru_h'].append(h_new)
            new['lru_conv'].append(lconv_new)
            new['ret'].append(ret_new)
        else:
            y, gla_new, C_new, n_new, m_new, mconv_new = _odd_mixer(
                hn, P, j, st['gla'][j], st['mlstm_C'][j], st['mlstm_n'][j], st['mlstm_m'][j], st['mlstm_conv'][j])
            new['gla'].append(gla_new)
            new['mlstm_C'].append(C_new)
            new['mlstm_n'].append(n_new)
            new['mlstm_m'].append(m_new)
            new['mlstm_conv'].append(mconv_new)
        x = x + g1 * y
        hn = _rms_norm(x, P['norm_ffn_g'][l]) * (1.0 + sc2) + sh2
        x = x + g2 * _swiglu(hn, P['w_ffn_in'][l], P['w_ffn_out'][l])
    y = _rms_norm(x, P['final_norm_g'])
    return y, {name: jnp.stack(vals) for name, vals in new.items()}

def _zero_states(nb):
    f32 = jnp.float32
    return {
        'lru_h': jnp.zeros((N_A, nb, LRU_WIDTH), f32),
        'lru_conv': jnp.zeros((N_A, nb, CONV_W - 1, LRU_WIDTH), f32),
        'ret': jnp.zeros((N_A, nb, RET_HEADS, RET_DK, RET_DV), f32),
        'gla': jnp.zeros((N_C, nb, GLA_HEADS, GLA_DK, GLA_DV), f32),
        'mlstm_C': jnp.zeros((N_C, nb, MLSTM_HEADS, MLSTM_DH, MLSTM_DH), f32),
        'mlstm_n': jnp.zeros((N_C, nb, MLSTM_HEADS, MLSTM_DH), f32),
        'mlstm_m': jnp.zeros((N_C, nb, MLSTM_HEADS), f32),
        'mlstm_conv': jnp.zeros((N_C, nb, CONV_W - 1, MLSTM_WIDTH), f32),
    }

def setup_inputs(seed: int = 0) -> dict:
    key = jax.random.key(seed)
    keys = iter(jax.random.split(key, 64))
    f32 = jnp.float32

    def nrm(shape, scale):
        return jax.random.normal(next(keys), shape, f32) * scale

    def gain(shape):
        return 1.0 + nrm(shape, 0.02)

    u = jax.random.uniform(next(keys), (N_A, LRU_WIDTH), f32, 0.9, 0.999)
    a = u ** (1.0 / LRU_C)
    lru_lambda = jnp.log(a) - jnp.log1p(-a)
    b_forget = jnp.linspace(3.0, 6.0, MLSTM_HEADS, dtype=f32)[None, :] + nrm((N_C, MLSTM_HEADS), 0.1)
    mlstm_b_if = jnp.concatenate([nrm((N_C, MLSTM_HEADS), 0.1), b_forget], axis=-1)
    return {
        'x_prompt': nrm((BATCH, SEQ, D_MODEL), 1.0),
        'x_sample': nrm((DEC_BATCH, DEC_SEQ, D_MODEL), 1.0),
        'c_prompt': nrm((BATCH, D_MODEL), 1.0),
        'c_sample': nrm((DEC_BATCH, D_MODEL), 1.0),
        'state_lru_h': nrm((N_A, DEC_BATCH, LRU_WIDTH), 0.5),
        'state_lru_conv': nrm((N_A, DEC_BATCH, CONV_W - 1, LRU_WIDTH), 1.0),
        'state_ret': nrm((N_A, DEC_BATCH, RET_HEADS, RET_DK, RET_DV), 1.0),
        'state_gla': nrm((N_C, DEC_BATCH, GLA_HEADS, GLA_DK, GLA_DV), 1.0),
        'state_mlstm_C': nrm((N_C, DEC_BATCH, MLSTM_HEADS, MLSTM_DH, MLSTM_DH), 0.5),
        'state_mlstm_n': nrm((N_C, DEC_BATCH, MLSTM_HEADS, MLSTM_DH), 0.5),
        'state_mlstm_m': nrm((N_C, DEC_BATCH, MLSTM_HEADS), 1.0),
        'state_mlstm_conv': nrm((N_C, DEC_BATCH, CONV_W - 1, MLSTM_WIDTH), 1.0),
        'w_mod': nrm((DEPTH, D_MODEL, 6 * D_MODEL), 0.5 * D_MODEL ** -0.5),
        'b_mod': nrm((DEPTH, 6 * D_MODEL), 0.02),
        'norm_mix_g': gain((DEPTH, D_MODEL)),
        'norm_ffn_g': gain((DEPTH, D_MODEL)),
        'w_ffn_in': nrm((DEPTH, D_MODEL, 2 * D_FF), D_MODEL ** -0.5),
        'w_ffn_out': nrm((DEPTH, D_FF, D_MODEL), D_FF ** -0.5),
        'final_norm_g': gain((D_MODEL,)),
        'a_w_in': nrm((N_A, D_MODEL, EVEN_IN), D_MODEL ** -0.5),
        'a_w_out': nrm((N_A, EVEN_OUT, D_MODEL), EVEN_OUT ** -0.5),
        'lru_conv_w': nrm((N_A, CONV_W, LRU_WIDTH), CONV_W ** -0.5),
        'lru_conv_b': nrm((N_A, LRU_WIDTH), 0.02),
        'lru_gate_w': nrm((N_A, LRU_HEADS, LRU_BLOCK, 2 * LRU_BLOCK), LRU_BLOCK ** -0.5),
        'lru_gate_b': nrm((N_A, LRU_HEADS, 2 * LRU_BLOCK), 0.02),
        'lru_lambda': lru_lambda,
        'ret_gn_g': gain((N_A, RET_HEADS * RET_DV)),
        'c_w_in': nrm((N_C, D_MODEL, ODD_IN), D_MODEL ** -0.5),
        'c_w_out': nrm((N_C, ODD_OUT, D_MODEL), ODD_OUT ** -0.5),
        'gla_w_gate': nrm((N_C, GLA_RANK, GLA_HEADS * GLA_DK), GLA_RANK ** -0.5),
        'gla_b_gate': nrm((N_C, GLA_HEADS * GLA_DK), 0.02),
        'gla_gn_g': gain((N_C, GLA_HEADS * GLA_DV)),
        'mlstm_conv_w': nrm((N_C, CONV_W, MLSTM_WIDTH), CONV_W ** -0.5),
        'mlstm_conv_b': nrm((N_C, MLSTM_WIDTH), 0.02),
        'mlstm_w_qk': nrm((N_C, MLSTM_HEADS, MLSTM_DH, 2 * MLSTM_DH), MLSTM_DH ** -0.5),
        'mlstm_w_v': nrm((N_C, MLSTM_HEADS, MLSTM_DH, MLSTM_DH), MLSTM_DH ** -0.5),
        'mlstm_b_if': mlstm_b_if,
        'mlstm_gn_g': gain((N_C, MLSTM_WIDTH)),
    }

def reference(x_prompt, x_sample, c_prompt, c_sample,
              state_lru_h, state_lru_conv, state_ret, state_gla,
              state_mlstm_C, state_mlstm_n, state_mlstm_m, state_mlstm_conv,
              w_mod, b_mod, norm_mix_g, norm_ffn_g, w_ffn_in, w_ffn_out, final_norm_g,
              a_w_in, a_w_out, lru_conv_w, lru_conv_b, lru_gate_w, lru_gate_b, lru_lambda, ret_gn_g,
              c_w_in, c_w_out, gla_w_gate, gla_b_gate, gla_gn_g,
              mlstm_conv_w, mlstm_conv_b, mlstm_w_qk, mlstm_w_v, mlstm_b_if, mlstm_gn_g):
    P = {
        'w_mod': w_mod, 'b_mod': b_mod, 'norm_mix_g': norm_mix_g, 'norm_ffn_g': norm_ffn_g,
        'w_ffn_in': w_ffn_in, 'w_ffn_out': w_ffn_out, 'final_norm_g': final_norm_g,
        'a_w_in': a_w_in, 'a_w_out': a_w_out, 'lru_conv_w': lru_conv_w, 'lru_conv_b': lru_conv_b,
        'lru_gate_w': lru_gate_w, 'lru_gate_b': lru_gate_b, 'lru_lambda': lru_lambda, 'ret_gn_g': ret_gn_g,
        'c_w_in': c_w_in, 'c_w_out': c_w_out, 'gla_w_gate': gla_w_gate, 'gla_b_gate': gla_b_gate,
        'gla_gn_g': gla_gn_g, 'mlstm_conv_w': mlstm_conv_w, 'mlstm_conv_b': mlstm_conv_b,
        'mlstm_w_qk': mlstm_w_qk, 'mlstm_w_v': mlstm_w_v, 'mlstm_b_if': mlstm_b_if, 'mlstm_gn_g': mlstm_gn_g,
    }
    y_prompt, sp = _trunk(x_prompt, c_prompt, _zero_states(x_prompt.shape[0]), P, 0)
    past = {
        'lru_h': state_lru_h, 'lru_conv': state_lru_conv, 'ret': state_ret, 'gla': state_gla,
        'mlstm_C': state_mlstm_C, 'mlstm_n': state_mlstm_n, 'mlstm_m': state_mlstm_m,
        'mlstm_conv': state_mlstm_conv,
    }
    y_sample, ss = _trunk(x_sample, c_sample, past, P, PAST_LEN)
    return (y_prompt, y_sample,
            sp['lru_h'], sp['lru_conv'], sp['ret'], sp['gla'],
            sp['mlstm_C'], sp['mlstm_n'], sp['mlstm_m'], sp['mlstm_conv'],
            ss['lru_h'], ss['lru_conv'], ss['ret'], ss['gla'],
            ss['mlstm_C'], ss['mlstm_n'], ss['mlstm_m'], ss['mlstm_conv'])


_drawn_inputs = setup_inputs


def setup_inputs(seed=0):
    import zlib

    import numpy as np

    out = dict(_drawn_inputs(seed))
    spreads = {}
    factors = {'norm_ffn_g': 6.828,
     'final_norm_g': 2.743,
     'lru_gate_b': 7.599,
     'ret_gn_g': 8.0,
     'gla_b_gate': 5.389,
     'gla_gn_g': 8.0,
     'mlstm_gn_g': 8.0}
    for name, (base, spread) in spreads.items():
        noise = np.random.default_rng([zlib.crc32(name.encode()), seed]).standard_normal(out[name].shape)
        drawn = base * np.exp(spread * noise) if base else spread * noise
        out[name] = __import__('jax').numpy.asarray(drawn.astype(out[name].dtype))
    for name, factor in factors.items():
        out[name] = (out[name] * factor).astype(out[name].dtype)
    return out
```

```python
from contextlib import ExitStack

import numpy as np

import concourse.bass as bass
import concourse.mybir as mybir

F32 = mybir.dt.float32
F32R = mybir.dt.float32r
U32 = mybir.dt.uint32
ACT = mybir.ActivationFunctionType
ALU = mybir.AluOpType
ds = bass.ds

P = 128
D = 1024
KD = D // P
TP, TS = 512, 32
T = TP + TS
HALF = T // 2
CONV = 4
PAD = CONV - 1
TC = T + PAD + 1
SC = TP + PAD
DEPTH = 2
DFF = 2816
FFN_CUTS = (8, 8, 6)
HEADS = 4
NB = TP // P
MOD_TILES = 6 * KD
EPS = 1e-6
BIG = 1e30

RET_SCALE = float(P) ** -0.5
GLA_SCALE = float(64) ** -0.5
GLA_TAU = 16.0
GELU_A, GELU_B = 0.7978845608028654, 0.044715

C_ID, C_COS, C_SIN = 0, P, P + T
C_DEC = C_SIN + T
C_QD = C_DEC + HEADS * P
C_KD = C_QD + HEADS * P
C_SD = C_KD + 2 * HEADS
C_NEG = C_SD + 2 * HEADS
C_MASK = C_NEG + P
C_ALL = C_MASK + P
AREA_ALL = 16400

R1 = {}
R2 = {}
_n = 0
for _name, _k in (("norm_mix_g", 16), ("norm_ffn_g", 16), ("final_norm_g", 8), ("lru_conv_w", 16),
                  ("lru_conv_b", 4), ("lru_gate_b", 8), ("lru_lambda", 4), ("ret_gn_g", 4),
                  ("state_lru_h", 4), ("state_lru_conv", 12), ("c_prompt", 8), ("c_sample", 8)):
    R1[_name] = _n
    _n += _k
R1_ALL = _n
_n = 0
for _name, _k in (("gla_b_gate", 2), ("gla_gn_g", 4), ("mlstm_conv_w", 16), ("mlstm_conv_b", 4),
                  ("mlstm_gn_g", 4), ("state_mlstm_conv", 12), ("state_mlstm_n", 4)):
    R2[_name] = _n
    _n += _k
R2_ALL = _n
MOD_ROWS = DEPTH * MOD_TILES

A_ORDER = (("k", 1536), ("q", 1024), ("v", 2048), ("xb", 0), ("g", 2560), ("gb", 512))


def constants():
    c = np.zeros((P, C_ALL), np.float32)
    c[:, C_ID:C_ID + P] = np.eye(P)
    half = P // 2
    inv = np.float32(10000.0) ** (-np.arange(half, dtype=np.float32) / np.float32(half))
    pos = np.concatenate([np.arange(TP), 256 + np.arange(TS)]).astype(np.float32)
    ang = (pos[None, :] * inv.astype(np.float32)[:, None]).astype(np.float32).astype(np.float64)
    c[:half, C_COS:C_COS + T] = c[half:, C_COS:C_COS + T] = np.cos(ang)
    c[:half, C_SIN:C_SIN + T] = np.sin(ang)
    c[half:, C_SIN:C_SIN + T] = -np.sin(ang)
    lg = np.log1p(-np.exp2(-5.0 - np.arange(HEADS))).astype(np.float32).astype(np.float64)
    s, l = np.arange(P)[:, None], np.arange(P)[None, :]
    for h in range(HEADS):
        c[:, C_DEC + h * P:C_DEC + (h + 1) * P] = np.where(l >= s, np.exp((l - s) * lg[h]), 0) * RET_SCALE
        c[:, C_QD + h * P:C_QD + (h + 1) * P] = np.exp((l + 1) * lg[h])
        c[:, C_KD + 2 * h] = np.exp((P - 1 - np.arange(P)) * lg[h]) * RET_SCALE
        c[:TS, C_KD + 2 * h + 1] = np.exp((TS - 1 - np.arange(TS)) * lg[h]) * RET_SCALE
        c[:, C_SD + 2 * h] = np.exp(P * lg[h])
        c[:, C_SD + 2 * h + 1] = np.exp(TS * lg[h])
    c[:, C_NEG:C_NEG + P] = np.where(l >= s, 0.0, -BIG)
    c[:, C_MASK:C_MASK + P] = (l >= s) & (l // 64 == s // 64)
    return c


def selectors():
    s = np.zeros((HEADS, HEADS, P), np.float32)
    for h in range(HEADS):
        s[h, h] = 1.0
    return s


ACT_HEAD, DVE_HEAD, ACT_PAIR, DVE_PAIR, ACT_ML, DVE_ML = 11, 29, 12, 41, 14, 26 


class Turn:

    def __init__(self, base, j=0, per=0, i=0):
        self.slot = (base + j) % 2
        self.before = (base + j) // 2 + (per // 2) * i
        self.index = base + j + per * i


class Steps:

    def __init__(self, eng, sem):
        self.eng, self.sem, self.n, self.i, self.per = eng, sem, 0, 0, 0

    def loop(self, i, per):
        self.i, self.per, self.start = i, per, self.n

    def end(self, count):
        assert self.n - self.start == self.per, self.n - self.start
        self.n, self.i, self.per = self.start + self.per * count, 0, 0

    def add(self, ins):
        ins.then_inc(self.sem, 1)
        self.n += 1

    def wait(self):
        self.eng.wait_ge(self.sem, self.n + self.per * self.i if self.per else self.n)

    def done(self, ins):
        self.add(ins)
        self.wait()


def encoder(nc, t, out):
    with ExitStack() as ctx:
        def sb(name, shape, dt=F32):
            return ctx.enter_context(nc.sbuf_tensor(name, shape, dt))

        def sem(name):
            return ctx.enter_context(nc.semaphore(name))

        CST = sb("constants", [P, C_ALL])
        IDENT = CST[:, C_ID:C_ID + P]
        COS, SIN = CST[:, C_COS:C_COS + T], CST[:, C_SIN:C_SIN + T]
        DECAY = CST[:, C_DEC:C_DEC + HEADS * P].rearrange("p (h l) -> p h l", h=HEADS)
        QDEC = CST[:, C_QD:C_QD + HEADS * P].rearrange("p (h l) -> p h l", h=HEADS)
        NEG = CST[:, C_NEG:C_NEG + P]
        CHUNK_MASK = CST[:, C_MASK:C_MASK + P].bitcast(U32)
        ONES = sb("ones", [P, P])
        MEAN = sb("mean_matrix", [P, P])
        EPSC = sb("eps_column", [P, 1])
        ROWS = sb("param_rows", [P, 3, P])
        COLS = sb("param_columns", [P, MOD_ROWS + R1_ALL + R2_ALL])
        BMOD = COLS[:, 0:MOD_ROWS]
        IF_BIAS = sb("if_bias", [HEADS, 2])
        M0 = sb("m_state", [HEADS, 1])

        def col1(name, k, n=1):
            a = MOD_ROWS + R1[name] + k
            return COLS[:, ds(a, n)]

        def cols1(name, n):
            a = MOD_ROWS + R1[name]
            return COLS[:, a:a + n]

        def cols2(name, n):
            a = MOD_ROWS + R1_ALL + R2[name]
            return COLS[:, a:a + n]

        def col2(name, k, n=1):
            a = MOD_ROWS + R1_ALL + R2[name] + k
            return COLS[:, ds(a, n)]

        CS = sb("silu_c", [P, 2, KD])
        CTMP = sb("silu_c_tanh", [P, 2, KD])
        MOD = sb("modulation", [P, DEPTH * MOD_TILES, 2])
        GAIN = sb("norm_gain", [P, KD, 2])
        X = sb("residual", [P, KD, T])
        HNH = sb("normed_high", [P, KD, T], F32R)
        HNL = sb("normed_low", [P, KD, T], F32R)
        GH = sb("mixed_high", [P, KD, T], F32R)
        GL = sb("mixed_low", [P, KD, T], F32R)
        RAW = [sb(f"weight_raw{s}", [P, KD, P]) for s in range(2)]
        WH = [sb(f"weight_high{s}", [P, KD, P], F32R) for s in range(2)]
        WL = [sb(f"weight_low{s}", [P, KD, P], F32R) for s in range(2)]
        MW = [sb(f"mod_weight{s}", [P, KD, P]) for s in range(2)]
        SP = sb("softplus", [P, 6, 4])
        BRH = sb("half_gate_bias", [P, 8])
        HGAIN = sb("half_head_gains", [P, 12])
        OV = sb("vector_outputs", [P, DEPTH, 32])
        OVR = sb("vector_output_rows", [32, DEPTH, P])
        NV = sb("norm_value", [P, T])
        NR = sb("norm_rstd", [P, T])
        NT = sb("norm_step", [P, T])
        TMP = sb("norm_temp", [P, 2, T])
        AREA = sb("mixer_area", [P, AREA_ALL])
        mark = [0]

        def area(*shape):
            n = int(np.prod(shape))
            a = AREA[:, mark[0]:mark[0] + n]
            mark[0] += n
            assert mark[0] <= AREA_ALL, mark[0]
            return a.rearrange("p (a b) -> p a b", a=shape[0]) if len(shape) == 2 else a

        OT, OC, OSQ, OB = area(T), area(T), area(T), area(T)
        THG, SG = area(T), area(T)
        common = mark[0]
        ROTA, ROTB = area(T), area(T)
        KT, QT, VT, QD = area(T), area(T), area(T), area(T)
        KDT = area(NB + 1, P)
        VTOK = area(NB + 1, P)
        ATT = area(NB + 1, P)
        ST = area(NB, P)
        S0, SN = area(P), area(P)
        XB = area(TC + PAD)
        XC, TR, TI = area(TC), area(TC), area(TC)
        LA, LTH, LA2, LB, LS = area(TC), area(TC), area(TC), area(TC), area(TC)
        HS = LA2
        GX2, GT, OA = area(T), area(T), area(T)
        GW = [area(P), area(P)]
        mark[0] = common
        CUM = area(2, T)
        RI, RF, RM, RB, RA = area(T), area(T), area(T), area(T), area(T)
        GTOK = area(NB + 1, HEADS)
        layer1 = mark[0]
        CR, LC = OT, OC
        EQ1, EK1, EQ3, EK4 = area(T), area(T), area(T), area(T)
        Q1, Q3 = [area(T), area(T)], [area(T), area(T)]
        EL = area(16)
        VG = area(T)
        K4T, VTG, AG = area(NB + 1, P), area(NB + 1, P), area(NB + 1, P)
        SG8 = area(8, P)
        SG0, SGN, SGF = area(P), area(P), area(P)
        mark[0] = layer1
        SMALLW = area(KD, 72)
        WGATE, GLR = area(2 * P), area(T)
        MASK64, MASKR = area(T), area(T)
        GA, GX = area(T), area(T)
        mark[0] = layer1
        UP, UC, UT = area(TC + PAD), area(TC), area(TC)
        QM, KM, QI = area(T), area(T), area(T)
        VO = area(NB + 1, 2 * P)
        CN = area(NB, 2 * P)
        CN0, CNS = area(2 * P), area(2 * P)
        EW, AM, KW = area(NB + 1, P), area(NB + 1, P), area(NB + 1, P)
        WB = area(T)
        ENB, DD = CUM[:, 0, :], CUM[:, 1, :]
        WQK, WV = area(2 * P), area(P)
        SEL = area(P)
        mark[0] = 0
        Y = area(KD, T)
        YR = [area(D), area(D)]
        XROW = AREA[:, 0:NB * D].rearrange("p (b d) -> p b d", b=NB)
        XSROW = AREA[:, NB * D:(NB + 1) * D]

        PS = [ctx.enter_context(nc.psum_tensor(f"ring{s}", [P, 2, 512], F32)) for s in range(2)]
        K = ctx.enter_context(nc.psum_tensor("core_k", [P, 2, 512], F32))
        J = ctx.enter_context(nc.psum_tensor("core_j", [P, 2, 512], F32))
        MODPS = J[:, 1, 256:260]

        s_cst, s_rows, s_small, s_x = sem("constants_in"), sem("rows_in"), sem("small_in"), sem("x_in")
        s_init = sem("memory_set")
        s_raw = [sem(f"weight_in{s}") for s in range(2)]
        s_mw = [sem(f"mod_weight_in{s}") for s in range(2)]
        s_hi, s_lo, s_used = sem("weight_high"), sem("weight_low"), sem("product_done")
        s_free = [sem(f"ring_free{s}") for s in range(2)]
        s_modu, s_modp, s_mod = sem("mod_weight_used"), sem("mod_product"), sem("mod_ready")
        s_tr = sem("transposed")
        s_cols, s_cs, s_cth = sem("columns_ready"), sem("silu_c_ready"), sem("silu_c_tanh_ready")
        s_sq, s_squ, s_sum = sem("squared"), sem("square_used"), sem("squares_summed")
        s_ln, s_hln = sem("norm_log"), sem("head_norm_log")
        s_r0, s_hf, s_hnh, s_hnl = sem("rstd_start"), sem("normed"), sem("normed_high"), sem("normed_low")
        s_dve, s_act = sem("vector_step"), sem("scalar_step")
        s_kt, s_qt, s_qd = sem("k_rotated"), sem("q_rotated"), sem("q_decayed")
        s_ktr, s_kd, s_sc, s_att = sem("k_transposed"), sem("k_by_token"), sem("scores"), sem("attention")
        s_vtr, s_vtok, s_kv, s_st = sem("v_transposed"), sem("v_by_token"), sem("kv"), sem("states")
        s_ot, s_o, s_mean, s_oc = sem("head_out"), sem("head_out_copied"), sem("head_mean"), sem("centered")
        s_osq, s_var, s_hr0, s_ob = sem("centered_squared"), sem("head_var"), sem("head_rstd_start"), sem("head_done")
        s_thg = sem("gate_tanh")
        s_xb, s_xc, s_gw, s_s0, s_sout = sem("xb_ready"), sem("conv_done"), sem("gate_weights_in"), sem("state_in"), sem("state_out")
        s_gr, s_gi, s_la, s_lq, s_ls = sem("r_gate"), sem("i_gate"), sem("decay_ready"), sem("one_minus_a2"), sem("root_ready")
        s_gx2, s_gt2, s_gth, s_oa = sem("gelu_square"), sem("gelu_inner"), sem("gelu_tanh"), sem("lru_done")
        s_gah, s_ov, s_ovt, s_out = sem("mixed_high_done"), sem("vectors_ready"), sem("vectors_transposed"), sem("output_written")
        s_glo = sem("mixed_low_done")
        s_seen, s_asked = sem("scores_seen"), sem("weight_asked")
        s_yout = [sem(f"y_written{b}") for b in range(2)]
        s_fth = sem("ffn_tanh")
        s_area, s_smw, s_small_p = sem("area_cleared"), sem("small_weights_in"), sem("small_product")
        s_rows1, s_rabs, s_rln, s_rwin = sem("gate_rows"), sem("gate_rows_biased"), sem("gate_rows_log"), sem("gate_rows_in")
        s_rg, s_gt, s_gtok, s_rexp = sem("gate_rows_ready"), sem("gate_transposed"), sem("gate_by_token"), sem("gate_rows_exp")
        s_gp, s_gab, s_gln, s_cum = sem("decay_product"), sem("decay_abs"), sem("decay_log"), sem("decay_sums")
        s_cr, s_ef, s_k4, s_q3 = sem("decay_centered"), sem("decay_factors"), sem("gla_keys"), sem("gla_queries")
        s_k4t, s_k4tok = sem("gla_keys_transposed"), sem("gla_keys_by_token")
        s_gsc, s_gatt, s_gvt, s_gvtok = sem("gla_scores"), sem("gla_attention"), sem("gla_v_transposed"), sem("gla_v_by_token")
        s_gkv, s_gst, s_got, s_gs0, s_gsout = sem("gla_kv"), sem("gla_states"), sem("gla_out"), sem("gla_state_in"), sem("gla_state_out")
        s_mw2, s_c0, s_cout, s_uc, s_uct, s_ucs = (sem("mlstm_weights_in"), sem("mlstm_state_in"), sem("mlstm_state_out"),
                                                   sem("mlstm_conv"), sem("mlstm_conv_tanh"), sem("mlstm_conv_silu"))
        s_ba, s_ex, s_ew, s_mv, s_vo, s_bw, s_wb = (sem("gate_spread"), sem("exponent"), sem("weights_exp"), sem("mlstm_v"),
                                                    sem("mlstm_v_ready"), sem("win_spread"), sem("win_ready"))
        s_mq, s_mk, s_qm, s_km, s_qi = (sem("mlstm_q"), sem("mlstm_k"), sem("mlstm_q_ready"), sem("mlstm_k_ready"),
                                        sem("mlstm_q_weighted"))
        s_msc, s_am, s_mkt, s_kw, s_be, s_enb = (sem("mlstm_scores"), sem("mlstm_attention"), sem("mlstm_k_tokens"),
                                                 sem("mlstm_k_weighted"), sem("floor_spread"), sem("floor_ready"))
        s_cu, s_cn, s_cn0, s_nd, s_dabs, s_dmax, s_d2, s_nv = (
            sem("mlstm_update"), sem("mlstm_states"), sem("mlstm_n_spread"), sem("mlstm_out"), sem("den_abs"),
            sem("den_floored"), sem("den_squared"), sem("variance_plus"))
        s_hmo, s_y, s_yt, s_yr = sem("mlstm_gate"), sem("y_ready"), sem("y_transposed"), sem("y_rows")

        W_HEAD, W_OUT0, W_FFN0 = 0, 24, 32
        psn = [0]

        steps = {}


        def take(n):
            psn[0] += n
            return psn[0] - n

        R_PAR, R_X, R_N0 = take(1), take(KD), take(1)
        R_HEAD, R_OUT0 = take(HEADS * 8), take(KD)
        R_N1 = take(1)
        R_FFN0 = take(3 * KD + 2 * sum(FFN_CUTS))
        R_N2, R_G = take(1), take(2)
        R_GLA = take(2 * 6)
        R_ML = take(HEADS * 4)
        R_OUT1, R_N3 = take(KD), take(1)
        R_FFN1 = take(3 * KD + 2 * sum(FFN_CUTS))
        R_N4, R_Y = take(1), take(NB + 1)
        W1 = W_FFN0 + 3 * KD + 2 * sum(FFN_CUTS)
        W_GLA, W_ML = W1, W1 + 12
        W_OUT1, W_FFN1 = W1 + 12 + 2 * HEADS, W1 + 12 + 2 * HEADS + KD
        MG_START = 12

        def pair(a):
            return a[:, :T].rearrange("p (a b) -> p a b", a=2)

        def ring(p, n=HALF):
            return PS[p.slot][:, :, 0:n]

        def ring_done(eng, p):
            eng.wait_ge(s_free[p.slot], p.before + 1)

        def hi_of(act, n):
            act.wait_ge(s_raw[n.slot], 16 * (n.before + 1))
            act.wait_ge(s_used, n.index - 1 if not isinstance(n.index, int) else max(n.index - 1, 0))
            act.activation(WH[n.slot][:], RAW[n.slot][:], ACT.Copy).then_inc(s_hi, 1)

        def lo_of(dve, n):
            dve.wait_ge(s_hi, n.index + 1)
            dve.tensor_tensor(WL[n.slot][:], RAW[n.slot][:], WH[n.slot][:].bitcast(F32),
                              ALU.subtract).then_inc(s_lo, 1)

        def load_weight(q, n, src, a):
            q.wait_ge(s_lo, n.index)
            q.sem_inc(s_asked, 1)
            src = src[:, :, ds(a(), P)]
            q.dma_start(RAW[n.slot][:, 0:src.shape[1], :], src).then_inc(s_raw[n.slot], 16)

        def load_mod(q, g, per, i):
            for s in range(2):
                if not (isinstance(i, int) and g + per * i == 0):
                    q.wait_ge(s_modu, 2 * (g + per * i) - 1 + s)
                a = 2 * (g + per * i) + s
                l, a0 = (0, a) if g < MOD_TILES // 2 else (1, a - MOD_TILES)
                src = t["w_mod"][l].rearrange("(k p) m -> p k m", p=P)[:, :, ds(a0 * P, P)]
                q.dma_start(MW[s][:], src).then_inc(s_mw[s], 16)

        def mod_group(pe, g):
            pe.wait_ge(s_mod, g)
            for s in range(2):
                pe.wait_ge(s_mw[s], 16 * (g + 1))
                for k in range(KD):
                    mm = pe.matmul(MODPS[:, 2 * s:2 * s + 2], MW[s][:, k, :], CS[:, :, k],
                                   start=(k == 0), stop=(k == KD - 1))
                mm.then_inc(s_modu, 1)

        def mod_read(dve, g):
            dve.wait_ge(s_modu, 2 * g + 2)
            dve.tensor_tensor(MOD[:, ds(2 * g, 2), :], MODPS.rearrange("p (a b) -> p a b", a=2),
                              BMOD[:, ds(2 * g, 2)].unsqueeze(2).to_broadcast([P, 2, 2]),
                              ALU.add).then_inc(s_mod, 1)

        def project(pe, n, p, kt=KD, moving=(HNH, HNL)):
            pe.wait_ge(s_lo, n.index + 2)
            pe.wait_ge(s_free[p.slot], p.before)
            h, l = moving
            for k in range(kt):
                for w, x in ((WH, h), (WH, l), (WL, h)):
                    for half in range(2):
                        last = pe.matmul(PS[p.slot][:, half, 0:HALF], w[n.slot][:, k, :],
                                         x[:, k, half * HALF:(half + 1) * HALF],
                                         start=(k == 0 and w is WH and x is h),
                                         stop=(k == kt - 1 and w is WL))
            last.then_inc(s_used, 1)

        def newton(dve, st, v, y, tmp):
            st.done(dve.tensor_tensor(tmp, y, y, ALU.mult))
            st.done(dve.tensor_tensor(tmp, tmp, v, ALU.mult))
            st.done(dve.tensor_scalar(tmp, tmp, -0.5, 1.5, ALU.mult, ALU.add))
            st.done(dve.tensor_tensor(y, y, tmp, ALU.mult))

        def norm_pe(pe, q, p):
            pe.wait_ge(s_free[p.slot], p.before)
            for k in range(KD):
                pe.wait_ge(s_sq, KD * q + k + 1)
                for half in range(2):
                    mm = pe.matmul(PS[p.slot][:, half, 0:HALF], ONES[:, :],
                                   TMP[:, k % 2, half * HALF:(half + 1) * HALF],
                                   start=(k == 0), stop=(k == KD - 1))
                mm.then_inc(s_squ, 1)

        def norm_act(act, q, p, ready):
            for k in range(KD):
                if KD * q + k >= 2:
                    act.wait_ge(s_squ, KD * q + k - 1)
                ring_done(act, ready(k))
                act.activation(TMP[:, k % 2, :], X[:, k, :], ACT.Square).then_inc(s_sq, 1)
            act.wait_ge(s_squ, KD * (q + 1))
            act.wait_ge(s_hf, KD * q)
            act.activation(pair(NR), ring(p), ACT.Ln, bias=EPSC[:, 0:1], scale=1.0 / D).then_inc(s_ln, 1)
            act.wait_ge(s_ln, q + 1)
            act.activation(NR[:, :], NR[:, :], ACT.Exp, scale=-0.5).then_inc(s_r0, 1)

        def norm_high(act, q):
            for k in range(KD):
                act.wait_ge(s_hf, KD * q + k + 1)
                act.activation(HNH[:, k, :], TMP[:, k % 2, :], ACT.Copy).then_inc(s_hnh, 1)

        def norm_dve(dve, q, p, shift, scale, gain):
            st = steps["dve"]
            st.done(dve.scalar_tensor_tensor(out=GAIN[:, :, :], in0=MOD[:, scale:scale + KD, :], scalar=1.0,
                                             in1=gain.unsqueeze(2).to_broadcast([P, KD, 2]),
                                             op0=ALU.add, op1=ALU.mult))
            norm_rstd(dve, q, p)
            for k in range(KD):
                if KD * q + k >= 2:
                    dve.wait_ge(s_hnh, KD * q + k - 1)
                    dve.wait_ge(s_hnl, KD * q + k - 1)
                dve.wait_ge(s_hf, KD * q + k)
                st.done(dve.tensor_tensor(NT[:, :], X[:, k, :], NR[:, :], ALU.mult))
                st.add(dve.tensor_scalar(TMP[:, k % 2, 0:TP], NT[:, 0:TP], GAIN[:, k, 0:1],
                                         MOD[:, shift + k, 0:1], ALU.mult, ALU.add))
                dve.tensor_scalar(TMP[:, k % 2, TP:T], NT[:, TP:T], GAIN[:, k, 1:2],
                                  MOD[:, shift + k, 1:2], ALU.mult, ALU.add).then_inc(s_hf, 1)
                if k:
                    low_of_norm(dve, q, k - 1)
            low_of_norm(dve, q, KD - 1)

        def norm_rstd(dve, q, p):
            st = steps["dve"]
            dve.wait_ge(s_ln, q + 1)
            st.done(dve.tensor_scalar(pair(NV), ring(p), 1.0 / D, EPS, ALU.mult, ALU.add))
            dve.wait_ge(s_r0, q + 1)
            dve.tensor_tensor(NT[:, :], NR[:, :], NR[:, :], ALU.mult).then_inc(s_free[p.slot], 1)
            ring_done(dve, p)
            st.done(dve.tensor_tensor(NT[:, :], NT[:, :], NV[:, :], ALU.mult))
            st.done(dve.tensor_scalar(NT[:, :], NT[:, :], -0.5, 1.5, ALU.mult, ALU.add))
            st.done(dve.tensor_tensor(NR[:, :], NR[:, :], NT[:, :], ALU.mult))

        def low_of_norm(dve, q, k):
            dve.wait_ge(s_hnh, KD * q + k + 1)
            dve.tensor_tensor(HNL[:, k, :], TMP[:, k % 2, :], HNH[:, k, :].bitcast(F32),
                              ALU.subtract).then_inc(s_hnl, 1)

        def residual_dve(dve, n, p, gate, m):
            dve.wait_ge(s_used, n.index + 1)
            for lo, hi, half, g in ((0, HALF, 0, 0), (HALF, TP, 1, 0), (TP, T, 1, 1)):
                a = lo - half * HALF
                ins = dve.scalar_tensor_tensor(
                    out=X[:, m, lo:hi],
                    in0=PS[p.slot][:, half, a:a + hi - lo],
                    scalar=MOD[:, gate + m, g:g + 1],
                    in1=X[:, m, lo:hi],
                    op0=ALU.mult, op1=ALU.add)
                if hi == T:
                    ins.then_inc(s_free[p.slot], 1)

        def row_loads():
            yield ROWS[0:MOD_ROWS, 0, :], t["b_mod"].rearrange("l (m p) -> (l m) p", p=P)
            for name in ("norm_mix_g", "norm_ffn_g", "lru_lambda", "ret_gn_g", "lru_conv_b", "c_prompt", "c_sample"):
                n = t[name].shape[0] * t[name].shape[1] // P
                yield ROWS[R1[name]:R1[name] + n, 1, :], t[name].rearrange("a (k p) -> (a k) p", p=P)
            yield (ROWS[R1["final_norm_g"]:R1["final_norm_g"] + KD, 1, :],
                   t["final_norm_g"].rearrange("(k p) -> k p", p=P))
            yield (ROWS[R1["lru_conv_w"]:R1["lru_conv_w"] + 16, 1, :],
                   t["lru_conv_w"][0].rearrange("t (k p) -> (t k) p", p=P))
            yield (ROWS[R1["state_lru_conv"]:R1["state_lru_conv"] + 12, 1, :],
                   t["state_lru_conv"][0, 0].rearrange("t (k p) -> (t k) p", p=P))
            yield (ROWS[R1["state_lru_h"]:R1["state_lru_h"] + 4, 1, :],
                   t["state_lru_h"][0].rearrange("a (k p) -> (a k) p", p=P))
            for part in range(2):
                r = R1["lru_gate_b"] + 4 * part
                yield (ROWS[r:r + 4, 1, :].rearrange("r (two j) -> r two j", two=2),
                       t["lru_gate_b"][0].rearrange("(r two) j -> r two j", two=2)[:, :, 64 * part:64 * part + 64])
            for name in ("gla_b_gate", "gla_gn_g", "mlstm_conv_b", "mlstm_gn_g"):
                n = t[name].shape[1] // P
                yield ROWS[R2[name]:R2[name] + n, 2, :], t[name].rearrange("a (k p) -> (a k) p", p=P)
            yield (ROWS[R2["mlstm_conv_w"]:R2["mlstm_conv_w"] + 16, 2, :],
                   t["mlstm_conv_w"][0].rearrange("t (k p) -> (t k) p", p=P))
            yield (ROWS[R2["state_mlstm_conv"]:R2["state_mlstm_conv"] + 12, 2, :],
                   t["state_mlstm_conv"][0, 0].rearrange("t (k p) -> (t k) p", p=P))
            yield ROWS[R2["state_mlstm_n"]:R2["state_mlstm_n"] + 4, 2, :], t["state_mlstm_n"][0, 0]

        def ffn_parts(w, p, g):
            a = 0
            for n in FFN_CUTS:
                yield a, n, w, p, g
                a, w, p, g = a + n, w + 2 * n + KD, p + 2 * n + KD, g + n

        def out_loads(sp, w, src, kt):
            with sp.Fori(0, KD // 2) as i:
                for j in range(2):
                    load_weight(sp, Turn(w, j, 2, i), src.rearrange("(k p) m -> p k m", p=P),
                                lambda: i * 2 * P + j * P)

        def ffn_loads(sp, l, w0):
            for a, n, w, _, _ in ffn_parts(w0, 0, 0):
                with sp.Fori(0, n) as i:
                    for j in range(2):
                        load_weight(sp, Turn(w, j, 2, i), t["w_ffn_in"][l].rearrange("(k p) m -> p k m", p=P),
                                    lambda: i * P + j * DFF + a * P)
                out_loads(sp, w + 2 * n, t["w_ffn_out"][l][a * P:(a + n) * P, :], n)

        def transpose_blocks(pe, src, dst, dst_s):
            for b in range(NB):
                pe.transpose(dst[:, b * P:(b + 1) * P], src[:, b * P:(b + 1) * P], IDENT)
            return pe.transpose(dst_s, src[:, TP:T], IDENT)

        def out_pe(pe, w, p, kt, group=None):
            step = 4 if group is not None else 2
            with pe.Fori(0, KD // step) as i:
                for j in range(step):
                    project(pe, Turn(w, j, step, i), Turn(p, j, step, i), kt, (GH, GL))
                if group is not None:
                    mod_group(pe, group + i)

        def ffn_pe(pe, w0, p0, glo, group):
            for a, n, w, p, g in ffn_parts(w0, p0, group or 0):
                with pe.Fori(0, n) as i:
                    for j in range(2):
                        project(pe, Turn(w, j, 2, i), Turn(p, j, 2, i))
                    if group is not None:
                        mod_group(pe, g + i)
                pe.wait_ge(s_glo, glo + a + n)
                out_pe(pe, w + 2 * n, p + 2 * n, n)

        def head_mean(pe, src, ready, h):
            pe.wait_ge(ready, h + 1)
            pe.matmul(J[:, 0, :], MEAN[:, :], src[:, 0:TP], start=True, stop=True)
            pe.matmul(J[:, 1, 0:TS], MEAN[:, :], src[:, TP:T], start=True, stop=True).then_inc(s_mean, 1)

        def head_var(pe, src, ready, h):
            pe.wait_ge(ready, h + 1)
            pe.matmul(K[:, 0, :], MEAN[:, :], src[:, 0:TP], start=True, stop=True)
            pe.matmul(K[:, 1, 0:TS], MEAN[:, :], src[:, TP:T], start=True, stop=True).then_inc(s_var, 1)

        def out_act(act, w, last=False):
            n = KD // 2 - (1 if last else 0)
            with act.Fori(0, n) as i:
                for j in range(2):
                    hi_of(act, Turn(w, j + 1, 2, i))
            if last:
                hi_of(act, Turn(w + 2 * n + 1))

        def ffn_act(act, w0, p0, gah, done, last=False):
            parts = list(ffn_parts(w0, p0, 0))
            for a, n, w, p, _ in parts:
                act.preload_act_table(ACT.Tanh)
                with act.Fori(0, n) as i:
                    hi_of(act, Turn(w, 1, 2, i))
                    act.wait_ge(s_used, Turn(w, 0, 2, i).index + 1)
                    act.activation(pair(TMP[:, 0, :]), ring(Turn(p, 0, 2, i)), ACT.Tanh, scale=0.5).then_inc(s_fth, 1)
                    hi_of(act, Turn(w, 2, 2, i))
                    ring_done(act, Turn(p, 1, 2, i))
                    act.activation(GH[:, i, :], TMP[:, 1, :], ACT.Copy).then_inc(s_gah, 1)
                out_act(act, w + 2 * n, last and a == parts[-1][0])

        def fill_padded(act, st, dst, p):
            st.add(act.activation(dst[:, PAD:PAD + HALF], PS[p.slot][:, 0, 0:HALF], ACT.Copy))
            st.add(act.activation(dst[:, PAD + HALF:PAD + TP], PS[p.slot][:, 1, 0:TP - HALF], ACT.Copy))
            act.activation(dst[:, SC + PAD:SC + PAD + TS], PS[p.slot][:, 1, TP - HALF:HALF],
                           ACT.Copy).then_inc(s_free[p.slot], 1)
            ring_done(act, p)

        def conv_columns(act, st, src, l, h):
            for o, a in ((8, TP), (20, SC + TS)):
                st.add(act.activation(OV[:, l, o:o + 12].rearrange("p (t k) -> p t k", k=4)[:, :, h],
                                      src[:, a:a + PAD], ACT.Copy))

        def copy_head(act, st, ready, h, count):
            act.wait_ge(ready, count)
            act.wait_ge(s_oc, h)
            st.add(act.activation(OT[:, 0:TP], K[:, 0, :], ACT.Copy))
            act.activation(OT[:, TP:T], K[:, 1, P:P + TS], ACT.Copy).then_inc(s_o, 1)

        def head_rstd(act, st, h):
            act.wait_ge(s_var, h + 1)
            st.add(act.activation(NR[:, 0:TP], K[:, 0, :], ACT.Ln, bias=EPSC[:, 0:1]))
            act.activation(NR[:, TP:T], K[:, 1, 0:TS], ACT.Ln, bias=EPSC[:, 0:1]).then_inc(s_hln, 1)
            act.wait_ge(s_hln, h + 1)
            act.activation(NR[:, :], NR[:, :], ACT.Exp, scale=-0.5).then_inc(s_hr0, 1)

        def gate_dve(dve, n, p, h):
            dve.wait_ge(s_thg, h + 1)
            dve.scalar_tensor_tensor(out=pair(SG), in0=pair(THG), scalar=1.0, in1=ring(p), op0=ALU.add,
                                     op1=ALU.mult).then_inc(s_free[p.slot], 1)

        def center(dve, st, h):
            dve.wait_ge(s_mean, h + 1)
            dve.wait_ge(s_osq, h)
            st.add(dve.tensor_tensor(OC[:, 0:TP], OT[:, 0:TP], J[:, 0, :], ALU.subtract))
            dve.tensor_tensor(OC[:, TP:T], OT[:, TP:T], J[:, 1, 0:TS], ALU.subtract).then_inc(s_oc, 1)

        def finish_head(dve, st, h, gain):
            dve.wait_ge(s_hln, h + 1)
            st.add(dve.tensor_scalar(NV[:, 0:TP], K[:, 0, :], EPS, None, ALU.add))
            st.done(dve.tensor_scalar(NV[:, TP:T], K[:, 1, 0:TS], EPS, None, ALU.add))
            finish_rstd(dve, st, h, gain)

        def finish_rstd(dve, st, h, gain):
            dve.wait_ge(s_hr0, h + 1)
            newton(dve, st, NV[:, :], NR[:, :], NT[:, :])
            st.done(dve.tensor_tensor(NT[:, :], OC, NR[:, :], ALU.mult))
            dve.scalar_tensor_tensor(out=OB, in0=NT[:, :], scalar=gain, in1=SG, op0=ALU.mult,
                                     op1=ALU.mult).then_inc(s_ob, 1)
            dve.wait_ge(s_ob, h + 1)

        def convolve(dve, st, src, dst, w, b, h, ready, free):
            dve.wait_ge(*free)
            st.done(dve.tensor_scalar(dst, src[:, PAD:PAD + TC], w[:, PAD, ds(h, 1)], b[:, ds(h, 1)],
                                      ALU.mult, ALU.add))
            for tap in (2, 1, 0):
                ins = dve.scalar_tensor_tensor(out=dst, in0=src[:, tap:tap + TC], scalar=w[:, tap, ds(h, 1)],
                                               in1=dst, op0=ALU.mult, op1=ALU.add)
                if tap:
                    st.done(ins)
            ins.then_inc(ready, 1)

        def out_dve(dve, w, p, gate, group=None, last=False):
            step = 4 if group is not None else 2
            n = KD // step - (1 if last else 0)
            with dve.Fori(0, n) as i:
                for j in range(step):
                    lo_of(dve, Turn(w, j + 1, step, i))
                    residual_dve(dve, Turn(w, j, step, i), Turn(p, j, step, i), gate, i * step + j)
                if group is not None:
                    mod_read(dve, group + i)
            if last:
                a = step * n
                lo_of(dve, Turn(w + a + 1))
                for j in range(2):
                    residual_dve(dve, Turn(w + a, j), Turn(p + a, j), gate, a + j)

        def ffn_dve(dve, w0, p0, gah, done, gate, group, last=False):
            parts = list(ffn_parts(w0, p0, group or 0))
            for a, n, w, p, g in parts:
                with dve.Fori(0, n) as i:
                    gi, ui = Turn(p, 0, 2, i), Turn(p, 1, 2, i)
                    lo_of(dve, Turn(w, 1, 2, i))
                    dve.wait_ge(s_fth, i + done + a + 1)
                    dve.scalar_tensor_tensor(out=pair(NV), in0=pair(TMP[:, 0, :]), scalar=1.0, in1=ring(gi),
                                             op0=ALU.add, op1=ALU.mult).then_inc(s_free[gi.slot], 1)
                    lo_of(dve, Turn(w, 2, 2, i))
                    ring_done(dve, gi)
                    dve.wait_ge(s_used, Turn(w, 1, 2, i).index + 1)
                    dve.scalar_tensor_tensor(out=pair(TMP[:, 1, :]), in0=pair(NV), scalar=0.5, in1=ring(ui),
                                             op0=ALU.mult, op1=ALU.mult).then_inc(s_free[ui.slot], 1)
                    dve.wait_ge(s_gah, i + gah + a + 1)
                    dve.tensor_tensor(GL[:, i, :], TMP[:, 1, :], GH[:, i, :].bitcast(F32),
                                      ALU.subtract).then_inc(s_glo, 1)
                    if group is not None:
                        mod_read(dve, g + i)
                out_dve(dve, w + 2 * n, p + 2 * n, gate, None, last and a == parts[-1][0])

        CW = t["c_w_in"][0].rearrange("(k p) m -> p k m", p=P)
        C_GQ, C_GK, C_GV, C_GLR, C_GR, C_U, C_O, C_I, C_F = 0, 256, 512, 1024, 1040, 1552, 2064, 2576, 2580

        def pair_items(i):
            return [lambda: i * P + C_GK, lambda: i * P + C_GQ, lambda: i * 2 * P + C_GV, lambda: i * 2 * P + C_GR,
                    lambda: i * 2 * P + C_GV + P, lambda: i * 2 * P + C_GR + P]

        def layer1_sync(sp):
            sp.wait_ge(s_sout, 32 * HEADS)
            with sp.Fori(0, 2) as i:
                for j, a in enumerate(pair_items(i)):
                    load_weight(sp, Turn(W_GLA, j, 6, i), CW, a)
                    if j == 1:
                        sp.wait_ge(s_area, 1)
                        sp.wait_ge(s_gtok, 1)
                        sp.wait_ge(s_cum, 2)
                        sp.wait_ge(s_got, 2 * i)
                        sp.dma_start(SG0, t["state_gla"][0, 0, ds(2 * i, 2)].rearrange("h d e -> (h d) e")
                                     ).then_inc(s_gs0, 16)
            with sp.Fori(0, HEADS) as h:
                load_weight(sp, Turn(W_ML, 0, 2, h), CW, lambda: h * P + C_U)
                sp.wait_ge(s_gsout, 64)
                sp.wait_ge(s_got, HEADS)
                sp.wait_ge(s_nd, h)
                sp.dma_start(WQK, t["mlstm_w_qk"][0, h]).then_inc(s_mw2, 16)
                sp.dma_start(WV, t["mlstm_w_v"][0, h]).then_inc(s_mw2, 16)
                sp.dma_start(SEL[0:HEADS, :], t["selectors"][h]).then_inc(s_mw2, 16)
                sp.dma_start(CN0[:, 0:P], t["state_mlstm_C"][0, 0, h]).then_inc(s_c0, 16)
                load_weight(sp, Turn(W_ML, 1, 2, h), CW, lambda: h * P + C_O)
            sp.wait_ge(s_rg, 1)
            sp.dma_start(out["m_p"][0].rearrange("a h -> h a"), RM[0:HEADS, TP - 1:TP],
                         allow_slow_non_contiguous=True).then_inc(s_out, 16)
            sp.dma_start(out["m_s"][0].rearrange("a h -> h a"), RM[0:HEADS, T - 1:T],
                         allow_slow_non_contiguous=True).then_inc(s_out, 16)
            out_loads(sp, W_OUT1, t["c_w_out"][0], KD)
            ffn_loads(sp, 1, W_FFN1)
            sp.wait_ge(s_ov, 1)
            n = 2
            for l, (first, second) in enumerate((("lru_h", "lru_conv"), ("n", "conv"))):
                for g, group in enumerate(("_p", "_s")):
                    dst = out[first + group]
                    dst = dst[0, 0] if l else dst[0].rearrange("a (k p) -> (a k) p", p=P)
                    sp.dma_start(dst, OVR[4 * g:4 * g + 4, l, :]).then_inc(s_out, 16)
                    sp.dma_start(out[second + group][0, 0].rearrange("t (k p) -> (t k) p", p=P),
                                 OVR[8 + 12 * g:20 + 12 * g, l, :]).then_inc(s_out, 16)
                    n += 2
            for b in range(NB + 1):
                sp.wait_ge(s_yr, b + 1)
                dst = out["y_p"][0, b * P:(b + 1) * P, :] if b < NB else out["y_s"][0]
                sp.dma_start(dst, YR[b % 2][0:P if b < NB else TS, :]).then_inc(s_yout[b % 2], 16)
            sp.wait_ge(s_out, 16 * n)
            sp.wait_ge(s_yout[0], 16 * (NB // 2 + 1))
            sp.wait_ge(s_yout[1], 16 * (NB // 2))
            sp.wait_ge(s_cout, 32 * HEADS)
            sp.wait_ge(s_small, 32)

        def layer1_pool(pool):
            pool.wait_ge(s_glo, KD)
            pool.wait_ge(s_sout, 32 * HEADS)
            zero = pool.memset(SMALLW, 0.0)
            zero.then_inc(s_area, 1)
            pool.memset(MASK64, 1.0).then_inc(s_area, 1)
            pool.memset(MASKR, 1.0).then_inc(s_area, 1)
            pool.wait_ge(s_area, 3)
            pool.memset(MASK64[:, 0:T:64], 0.0).then_inc(s_area, 1)
            pool.memset(MASKR[:, 0:T:P], 0.0).then_inc(s_area, 1)
            for a, c, n in ((0, C_GLR, 16), (32, C_I, HEADS), (64, C_F, HEADS)):
                pool.dma_start(SMALLW[:, :, a:a + n], CW[:, :, c:c + n],
                               allow_slow_non_contiguous=True).then_inc(s_smw, 16)
            pool.dma_start(WGATE[0:16, :], t["gla_w_gate"][0]).then_inc(s_smw, 16)
            pool.wait_ge(s_cum, 2)
            pool.wait_ge(s_rg, 1)
            for a in (Q1[0], Q1[1], Q3[0], Q3[1], AG):
                pool.memset(a, 0.0).then_inc(s_area, 1)
            with pool.Fori(0, 2) as i:
                pool.wait_ge(s_gst, 2 * i + 2)
                for name, state in (("gla_p", SGF), ("gla_s", SGN)):
                    pool.dma_start(out[name][0, 0, ds(2 * i, 2)].rearrange("h d e -> (h d) e"),
                                   state).then_inc(s_gsout, 16)
            pool.wait_ge(s_ob, 2 * HEADS)
            pool.wait_ge(s_got, HEADS)
            pool.wait_ge(s_gsout, 64)
            for a in (UP[:, 0:PAD], UP[:, TC + PAD - 1:TC + PAD]):
                pool.memset(a, 0.0).then_inc(s_area, 1)
            pool.memset(VO[:, :, P:2 * P], 1.0).then_inc(s_area, 1)
            with pool.Fori(0, HEADS) as h:
                pool.wait_ge(s_cn, h + 1)
                pool.dma_start(out["C_p"][0, 0, h], CN[:, NB - 1, 0:P]).then_inc(s_cout, 16)
                pool.dma_start(out["C_s"][0, 0, h], CNS[:, 0:P]).then_inc(s_cout, 16)

        AREA_SMALL, AREA_GLA, AREA_ML = 5, 10, 13

        def small_pe(pe):
            pe.wait_ge(s_smw, 64)
            pe.wait_ge(s_area, AREA_SMALL)
            for k in range(KD):
                for half in range(2):
                    for x in (HNH, HNL):
                        mm = pe.matmul(K[0:68, half, 0:HALF], SMALLW[:, k, 0:68],
                                       x[:, k, half * HALF:(half + 1) * HALF].bitcast(F32),
                                       start=(k == 0 and x is HNH), stop=(k == KD - 1 and x is HNL),
                                       skip_group_check=True)
            mm.then_inc(s_small_p, 1)
            pe.wait_ge(s_rows1, 1)
            for i in range(2):
                p = Turn(R_G, i)
                pe.wait_ge(s_free[p.slot], p.before)
                for half in range(2):
                    mm = pe.matmul(PS[p.slot][:, half, 0:HALF], WGATE[0:16, i * P:(i + 1) * P],
                                   GLR[0:16, half * HALF:(half + 1) * HALF], start=True, stop=True)
                mm.then_inc(s_gp, 1)
            pe.wait_ge(s_rg, 1)
            for b in range(NB):
                pe.transpose(K[:, 0, 4 * b:4 * b + 4], RB[0:HEADS, b * P:(b + 1) * P], IDENT[0:HEADS, 0:HEADS])
            pe.transpose(K[0:TS, 0, 16:20], RB[0:HEADS, TP:T], IDENT[0:HEADS, 0:HEADS]).then_inc(s_gt, 1)

        def gla_head_pe(pe, i, j):
            n = 2 * i + j
            pe.wait_ge(s_q3, i + 1)
            for b in range(NB):
                pe.matmul(J[:, 0, b * P:(b + 1) * P], EK1[:, b * P:(b + 1) * P], Q1[j][:, b * P:(b + 1) * P],
                          start=True, stop=True)
            pe.matmul(J[0:TS, 1, 0:TS], EK1[:, TP:T], Q1[j][:, TP:T], start=True, stop=True).then_inc(s_gsc, 1)

        def gla_values_pe(pe, i, j, p):
            ring_done(pe, p)
            transpose_blocks(pe, VG, K[:, 0, :], K[0:TS, 1, 0:P]).then_inc(s_gvt, 1)

        def gla_out_pe(pe, i, j):
            n = 2 * i + j
            pe.wait_ge(s_gvtok, n + 1)
            pe.wait_ge(s_gatt, n + 1)
            for c in range(2 * NB):
                r = slice(64 * (c % 2), 64 * (c % 2) + 64)
                dst = (K, J)[c % 2][:, 0, (c // 2) * P:(c // 2 + 1) * P]
                pe.matmul(dst, K4T[r, c // 2, :], VTG[r, c // 2, :], start=True, stop=True)
            pe.matmul(K[:, 1, 0:P], K4T[0:TS, NB, :], VTG[0:TS, NB, :], start=True, stop=True).then_inc(s_gkv, 1)
            pe.wait_ge(s_gst, n + 1)
            pe.wait_ge(s_gs0, 16 * i + 16)
            for c in range(2 * NB):
                cols = slice(64 * c, 64 * c + 64)
                pe.matmul(K[:, 0, cols], VTG[:, c // 2, :], AG[:, c // 2, 64 * (c % 2):64 * (c % 2) + 64],
                          start=True, stop=(c == 0))
                if c:
                    pe.matmul(K[:, 0, cols], SG8[:, c - 1, :], Q3[j][:, cols], start=False, stop=True)
            pe.matmul(K[:, 1, P:P + TS], VTG[0:TS, NB, :], AG[0:TS, NB, 0:TS], start=True, stop=False)
            pe.matmul(K[:, 1, P:P + TS], SG0, Q3[j][:, TP:T], start=False, stop=True).then_inc(s_got, 1)

        def gla_pe(pe):
            pe.wait_ge(s_gtok, 1)
            with pe.Fori(0, 2) as i:
                def item(j):
                    project(pe, Turn(W_GLA, j, 6, i), Turn(R_GLA, j, 6, i))

                item(0)
                item(1)
                item(2)
                pe.wait_ge(s_k4, i + 1)
                pe.wait_ge(s_ob, 2 * i + HEADS)
                transpose_blocks(pe, EK4, K[:, 0, :], K[0:TS, 1, 0:P]).then_inc(s_k4t, 1)
                pe.wait_ge(s_oc, 2 * i + HEADS)
                gla_head_pe(pe, i, 0)
                item(3)
                pe.wait_ge(s_k4tok, i + 1)
                gla_values_pe(pe, i, 0, Turn(R_GLA, 2, 6, i))
                item(4)
                gla_out_pe(pe, i, 0)
                item(5)
                head_mean(pe, OT, s_o, 2 * i + HEADS)
                head_var(pe, OSQ, s_osq, 2 * i + HEADS)
                gla_head_pe(pe, i, 1)
                pe.wait_ge(s_ob, 2 * i + HEADS + 1)
                gla_values_pe(pe, i, 1, Turn(R_GLA, 4, 6, i))
                gla_out_pe(pe, i, 1)
                head_mean(pe, OT, s_o, 2 * i + HEADS + 1)
                head_var(pe, OSQ, s_osq, 2 * i + HEADS + 1)

        def mlstm_pe(pe):
            with pe.Fori(0, HEADS) as h:
                def r(j):
                    return Turn(R_ML, j, 4, h)

                def spread(row, dst):
                    pe.matmul(dst[:, 0, :], SEL[0:HEADS, :], row[0:HEADS, 0:TP], start=True, stop=True)
                    return pe.matmul(dst[:, 1, 0:TS], SEL[0:HEADS, :], row[0:HEADS, TP:T], start=True, stop=True)

                project(pe, Turn(W_ML, 0, 2, h), r(0))
                pe.wait_ge(s_mw2, 48 * h + 48)
                pe.wait_ge(s_rexp, 2)
                pe.wait_ge(s_ob, h + 2 * HEADS)
                spread(RA, K).then_inc(s_ba, 1)
                project(pe, Turn(W_ML, 1, 2, h), r(1))
                ring_done(pe, r(0))
                pe.wait_ge(s_oc, h + 2 * HEADS)
                for b in range(NB + 1):
                    n, a = (P, PAD + b * P) if b < NB else (TS, SC + PAD)
                    mm = pe.matmul(J[:, 0, b * P:(b + 1) * P] if b < NB else J[0:TS, 1, 0:P],
                                   UP[:, a:a + n], WV, start=True, stop=True)
                mm.then_inc(s_mv, 1)
                pe.wait_ge(s_ucs, h + 1)
                for part, s_q in ((0, s_mq), (1, s_mk)):
                    p = r(2 + part)
                    pe.wait_ge(s_free[p.slot], p.before)
                    pe.matmul(PS[p.slot][:, 0, :], WQK[:, part * P:(part + 1) * P], UC[:, 0:TP], start=True, stop=True)
                    pe.matmul(PS[p.slot][:, 1, 0:TS], WQK[:, part * P:(part + 1) * P], UC[:, SC:SC + TS],
                              start=True, stop=True).then_inc(s_q, 1)
                pe.wait_ge(s_vo, h + 1)
                spread(RI, J).then_inc(s_bw, 1)
                pe.wait_ge(s_qm, h + 1)
                pe.wait_ge(s_km, h + 1)
                pe.wait_ge(s_ex, h + 1)
                for b in range(NB):
                    pe.matmul(K[:, 0, b * P:(b + 1) * P], KM[:, b * P:(b + 1) * P], QM[:, b * P:(b + 1) * P],
                              start=True, stop=True)
                pe.matmul(K[0:TS, 1, 0:TS], KM[:, TP:T], QM[:, TP:T], start=True, stop=True).then_inc(s_msc, 1)
                pe.wait_ge(s_wb, h + 1)
                for b in range(NB + 1):
                    n, a = (P, b * P) if b < NB else (TS, SC)
                    mm = pe.matmul(J[:, 0, b * P:(b + 1) * P] if b < NB else J[0:TS, 1, 0:P],
                                   UC[:, a:a + n], WQK[:, P:2 * P], start=True, stop=True)
                mm.then_inc(s_mkt, 1)
                pe.wait_ge(s_am, h + 1)
                spread(RF, K).then_inc(s_be, 1)
                pe.wait_ge(s_kw, h + 1)
                pe.wait_ge(s_enb, h + 1)
                for b in range(NB):
                    pe.matmul(K[:, b // 2, (b % 2) * 256:(b % 2) * 256 + 256], KW[:, b, :], VO[:, b, :],
                              start=True, stop=True)
                pe.matmul(J[:, 1, 0:256], KW[0:TS, NB, :], VO[0:TS, NB, :], start=True, stop=True).then_inc(s_cu, 1)
                pe.wait_ge(s_cn, h + 1)
                pe.wait_ge(s_qi, h + 1)
                for b in range(NB):
                    cols = slice(b * P, (b + 1) * P)
                    for part, dst in ((0, K), (1, J)):
                        c = slice(part * P, (part + 1) * P)
                        pe.matmul(dst[:, 0, cols], VO[:, b, c], AM[:, b, :], start=True, stop=(b == 0))
                        if b:
                            pe.matmul(dst[:, 0, cols], CN[:, b - 1, c], QI[:, cols], start=False, stop=True)
                for part, dst in ((0, K[:, 1, P:P + TS]), (1, J[:, 1, 0:TS])):
                    c = slice(part * P, (part + 1) * P)
                    pe.matmul(dst, VO[0:TS, NB, c], AM[0:TS, NB, 0:TS], start=True, stop=False)
                    mm = pe.matmul(dst, CN0[:, c], QI[:, TP:T], start=False, stop=True)
                mm.then_inc(s_nd, 1)
                pe.wait_ge(s_dabs, h + 1)
                head_mean(pe, OT, s_o, h + 2 * HEADS)
                head_var(pe, OSQ, s_osq, h + 2 * HEADS)

        def layer1_pe(pe):
            norm_pe(pe, 2, Turn(R_N2))
            pe.wait_ge(s_hnl, 3 * KD)
            small_pe(pe)
            gla_pe(pe)
            mlstm_pe(pe)
            pe.wait_ge(s_glo, 2 * KD + DONE0)
            out_pe(pe, W_OUT1, R_OUT1, KD)
            norm_pe(pe, 3, Turn(R_N3))
            pe.wait_ge(s_hnl, 4 * KD)
            ffn_pe(pe, W_FFN1, R_FFN1, 2 * KD + DONE0, None)
            norm_pe(pe, 4, Turn(R_N4))
            for l in range(DEPTH):
                pe.transpose(K[0:32, 0, l * P:(l + 1) * P], OV[:, l, :], IDENT).then_inc(s_ovt, 1)
            for b in range(NB + 1):
                n = P if b < NB else TS
                p = Turn(R_Y, b)
                pe.wait_ge(s_free[p.slot], p.before)
                pe.wait_ge(s_y, KD)
                for k in range(KD):
                    mm = pe.transpose(PS[p.slot][0:n, k // 4, (k % 4) * P:(k % 4 + 1) * P],
                                      Y[:, k, b * P:b * P + n], IDENT)
                mm.then_inc(s_yt, 1)

        def small_act(act, st):
            act.wait_ge(s_small_p, 1)
            act.wait_ge(s_area, AREA_SMALL)
            st.add(act.activation(pair(GLR)[0:16], K[0:16, :, 0:HALF], ACT.Copy))
            st.add(act.activation(pair(RI)[0:HEADS], K[32:36, :, 0:HALF], ACT.Copy))
            act.activation(pair(RF)[0:HEADS], K[64:68, :, 0:HALF], ACT.Copy).then_inc(s_rows1, 1)
            act.wait_ge(s_rabs, 1)
            act.preload_act_table_set("natural_log_exp_and_others")
            st.done(act.activation(RA[0:HEADS], RF[0:HEADS], ACT.Abs))
            st.done(act.activation(RA[0:HEADS], RA[0:HEADS], ACT.Exp, scale=-1.0))
            act.activation(RA[0:HEADS], RA[0:HEADS], ACT.Ln, bias=ONES[0:HEADS, 0:1]).then_inc(s_rln, 1)
            for i in range(2):
                act.wait_ge(s_gp, i + 1)
                act.wait_ge(s_cum, i)
                act.activation(pair(GA), ring(Turn(R_G, i)), ACT.Abs, bias=col2("gla_b_gate", i)).then_inc(s_gab, 1)
                act.wait_ge(s_gab, i + 1)
                st.done(act.activation(GA, GA, ACT.Exp, scale=-1.0))
                act.activation(GA, GA, ACT.Ln, bias=ONES[:, 0:1]).then_inc(s_gln, 1)
            act.wait_ge(s_rwin, 1)
            act.activation(RI[0:HEADS], RI[0:HEADS], ACT.Exp).then_inc(s_rexp, 1)
            act.activation(RF[0:HEADS], RM[0:HEADS], ACT.Exp, scale=-1.0).then_inc(s_rexp, 1)
            act.wait_ge(s_gt, 1)
            st.add(act.activation(GTOK[:, 0:NB, :], K[:, 0, 0:16].rearrange("p (b h) -> p b h", b=NB), ACT.Copy))
            act.activation(GTOK[0:TS, NB, :], K[0:TS, 0, 16:20], ACT.Copy).then_inc(s_gtok, 1)

        def mixed_high(act, n, dst):
            act.wait_ge(s_ob, n + 1)
            act.activation(GH[:, dst, :], OB, ACT.Copy).then_inc(s_gah, 1)

        def gla_act(act, st):
            act.wait_ge(s_area, AREA_GLA)
            with act.Fori(0, 2) as i:
                st.loop(i, ACT_PAIR)

                def w(j):
                    return Turn(W_GLA, j, 6, i)

                def r(j):
                    return Turn(R_GLA, j, 6, i)

                act.wait_ge(s_cr, i + 1)
                act.wait_ge(s_gsc, 2 * i)
                act.wait_ge(s_k4t, i)
                st.add(act.activation(EK1, CR, ACT.Exp, scale=-1.0 / GLA_TAU))
                st.add(act.activation(EK4, LC, ACT.Exp, scale=1.0 / GLA_TAU))
                st.add(act.activation(EQ1, CR, ACT.Exp, scale=1.0 / GLA_TAU))
                st.add(act.activation(EL[:, 0:8], CUM[:, i, 63:TP:64], ACT.Exp, scale=1.0 / GLA_TAU))
                st.add(act.activation(EL[:, 8:9], CUM[:, i, T - 1:T], ACT.Exp, scale=1.0 / GLA_TAU))
                act.activation(EQ3, CUM[:, i, :], ACT.Exp, scale=1.0 / GLA_TAU).then_inc(s_ef, 1)
                hi_of(act, w(1))
                hi_of(act, w(2))
                hi_of(act, w(3))
                act.wait_ge(s_k4t, i + 1)
                act.wait_ge(s_gkv, 2 * i)
                st.add(act.activation(K4T[:, 0:NB, :], K[:, 0, :].rearrange("p (b c) -> p b c", b=NB), ACT.Copy))
                act.activation(K4T[0:TS, NB, :], K[0:TS, 1, 0:P], ACT.Copy).then_inc(s_k4tok, 1)
                for j in range(2):
                    n = 2 * i + j
                    v, g = r(2 + 2 * j), r(3 + 2 * j)
                    act.wait_ge(s_used, w(2 + 2 * j).index + 1)
                    act.wait_ge(s_gvt, n)
                    act.activation(pair(VG), ring(v), ACT.Copy).then_inc(s_free[v.slot], 1)
                    hi_of(act, w(6 if j else 4))
                    gla_values_act(act, st, i, j)
                    gla_gate_act(act, w(3 + 2 * j), g, n)
                    if not j:
                        hi_of(act, w(5))
                    copy_head(act, st, s_got, n + HEADS, n + 1)
                    gla_square(act, n)
                    head_rstd(act, st, n + HEADS)
                    mixed_high(act, n + HEADS, n)
            st.end(2)

        def gla_square(act, n):
            act.wait_ge(s_oc, n + HEADS + 1)
            act.activation(OSQ, OC, ACT.Square).then_inc(s_osq, 1)

        def gla_values_act(act, st, i, j):
            n = 2 * i + j
            act.wait_ge(s_gvt, n + 1)
            act.wait_ge(s_got, n)
            st.add(act.activation(VTG[:, 0:NB, :], K[:, 0, :].rearrange("p (b c) -> p b c", b=NB), ACT.Copy))
            act.activation(VTG[0:TS, NB, :], K[0:TS, 1, 0:P], ACT.Copy).then_inc(s_gvtok, 1)

        def gla_gate_act(act, w, g, n):
            act.wait_ge(s_used, w.index + 1)
            act.wait_ge(s_ob, n + HEADS)
            act.activation(pair(THG), ring(g), ACT.Tanh, scale=0.5).then_inc(s_thg, 1)

        def mlstm_act(act, st):
            act.wait_ge(s_area, AREA_ML)
            with act.Fori(0, HEADS) as h:
                st.loop(h, ACT_ML)

                def w(j):
                    return Turn(W_ML, j, 2, h)

                def r(j):
                    return Turn(R_ML, j, 4, h)

                hi_of(act, w(1))
                act.wait_ge(s_used, w(0).index + 1)
                act.wait_ge(s_uc, h)
                act.wait_ge(s_mv, h)
                st.done(act.activation(UP[:, SC:SC + PAD], cols2("state_mlstm_conv", 12).rearrange(
                    "p (t k) -> p t k", k=4)[:, :, h], ACT.Copy))
                fill_padded(act, st, UP, r(0))
                conv_columns(act, st, UP, 1, h)
                act.wait_ge(s_ex, h + 1)
                act.wait_ge(s_am, h)
                act.wait_ge(s_kw, h)
                st.add(act.activation(EW[:, 0:NB, :], EW[:, 0:NB, :], ACT.Exp))
                act.activation(EW[0:TS, NB, 0:TS], EW[0:TS, NB, 0:TS], ACT.Exp).then_inc(s_ew, 1)
                hi_of(act, w(2))
                act.wait_ge(s_uc, h + 1)
                act.activation(UT, UC, ACT.Tanh, scale=0.5).then_inc(s_uct, 1)
                act.wait_ge(s_mv, h + 1)
                act.wait_ge(s_nd, h)
                st.add(act.activation(VO[:, 0:NB, 0:P], J[:, 0, :].rearrange("p (b c) -> p b c", b=NB), ACT.Copy))
                act.activation(VO[0:TS, NB, 0:P], J[0:TS, 1, 0:P], ACT.Copy).then_inc(s_vo, 1)
                act.wait_ge(s_used, w(1).index + 1)
                act.wait_ge(s_ob, h + 2 * HEADS)
                act.activation(pair(THG), ring(r(1)), ACT.Tanh, scale=0.5).then_inc(s_free[r(1).slot], 1)
                for part, s_q, dst, sc, ready in ((0, s_mq, QM, 0.5, s_qm), (1, s_mk, KM, 0.5 * RET_SCALE, s_km)):
                    p = r(2 + part)
                    act.wait_ge(s_q, h + 1)
                    act.wait_ge(s_msc, h)
                    st.add(act.activation(dst[:, 0:TP], PS[p.slot][:, 0, :], ACT.Copy, scale=sc))
                    act.activation(dst[:, TP:T], PS[p.slot][:, 1, 0:TS], ACT.Copy,
                                   scale=sc).then_inc(s_free[p.slot], 1)
                    ring_done(act, p)
                    act.sem_inc(ready, 1)
                act.wait_ge(s_bw, h + 1)
                act.wait_ge(s_cn, h)
                st.add(act.activation(WB[:, 0:TP], J[:, 0, :], ACT.Copy))
                act.activation(WB[:, TP:T], J[:, 1, 0:TS], ACT.Copy).then_inc(s_wb, 1)
                act.wait_ge(s_be, h + 1)
                act.wait_ge(s_dmax, h)
                st.add(act.activation(ENB[:, 0:TP], K[:, 0, :], ACT.Copy))
                act.activation(ENB[:, TP:T], K[:, 1, 0:TS], ACT.Copy).then_inc(s_enb, 1)
                copy_head(act, st, s_nd, h + 2 * HEADS, h + 1)
                st.add(act.activation(DD[:, 0:TP], J[:, 0, :], ACT.Abs))
                act.activation(DD[:, TP:T], J[:, 1, 0:TS], ACT.Abs).then_inc(s_dabs, 1)
                act.wait_ge(s_dmax, h + 1)
                act.activation(DD, DD, ACT.Square, scale=float(EPS) ** 0.5).then_inc(s_d2, 1)
                act.wait_ge(s_oc, h + 2 * HEADS + 1)
                act.activation(OSQ, OC, ACT.Square).then_inc(s_osq, 1)
                act.wait_ge(s_nv, h + 1)
                st.done(act.activation(NR[:, :], NV[:, :], ACT.Ln))
                act.activation(NR[:, :], NR[:, :], ACT.Exp, scale=-0.5).then_inc(s_hr0, 1)
                mixed_high(act, h + 2 * HEADS, h + 4)
            st.end(HEADS)

        def layer1_act(act):
            st = steps["act"]
            norm_act(act, 2, Turn(R_N2), lambda k: Turn(R_FFN0 + LAST_OUT, k))
            norm_high(act, 2)
            small_act(act, st)
            gla_act(act, st)
            mlstm_act(act, st)
            out_act(act, W_OUT1)
            norm_act(act, 3, Turn(R_N3), lambda k: Turn(R_OUT1, k))
            norm_high(act, 3)
            ffn_act(act, W_FFN1, R_FFN1, 2 * KD + DONE0, DONE0, last=True)
            norm_act(act, 4, Turn(R_N4), lambda k: Turn(R_FFN1 + LAST_OUT, k))
            for b in range(NB + 1):
                n = P if b < NB else TS
                p = Turn(R_Y, b)
                act.wait_ge(s_yt, b + 1)
                if b >= 2:
                    act.wait_ge(s_yout[b % 2], 16 * (b // 2))
                st.add(act.activation(YR[b % 2][0:n, 0:512], PS[p.slot][0:n, 0, :], ACT.Copy))
                act.activation(YR[b % 2][0:n, 512:D], PS[p.slot][0:n, 1, :], ACT.Copy).then_inc(s_yr, 1)
                act.wait_ge(s_yr, b + 1)
                act.sem_inc(s_free[p.slot], 1)

        def small_dve(dve, st):
            H4 = slice(0, HEADS)
            dve.wait_ge(s_area, AREA_SMALL)
            dve.wait_ge(s_rows1, 1)
            dve.wait_ge(s_small, 32)
            st.add(dve.tensor_scalar(RI[H4], RI[H4], IF_BIAS[:, 0:1], None, ALU.add))
            dve.tensor_scalar(RF[H4], RF[H4], IF_BIAS[:, 1:2], None, ALU.add).then_inc(s_rabs, 1)
            dve.wait_ge(s_rabs, 1)
            dve.wait_ge(s_rln, 1)
            st.done(dve.scalar_tensor_tensor(out=RF[H4], in0=RF[H4], scalar=0.0, in1=RA[H4], op0=ALU.min,
                                             op1=ALU.subtract))
            st.add(dve.tensor_tensor_scan(RM[H4, 0:TP], RF[H4, 0:TP], RI[H4, 0:TP], 0.0, ALU.add, ALU.max))
            st.add(dve.tensor_tensor_scan(RM[H4, TP:T], RF[H4, TP:T], RI[H4, TP:T], M0[:, 0:1], ALU.add, ALU.max))
            st.done(dve.tensor_tensor_scan(RB[H4], MASKR[H4], RF[H4], 0.0, ALU.mult, ALU.add))
            st.done(dve.tensor_tensor(RA[H4], RB[H4], RM[H4], ALU.subtract))
            dve.tensor_tensor(RB[H4], RI[H4], RB[H4], ALU.subtract).then_inc(s_rg, 1)
            dve.wait_ge(s_rg, 1)
            st.add(dve.tensor_copy(RI[H4, 0:P], RA[H4, 0:P]))
            st.add(dve.tensor_tensor(RI[H4, P:TP].rearrange("p (b c) -> p b c", c=P),
                                     RA[H4, P:TP].rearrange("p (b c) -> p b c", c=P),
                                     RM[H4, P - 1:TP - P:P].unsqueeze(2).to_broadcast([HEADS, NB - 1, P]), ALU.add))
            dve.tensor_scalar(RI[H4, TP:T], RA[H4, TP:T], M0[:, 0:1], None, ALU.add).then_inc(s_rwin, 1)
            for i in range(2):
                p = Turn(R_G, i)
                dve.wait_ge(s_gab, i + 1)
                dve.wait_ge(s_cum, i)
                dve.tensor_scalar(pair(GX), ring(p), col2("gla_b_gate", i), 0.0, ALU.add,
                                  ALU.min).then_inc(s_free[p.slot], 1)
                ring_done(dve, p)
                dve.wait_ge(s_gln, i + 1)
                st.done(dve.tensor_tensor(GX, GX, GA, ALU.subtract))
                dve.tensor_tensor_scan(CUM[:, i, :], MASK64, GX, 0.0, ALU.mult, ALU.add).then_inc(s_cum, 1)
            dve.wait_ge(s_cum, 2)

        def gla_head_dve(dve, st, i, j):
            n = 2 * i + j
            dve.wait_ge(s_gsc, n + 1)
            dve.wait_ge(s_got, n)
            dve.sem_inc(s_seen, 1)
            st.add(dve.copy_predicated(AG[:, 0:NB, :], CHUNK_MASK.unsqueeze(1).to_broadcast([P, NB, P]),
                                       J[:, 0, :].rearrange("p (b c) -> p b c", b=NB)))
            dve.copy_predicated(AG[0:TS, NB, 0:TS], CHUNK_MASK[0:TS, 0:TS], J[0:TS, 1, 0:TS]).then_inc(s_gatt, 1)

        def gla_states_dve(dve, st, i, j):
            n = 2 * i + j
            r = slice(64 * j, 64 * j + 64)
            dve.wait_ge(s_gkv, n + 1)
            st.done(dve.tensor_copy(SG8[:, 0, :], K[:, 0, 0:P]))
            for c in range(1, 2 * NB):
                last = c == 2 * NB - 1
                q = r if last else slice(0, P)
                st.done(dve.scalar_tensor_tensor(
                    out=SGF[q] if last else SG8[:, c, :], in0=SG8[q, c - 1, :], scalar=EL[q, c:c + 1],
                    in1=(K, J)[c % 2][q, 0, (c // 2) * P:(c // 2 + 1) * P], op0=ALU.mult, op1=ALU.add))
            dve.wait_ge(s_gs0, 16 * i + 16)
            dve.scalar_tensor_tensor(out=SGN[r], in0=SG0[r], scalar=EL[r, 8:9], in1=K[r, 1, 0:P],
                                     op0=ALU.mult, op1=ALU.add).then_inc(s_gst, 1)

        def low_of_head(dve, n, tile):
            dve.wait_ge(s_gah, n + 1)
            dve.tensor_tensor(GL[:, tile, :], OB, GH[:, tile, :].bitcast(F32), ALU.subtract).then_inc(s_glo, 1)

        def gla_dve(dve, st):
            dve.wait_ge(s_area, AREA_GLA)
            with dve.Fori(0, 2) as i:
                st.loop(i, DVE_PAIR)

                def w(j):
                    return Turn(W_GLA, j, 6, i)

                def r(j):
                    return Turn(R_GLA, j, 6, i)

                cum = CUM[:, i, 0:TP].rearrange("p (c l) -> p c l", l=64)
                end = CUM[:, i, 63:TP:64].unsqueeze(2).to_broadcast([P, 8, 64])
                end_s = CUM[:, i, T - 1:T].to_broadcast([P, TS])
                chunks = lambda a: a[:, 0:TP].rearrange("p (c l) -> p c l", l=64)
                dve.wait_ge(s_osq, 2 * i + HEADS)
                dve.wait_ge(s_o, 2 * i + HEADS)
                st.wait()
                st.add(dve.scalar_tensor_tensor(out=chunks(CR), in0=end, scalar=-0.5, in1=cum, op0=ALU.mult, op1=ALU.add))
                st.add(dve.scalar_tensor_tensor(out=CR[:, TP:T], in0=end_s, scalar=-0.5, in1=CUM[:, i, TP:T],
                                                op0=ALU.mult, op1=ALU.add))
                st.add(dve.tensor_tensor(chunks(LC), end, cum, ALU.subtract))
                dve.tensor_tensor(LC[:, TP:T], end_s, CUM[:, i, TP:T], ALU.subtract).then_inc(s_cr, 1)
                lo_of(dve, w(1))
                dve.wait_ge(s_ef, i + 1)
                dve.wait_ge(s_used, w(0).index + 1)
                st.add(dve.scalar_tensor_tensor(out=pair(EK4), in0=ring(r(0)), scalar=GLA_SCALE, in1=pair(EK4),
                                                op0=ALU.mult, op1=ALU.mult))
                dve.scalar_tensor_tensor(out=pair(EK1), in0=ring(r(0)), scalar=GLA_SCALE, in1=pair(EK1),
                                         op0=ALU.mult, op1=ALU.mult).then_inc(s_free[r(0).slot], 1)
                ring_done(dve, r(0))
                dve.sem_inc(s_k4, 1)
                lo_of(dve, w(2))
                dve.wait_ge(s_used, w(1).index + 1)
                dve.wait_ge(s_got, 2 * i)
                for j in range(2):
                    q = slice(64 * j, 64 * j + 64)
                    for dst, f in ((Q1[j], EQ1), (Q3[j], EQ3)):
                        ins = dve.tensor_tensor(pair(dst)[q], PS[r(1).slot][q, :, 0:HALF], pair(f)[q], ALU.mult)
                        if j and f is EQ3:
                            ins.then_inc(s_free[r(1).slot], 1)
                        else:
                            st.add(ins)
                ring_done(dve, r(1))
                dve.sem_inc(s_q3, 1)
                lo_of(dve, w(3))
                dve.wait_ge(s_gsout, 32 * i)
                gla_head_dve(dve, st, i, 0)
                lo_of(dve, w(4))
                gate_dve(dve, w(3), r(3), HEADS + 2 * i)
                lo_of(dve, w(5))
                for j in range(2):
                    n = 2 * i + j
                    gla_states_dve(dve, st, i, j)
                    if j:
                        gate_dve(dve, w(5), r(5), n + HEADS)
                    center(dve, st, n + HEADS)
                    finish_head(dve, st, n + HEADS, HGAIN[:, ds(n + 4, 1)])
                    low_of_head(dve, n + KD + DONE0, n)
                    if not j:
                        lo_of(dve, w(6))
                        gla_head_dve(dve, st, i, 1)
            st.end(2)

        def mlstm_dve(dve, st):
            dve.wait_ge(s_area, AREA_ML)
            with dve.Fori(0, HEADS) as h:
                st.loop(h, DVE_ML)

                def w(j):
                    return Turn(W_ML, j, 2, h)

                def r(j):
                    return Turn(R_ML, j, 4, h)

                lo_of(dve, w(1))
                dve.wait_ge(s_ba, h + 1)
                dve.wait_ge(s_kw, h)
                dve.wait_ge(s_am, h)
                for b in range(NB):
                    st.add(dve.scalar_tensor_tensor(out=EW[:, b, :], in0=K[:, 0, b * P:(b + 1) * P],
                                                    scalar=GTOK[:, b, ds(h, 1)], in1=NEG, op0=ALU.add, op1=ALU.add))
                dve.scalar_tensor_tensor(out=EW[0:TS, NB, 0:TS], in0=K[0:TS, 1, 0:TS],
                                         scalar=GTOK[0:TS, NB, ds(h, 1)], in1=NEG[0:TS, 0:TS], op0=ALU.add,
                                         op1=ALU.add).then_inc(s_ex, 1)
                ring_done(dve, r(0))
                convolve(dve, st, UP, UC, cols2("mlstm_conv_w", 16).rearrange("p (t k) -> p t k", k=4),
                         cols2("mlstm_conv_b", 4), h, s_uc, (s_mkt, h))
                dve.wait_ge(s_uc, h + 1)
                dve.wait_ge(s_uct, h + 1)
                dve.scalar_tensor_tensor(out=UC, in0=UT, scalar=1.0, in1=UC, op0=ALU.add,
                                         op1=ALU.mult).then_inc(s_ucs, 1)
                lo_of(dve, w(2))
                dve.wait_ge(s_nd, h)
                dve.tensor_copy(CN0[:, P:2 * P], col2("state_mlstm_n", h).to_broadcast([P, P])).then_inc(s_cn0, 1)
                dve.wait_ge(s_msc, h + 1)
                dve.wait_ge(s_ew, h + 1)
                st.add(dve.tensor_tensor(AM[:, 0:NB, :], J4(K[:, 0, :]), EW[:, 0:NB, :], ALU.mult))
                dve.tensor_tensor(AM[0:TS, NB, 0:TS], K[0:TS, 1, 0:TS], EW[0:TS, NB, 0:TS],
                                  ALU.mult).then_inc(s_am, 1)
                dve.wait_ge(s_mkt, h + 1)
                dve.wait_ge(s_cu, h)
                for b in range(NB):
                    st.add(dve.tensor_scalar(KW[:, b, :], J[:, 0, b * P:(b + 1) * P], EW[:, b, P - 1:P],
                                             0.5 * RET_SCALE, ALU.mult, ALU.mult))
                dve.tensor_scalar(KW[0:TS, NB, :], J[0:TS, 1, 0:P], EW[0:TS, NB, TS - 1:TS], 0.5 * RET_SCALE,
                                  ALU.mult, ALU.mult).then_inc(s_kw, 1)
                dve.wait_ge(s_wb, h + 1)
                dve.wait_ge(s_qm, h + 1)
                dve.tensor_tensor(QI, QM, WB, ALU.mult).then_inc(s_qi, 1)
                dve.wait_ge(s_cu, h + 1)
                dve.wait_ge(s_cout, 32 * h)
                st.done(dve.tensor_copy(CN[:, 0, :], K[:, 0, 0:256]))
                for b in range(1, NB):
                    st.done(dve.scalar_tensor_tensor(out=CN[:, b, :], in0=CN[:, b - 1, :],
                                                     scalar=WB[:, b * P + P - 1:b * P + P],
                                                     in1=K[:, b // 2, (b % 2) * 256:(b % 2) * 256 + 256],
                                                     op0=ALU.mult, op1=ALU.add))
                dve.wait_ge(s_c0, 16 * h + 16)
                dve.wait_ge(s_cn0, h + 1)
                dve.scalar_tensor_tensor(out=CNS, in0=CN0, scalar=WB[:, T - 1:T], in1=J[:, 1, 0:256],
                                         op0=ALU.mult, op1=ALU.add).then_inc(s_cn, 1)
                dve.wait_ge(s_cn, h + 1)
                st.add(dve.tensor_copy(OV[:, 1, ds(h, 1)], CN[:, NB - 1, P:P + 1]))
                st.add(dve.tensor_copy(OV[:, 1, ds(h + 4, 1)], CNS[:, P:P + 1]))
                ring_done(dve, r(1))
                dve.wait_ge(s_ob, h + 2 * HEADS)
                st.done(dve.tensor_scalar(SG, THG, 1.0, None, ALU.add))
                dve.wait_ge(s_dabs, h + 1)
                dve.tensor_tensor(DD, DD, ENB, ALU.max).then_inc(s_dmax, 1)
                center(dve, st, h + 2 * HEADS)
                dve.wait_ge(s_var, h + 2 * HEADS + 1)
                dve.wait_ge(s_d2, h + 1)
                st.add(dve.tensor_tensor(NV[:, 0:TP], K[:, 0, :], DD[:, 0:TP], ALU.add))
                dve.tensor_tensor(NV[:, TP:T], K[:, 1, 0:TS], DD[:, TP:T], ALU.add).then_inc(s_nv, 1)
                dve.wait_ge(s_nv, h + 1)
                finish_rstd(dve, st, h + 2 * HEADS, HGAIN[:, ds(h + 8, 1)])
                low_of_head(dve, h + KD + HEADS + DONE0, h + 4)
            st.end(HEADS)

        def J4(a):
            return a.rearrange("p (b c) -> p b c", b=NB)

        def layer1_dve(dve):
            st = steps["dve"]
            norm_dve(dve, 2, Turn(R_N2), MOD_TILES, MOD_TILES + KD, col1("norm_mix_g", KD, KD))
            small_dve(dve, st)
            gla_dve(dve, st)
            mlstm_dve(dve, st)
            out_dve(dve, W_OUT1, R_OUT1, MOD_TILES + 2 * KD)
            norm_dve(dve, 3, Turn(R_N3), MOD_TILES + 3 * KD, MOD_TILES + 4 * KD, col1("norm_ffn_g", KD, KD))
            ffn_dve(dve, W_FFN1, R_FFN1, 2 * KD + DONE0, DONE0, MOD_TILES + 5 * KD, None, last=True)
            norm_rstd(dve, 4, Turn(R_N4))
            for k in range(KD):
                dve.scalar_tensor_tensor(out=Y[:, k, :], in0=X[:, k, :], scalar=col1("final_norm_g", k),
                                         in1=NR[:, :], op0=ALU.mult, op1=ALU.mult).then_inc(s_y, 1)
            dve.wait_ge(s_ovt, DEPTH)
            dve.tensor_copy(OVR[:, :, :], K[0:32, 0, 0:DEPTH * P].rearrange("p (l c) -> p l c", l=DEPTH)
                            ).then_inc(s_ov, 1)

        DONE0 = sum(FFN_CUTS)
        LAST_OUT = 3 * KD + 2 * sum(FFN_CUTS) - KD

        N_ROWS = len(list(row_loads()))
        block = ctx.enter_context(nc.Block())

        @block.sync
        def _(sp):
            sp.dma_start(CST[:, :], t["constants"]).then_inc(s_cst, 16)
            sp.dma_start(XROW[:, :, :], t["x_prompt"][0].rearrange("(b p) d -> p b d", p=P)).then_inc(s_x, 16)
            sp.dma_start(XSROW[0:TS, :], t["x_sample"][0]).then_inc(s_x, 16)
            with sp.Fori(0, HEADS) as h:
                for j, (_, a) in enumerate(A_ORDER):
                    load_weight(sp, Turn(W_HEAD, j, 6, h), t["a_w_in"][0].rearrange("(k p) m -> p k m", p=P),
                                lambda: h * P + a)
                    if j == 1:
                        sp.wait_ge(s_init, 1)
                        sp.wait_ge(s_ot, h)
                        sp.dma_start(S0[:, :], t["state_ret"][0, 0, h]).then_inc(s_s0, 16)
                        sp.wait_ge(s_gi, h)
                        for part in range(2):
                            for head in range(2):
                                sp.dma_start(
                                    GW[part][64 * head:64 * head + 64, 64 * head:64 * head + 64],
                                    t["lru_gate_w"][0, 2 * h + head, :, 64 * part:64 * part + 64],
                                ).then_inc(s_gw, 16)
                sp.wait_ge(s_st, h + 1)
                sp.dma_start(out["ret_p"][0, 0, h], ST[:, NB - 1, :]).then_inc(s_sout, 16)
                sp.dma_start(out["ret_s"][0, 0, h], SN[:, :]).then_inc(s_sout, 16)
            out_loads(sp, W_OUT0, t["a_w_out"][0], KD)
            ffn_loads(sp, 0, W_FFN0)
            layer1_sync(sp)

        @block.gpsimd
        def _(pool):
            for a, v in ((ONES[:, :], 1.0), (MEAN[:, :], 1.0 / P), (EPSC[:, :], EPS), (XB[:, 0:PAD], 0.0),
                         (XB[:, TC + PAD - 1:TC + PAD], 0.0), (GW[0], 0.0), (GW[1], 0.0)):
                ins = pool.memset(a, v)
            ins.then_inc(s_init, 1)
            for g in range(MG_START):
                load_mod(pool, g, 0, 0)
            with pool.Fori(0, HEADS) as h:
                for k in range(3):
                    load_mod(pool, MG_START + k, 3, h)
            with pool.Fori(0, 2) as i:
                load_mod(pool, 24, 1, i)
            for _, n, _, _, g in ffn_parts(0, 0, 26):
                with pool.Fori(0, n) as i:
                    load_mod(pool, g, 1, i)
            layer1_pool(pool)

        @block.tensor
        def _(pe):
            pe.wait_ge(s_cst, 16)
            pe.wait_ge(s_rows, 16 * N_ROWS)
            o = 0
            for r, n in enumerate((MOD_ROWS, R1_ALL, R2_ALL)):
                ins = pe.transpose(PS[0][:, 0, o:o + n], ROWS[0:n, r, :], IDENT[0:n, 0:n])
                o += n
            ins.then_inc(s_tr, 1)
            pe.wait_ge(s_x, 32)
            for k in range(KD):
                p = Turn(R_X, k)
                pe.wait_ge(s_free[p.slot], p.before)
                for b in range(NB):
                    pe.transpose(PS[p.slot][:, 0, b * P:(b + 1) * P], XROW[:, b, k * P:(k + 1) * P], IDENT)
                pe.transpose(PS[p.slot][:, 1, 0:TS], XSROW[0:TS, k * P:(k + 1) * P],
                             IDENT[0:TS, 0:TS]).then_inc(s_tr, 1)
            pe.wait_ge(s_init, 1)
            norm_pe(pe, 0, Turn(R_N0))
            pe.wait_ge(s_cs, 1)
            for g in range(MG_START):
                mod_group(pe, g)
            pe.wait_ge(s_hnl, KD)

            with pe.Fori(0, HEADS) as h:
                def item(j, pj):
                    project(pe, Turn(W_HEAD, j, 6, h), Turn(R_HEAD, pj, 8, h))

                item(0, 0)
                item(1, 1)
                pe.wait_ge(s_kt, h + 1)
                pe.wait_ge(s_ob, h)
                transpose_blocks(pe, KT, K[:, 0, :], K[0:TS, 1, 0:P]).then_inc(s_ktr, 1)
                pe.wait_ge(s_oc, h)
                mod_group(pe, 3 * h + MG_START)
                item(2, 2)
                pe.wait_ge(s_qt, h + 1)
                pe.wait_ge(s_mod, 3 * h + MG_START + 1)
                for b in range(NB):
                    pe.matmul(J[:, 0, b * P:(b + 1) * P], KT[:, b * P:(b + 1) * P], QT[:, b * P:(b + 1) * P],
                              start=True, stop=True)
                pe.matmul(J[0:TS, 1, 0:TS], KT[:, TP:T], QT[:, TP:T], start=True, stop=True).then_inc(s_sc, 1)
                item(3, 3)
                ring_done(pe, Turn(R_HEAD, 2, 8, h))
                pe.wait_ge(s_kd, h + 1)
                transpose_blocks(pe, VT, K[:, 0, :], K[0:TS, 1, 0:P]).then_inc(s_vtr, 1)
                pe.wait_ge(s_att, h + 1)
                mod_group(pe, 3 * h + MG_START + 1)
                item(4, 4)
                pe.wait_ge(s_vtok, h + 1)
                pe.wait_ge(s_mod, 3 * h + MG_START + 2)
                for b in range(NB):
                    pe.matmul(J[:, 0, b * P:(b + 1) * P], KDT[:, b, :], VTOK[:, b, :], start=True, stop=True)
                pe.matmul(J[:, 1, TS:TS + P], KDT[0:TS, NB, :], VTOK[0:TS, NB, :],
                          start=True, stop=True).then_inc(s_kv, 1)
                pe.wait_ge(s_xc, h + 1)
                pe.wait_ge(s_gw, 64 * h + 64)
                for part, s_gate in ((0, s_gr), (1, s_gi)):
                    p = Turn(R_HEAD, 5 + part, 8, h)
                    pe.wait_ge(s_free[p.slot], p.before)
                    for half in range(2):
                        ins = pe.matmul(PS[p.slot][:, half, 0:TC // 2], GW[part],
                                        XC[:, half * (TC // 2):(half + 1) * (TC // 2)], start=True, stop=True)
                    ins.then_inc(s_gate, 1)
                pe.wait_ge(s_st, h + 1)
                pe.wait_ge(s_qd, h + 1)
                for b in range(NB):
                    pe.matmul(K[:, 0, b * P:(b + 1) * P], VTOK[:, b, :], ATT[:, b, :], start=True, stop=(b == 0))
                    if b:
                        pe.matmul(K[:, 0, b * P:(b + 1) * P], ST[:, b - 1, :], QD[:, b * P:(b + 1) * P],
                                  start=False, stop=True)
                pe.wait_ge(s_s0, 16 * h + 16)
                pe.matmul(K[:, 1, P:P + TS], VTOK[0:TS, NB, :], ATT[0:TS, NB, 0:TS], start=True, stop=False)
                pe.matmul(K[:, 1, P:P + TS], S0, QD[:, TP:T], start=False, stop=True).then_inc(s_ot, 1)
                item(5, 7)
                head_mean(pe, OT, s_o, h)
                head_var(pe, OSQ, s_osq, h)
                mod_group(pe, 3 * h + MG_START + 2)
            pe.wait_ge(s_glo, KD)
            out_pe(pe, W_OUT0, R_OUT0, KD, 24)
            norm_pe(pe, 1, Turn(R_N1))
            pe.wait_ge(s_hnl, 2 * KD)
            ffn_pe(pe, W_FFN0, R_FFN0, KD, 26)
            layer1_pe(pe)

        @block.scalar
        def _(act):
            steps["act"] = Steps(act, s_act)
            st = steps["act"]
            for dst, src in row_loads():
                act.dma_start(dst, src).then_inc(s_rows, 16)
            act.dma_start(IF_BIAS[:, :], t["mlstm_b_if"].rearrange("a (two h) -> (a h) two", two=2),
                          allow_slow_non_contiguous=True).then_inc(s_small, 16)
            act.dma_start(M0[:, :], t["state_mlstm_m"][0].rearrange("a h -> h a"),
                          allow_slow_non_contiguous=True).then_inc(s_small, 16)
            act.wait_ge(s_cols, 1)
            act.activation(CTMP[:, :, :], cols1("c_prompt", 2 * KD).rearrange("p (c k) -> p c k", c=2),
                           ACT.Tanh, scale=0.5).then_inc(s_cth, 1)
            st.done(act.activation(SP[:, 0, :], cols1("lru_lambda", 4), ACT.Abs))
            act.activation(SP[:, 0, :], SP[:, 0, :], ACT.Exp, scale=-1.0).then_inc(s_cth, 1)
            for k in range(KD):
                p = Turn(R_X, k)
                act.wait_ge(s_tr, k + 2)
                st.add(act.activation(X[:, k, 0:TP], PS[p.slot][:, 0, :], ACT.Copy))
                act.activation(X[:, k, TP:T], PS[p.slot][:, 1, 0:TS], ACT.Copy).then_inc(s_free[p.slot], 1)
            norm_act(act, 0, Turn(R_N0), lambda k: Turn(R_X, k))
            norm_high(act, 0)
            hi_of(act, Turn(W_HEAD))
            with act.Fori(0, HEADS) as h:
                st.loop(h, ACT_HEAD)

                def w(j):
                    return Turn(W_HEAD, j, 6, h)

                def r(j):
                    return Turn(R_HEAD, j, 8, h)

                hi_of(act, w(1))
                hi_of(act, w(2))
                act.wait_ge(s_ktr, h + 1)
                act.wait_ge(s_kv, h)
                st.add(act.activation(KDT[:, 0:NB, :], K[:, 0, :].rearrange("p (b c) -> p b c", b=NB), ACT.Copy,
                                      scale=CST[:, ds(2 * h + C_KD, 1)]))
                act.activation(KDT[0:TS, NB, :], K[0:TS, 1, 0:P], ACT.Copy,
                               scale=CST[0:TS, ds(2 * h + C_KD + 1, 1)]).then_inc(s_kd, 1)
                hi_of(act, w(3))
                act.wait_ge(s_used, w(2).index + 1)
                act.activation(pair(VT), ring(r(2)), ACT.Copy).then_inc(s_free[r(2).slot], 1)
                hi_of(act, w(4))
                act.wait_ge(s_used, w(3).index + 1)
                act.wait_ge(s_xc, h)
                st.done(act.activation(XB[:, SC:SC + PAD], cols1("state_lru_conv", 12).rearrange(
                    "p (t k) -> p t k", k=4)[:, :, h], ACT.Copy))
                fill_padded(act, st, XB, r(3))
                act.wait_ge(s_vtr, h + 1)
                act.wait_ge(s_ot, h)
                st.add(act.activation(VTOK[:, 0:NB, :], K[:, 0, :].rearrange("p (b c) -> p b c", b=NB), ACT.Copy))
                act.activation(VTOK[0:TS, NB, :], K[0:TS, 1, 0:P], ACT.Copy).then_inc(s_vtok, 1)
                hi_of(act, w(5))
                conv_columns(act, st, XB, 0, h)
                act.wait_ge(s_used, w(4).index + 1)
                act.wait_ge(s_ob, h)
                act.activation(pair(THG), ring(r(4)), ACT.Tanh, scale=0.5).then_inc(s_thg, 1)
                act.wait_ge(s_oa, h)
                for dst, part, s_gate in ((TR, 0, s_gr), (TI, 1, s_gi)):
                    act.wait_ge(s_gate, h + 1)
                    act.activation(dst.rearrange("p (a b) -> p a b", a=2), ring(r(5 + part), TC // 2), ACT.Tanh,
                                   bias=BRH[:, ds(h + 4 * part, 1)], scale=0.5).then_inc(s_free[r(5 + part).slot], 1)
                ring_done(act, r(5))
                st.done(act.activation(LA, TR, ACT.Exp, bias=SP[:, 4, ds(h, 1)], scale=SP[:, 4, ds(h, 1)]))
                st.add(act.activation(LTH, TR, ACT.Tanh, bias=SP[:, 5, ds(h, 1)], scale=SP[:, 5, ds(h, 1)]))
                act.activation(LA2, LA, ACT.Square).then_inc(s_la, 1)
                copy_head(act, st, s_ot, h, h + 1)
                act.wait_ge(s_lq, h + 1)
                act.activation(LS, LA2, ACT.Sqrt, scale=0.25).then_inc(s_ls, 1)
                hi_of(act, w(6))
                act.wait_ge(s_used, w(5).index + 1)
                act.activation(pair(GX2), ring(r(7)), ACT.Square).then_inc(s_gx2, 1)
                act.wait_ge(s_oc, h + 1)
                act.activation(OSQ, OC, ACT.Square).then_inc(s_osq, 1)
                act.wait_ge(s_gt2, h + 1)
                act.activation(GT, GT, ACT.Tanh, scale=GELU_A).then_inc(s_gth, 1)
                act.wait_ge(s_oa, h + 1)
                act.activation(GH[:, h, :], OA, ACT.Copy).then_inc(s_gah, 1)
                head_rstd(act, st, h)
                act.wait_ge(s_ob, h + 1)
                act.activation(GH[:, 4 + h, :], OB, ACT.Copy).then_inc(s_gah, 1)
            st.end(HEADS)
            out_act(act, W_OUT0)
            norm_act(act, 1, Turn(R_N1), lambda k: Turn(R_OUT0, k))
            norm_high(act, 1)
            ffn_act(act, W_FFN0, R_FFN0, KD, 0)
            layer1_act(act)

        @block.vector
        def _(dve):
            steps["dve"] = Steps(dve, s_dve)
            st = steps["dve"]
            dve.sem_inc(s_lo, 1)
            dve.wait_ge(s_tr, 1)
            dve.tensor_copy(COLS[:, :], PS[0][:, 0, 0:MOD_ROWS + R1_ALL + R2_ALL]).then_inc(s_free[0], 1)
            ring_done(dve, Turn(R_PAR))
            dve.tensor_scalar(BRH[:, :], cols1("lru_gate_b", 8), 0.5, None, ALU.mult).then_inc(s_cols, 1)
            st.add(dve.tensor_scalar(HGAIN[:, 0:4], cols1("ret_gn_g", 4), 0.5, None, ALU.mult))
            st.add(dve.tensor_scalar(HGAIN[:, 4:8], cols2("gla_gn_g", 4), 0.5, None, ALU.mult))
            st.add(dve.tensor_scalar(HGAIN[:, 8:12], cols2("mlstm_gn_g", 4), 0.5, None, ALU.mult))
            dve.wait_ge(s_cth, 1)
            c = cols1("c_prompt", 2 * KD).rearrange("p (c k) -> p c k", c=2)
            st.done(dve.scalar_tensor_tensor(out=CS[:, :, :], in0=CTMP[:, :, :], scalar=1.0, in1=c,
                                             op0=ALU.add, op1=ALU.mult))
            dve.tensor_scalar(CS[:, :, :], CS[:, :, :], 0.5, None, ALU.mult).then_inc(s_cs, 1)
            dve.wait_ge(s_cth, 2)
            e, s, z, y = SP[:, 0, :], SP[:, 1, :], SP[:, 2, :], SP[:, 3, :]
            st.done(dve.tensor_scalar(z, e, 2.0, None, ALU.add))
            st.done(dve.reciprocal(z, z))
            st.done(dve.tensor_tensor(s, e, z, ALU.mult))
            st.done(dve.tensor_tensor(z, s, s, ALU.mult))
            st.done(dve.tensor_scalar(y, z, 1.0 / 19.0, None, ALU.mult))
            for k in range(8, 0, -1):
                st.done(dve.scalar_tensor_tensor(out=y, in0=y, scalar=1.0 / (2 * k + 1), in1=z,
                                                 op0=ALU.add, op1=ALU.mult))
            st.done(dve.scalar_tensor_tensor(out=y, in0=y, scalar=1.0, in1=s, op0=ALU.add, op1=ALU.mult))
            st.done(dve.tensor_scalar(z, cols1("lru_lambda", 4), -1.0, 0.0, ALU.mult, ALU.max))
            st.done(dve.scalar_tensor_tensor(out=y, in0=y, scalar=2.0, in1=z, op0=ALU.mult, op1=ALU.add))
            st.add(dve.tensor_scalar(SP[:, 4, :], y, -4.0, None, ALU.mult))
            st.done(dve.tensor_scalar(SP[:, 5, :], y, 4.0, None, ALU.mult))
            for g in range(MG_START):
                mod_read(dve, g)
            dve.wait_ge(s_mod, MG_START)
            norm_dve(dve, 0, Turn(R_N0), 0, KD, cols1("norm_mix_g", KD))
            lo_of(dve, Turn(W_HEAD))
            with dve.Fori(0, HEADS) as h:
                st.loop(h, DVE_HEAD)

                def w(j):
                    return Turn(W_HEAD, j, 6, h)

                def r(j):
                    return Turn(R_HEAD, j, 8, h)

                def rotate(j, dst, ready):
                    dve.wait_ge(s_used, w(j).index + 1)
                    dve.wait_ge(s_kt if j else s_qt, h + j)
                    p = PS[r(j).slot]
                    st.add(dve.tensor_tensor(pair(ROTA), ring(r(j)), pair(COS), ALU.mult))
                    st.add(dve.tensor_tensor(pair(ROTB)[0:64], p[64:P, :, 0:HALF], pair(SIN)[64:P], ALU.mult))
                    dve.tensor_tensor(pair(ROTB)[64:P], p[0:64, :, 0:HALF], pair(SIN)[0:64],
                                      ALU.mult).then_inc(s_free[r(j).slot], 1)
                    ring_done(dve, r(j))
                    dve.wait_ge(s_sc, h)
                    dve.tensor_tensor(dst, ROTA, ROTB, ALU.add).then_inc(ready, 1)

                lo_of(dve, w(1))
                rotate(0, KT, s_kt)
                lo_of(dve, w(2))
                rotate(1, QT, s_qt)
                dve.wait_ge(s_qt, h + 1)
                dve.wait_ge(s_ot, h)
                blk = lambda a: a[:, 0:TP].rearrange("p (b c) -> p b c", b=NB)
                st.add(dve.tensor_tensor(blk(QD), blk(QT), QDEC[:, h, :].unsqueeze(1).to_broadcast([P, NB, P]),
                                         ALU.mult))
                dve.tensor_tensor(QD[:, TP:T], QT[:, TP:T], QDEC[:, h, 0:TS], ALU.mult).then_inc(s_qd, 1)
                mod_read(dve, 3 * h + MG_START)
                lo_of(dve, w(3))
                dve.wait_ge(s_sc, h + 1)
                st.add(dve.tensor_tensor(ATT[:, 0:NB, :], blk(J[:, 0, :]),
                                         DECAY[:, h, :].unsqueeze(1).to_broadcast([P, NB, P]), ALU.mult))
                dve.tensor_tensor(ATT[0:TS, NB, 0:TS], J[0:TS, 1, 0:TS], DECAY[0:TS, h, 0:TS],
                                  ALU.mult).then_inc(s_att, 1)
                lo_of(dve, w(4))
                ring_done(dve, r(3))
                convolve(dve, st, XB, XC, cols1("lru_conv_w", 16).rearrange("p (t k) -> p t k", k=4),
                         cols1("lru_conv_b", 4), h, s_xc, (s_gi, h))
                mod_read(dve, 3 * h + MG_START + 1)
                lo_of(dve, w(5))
                dve.wait_ge(s_kv, h + 1)
                dve.wait_ge(s_ot, h)
                dve.wait_ge(s_sout, 32 * h)
                st.done(dve.tensor_copy(ST[:, 0, :], J[:, 0, 0:P]))
                for b in range(1, NB):
                    st.done(dve.scalar_tensor_tensor(out=ST[:, b, :], in0=ST[:, b - 1, :],
                                                     scalar=CST[:, ds(2 * h + C_SD, 1)],
                                                     in1=J[:, 0, b * P:(b + 1) * P], op0=ALU.mult, op1=ALU.add))
                dve.wait_ge(s_s0, 16 * h + 16)
                dve.scalar_tensor_tensor(out=SN, in0=S0, scalar=CST[:, ds(2 * h + C_SD + 1, 1)],
                                         in1=J[:, 1, TS:TS + P], op0=ALU.mult, op1=ALU.add).then_inc(s_st, 1)
                gate_dve(dve, w(4), r(4), h)
                dve.wait_ge(s_la, h + 1)
                dve.scalar_tensor_tensor(out=LA2, in0=LA2, scalar=1.0, in1=LTH, op0=ALU.add,
                                         op1=ALU.mult).then_inc(s_lq, 1)
                ring_done(dve, r(6))
                st.add(dve.scalar_tensor_tensor(out=LB, in0=TI, scalar=1.0, in1=XC, op0=ALU.add, op1=ALU.mult))
                lo_of(dve, w(6))
                dve.wait_ge(s_ls, h + 1)
                st.wait()
                st.done(dve.tensor_tensor(LB, LB, LS, ALU.mult))
                st.add(dve.tensor_tensor_scan(HS[:, 0:TP], LA[:, 0:TP], LB[:, 0:TP], 0.0, ALU.mult, ALU.add))
                st.done(dve.tensor_tensor_scan(HS[:, SC:SC + TS], LA[:, SC:SC + TS], LB[:, SC:SC + TS],
                                               col1("state_lru_h", h), ALU.mult, ALU.add))
                st.add(dve.tensor_copy(OV[:, 0, ds(h, 1)], HS[:, TP - 1:TP]))
                st.add(dve.tensor_copy(OV[:, 0, ds(h + 4, 1)], HS[:, SC + TS - 1:SC + TS]))
                dve.wait_ge(s_gx2, h + 1)
                st.done(dve.tensor_scalar(GT, GX2, GELU_B, 1.0, ALU.mult, ALU.add))
                dve.tensor_tensor(pair(GT), ring(r(7)), pair(GT), ALU.mult).then_inc(s_gt2, 1)
                center(dve, st, h)
                dve.wait_ge(s_gth, h + 1)
                dve.scalar_tensor_tensor(out=pair(GX2), in0=pair(GT), scalar=1.0, in1=ring(r(7)),
                                         op0=ALU.add, op1=ALU.mult).then_inc(s_free[r(7).slot], 1)
                ring_done(dve, r(7))
                st.add(dve.scalar_tensor_tensor(out=OA[:, 0:TP], in0=GX2[:, 0:TP], scalar=0.5, in1=HS[:, 0:TP],
                                                op0=ALU.mult, op1=ALU.mult))
                dve.scalar_tensor_tensor(out=OA[:, TP:T], in0=GX2[:, TP:T], scalar=0.5, in1=HS[:, SC:SC + TS],
                                         op0=ALU.mult, op1=ALU.mult).then_inc(s_oa, 1)
                dve.wait_ge(s_gah, 2 * h + 1)
                dve.tensor_tensor(GL[:, h, :], OA, GH[:, h, :].bitcast(F32), ALU.subtract).then_inc(s_glo, 1)
                mod_read(dve, 3 * h + MG_START + 2)
                finish_head(dve, st, h, HGAIN[:, ds(h, 1)])
                dve.wait_ge(s_gah, 2 * h + 2)
                dve.tensor_tensor(GL[:, 4 + h, :], OB, GH[:, 4 + h, :].bitcast(F32),
                                  ALU.subtract).then_inc(s_glo, 1)
            st.end(HEADS)
            out_dve(dve, W_OUT0, R_OUT0, 2 * KD, 24)
            norm_dve(dve, 1, Turn(R_N1), 3 * KD, 4 * KD, cols1("norm_ffn_g", KD))
            ffn_dve(dve, W_FFN0, R_FFN0, KD, 0, 5 * KD, 26)
            layer1_dve(dve)



_INS = ['x_prompt', 'x_sample', 'c_prompt', 'c_sample', 'state_lru_h', 'state_lru_conv', 'state_ret', 'state_gla',
        'state_mlstm_C', 'state_mlstm_n', 'state_mlstm_m', 'state_mlstm_conv', 'w_mod', 'b_mod', 'norm_mix_g',
        'norm_ffn_g', 'w_ffn_in', 'w_ffn_out', 'final_norm_g', 'a_w_in', 'a_w_out', 'lru_conv_w', 'lru_conv_b',
        'lru_gate_w', 'lru_gate_b', 'lru_lambda', 'ret_gn_g', 'c_w_in', 'c_w_out', 'gla_w_gate', 'gla_b_gate',
        'gla_gn_g', 'mlstm_conv_w', 'mlstm_conv_b', 'mlstm_w_qk', 'mlstm_w_v', 'mlstm_b_if', 'mlstm_gn_g']
_OUTS = [('y_p', (1, TP, D)), ('y_s', (1, TS, D))] + [
    (name + group, shape) for group in ('_p', '_s') for name, shape in (
        ('lru_h', (1, 1, 512)), ('lru_conv', (1, 1, PAD, 512)), ('ret', (1, 1, HEADS, P, P)),
        ('gla', (1, 1, HEADS, 64, P)), ('C', (1, 1, HEADS, P, P)), ('n', (1, 1, HEADS, P)), ('m', (1, 1, HEADS)),
        ('conv', (1, 1, PAD, 512)))]


def kernel(**inputs):
    import concourse.bacc as _bacc
    from concourse.bass_utils import run_bass_kernel_spmd as _run

    nc = _bacc.Bacc("TRN2", target_bir_lowering=False, num_devices=1)
    arrays, ins, outs = {}, {}, {}
    for name in _INS:
        arrays["in_" + name] = np.ascontiguousarray(inputs[name])
    arrays["in_constants"] = constants()
    arrays["in_selectors"] = selectors()
    for key, a in arrays.items():
        ins[key[3:]] = nc.dram_tensor(key, a.shape, F32, kind="ExternalInput").ap()
    for name, shape in _OUTS:
        outs[name] = nc.dram_tensor("out_" + name, shape, F32, kind="ExternalOutput").ap()
    encoder(nc, ins, outs)
    r = _run(nc, [arrays], core_ids=[0])
    return tuple(r.results[0]["out_" + name] for name, _ in _OUTS)
```

```python
from contextlib import ExitStack

import numpy as np

import concourse.bass as bass
import concourse.mybir as mybir

F32 = mybir.dt.float32
F32R = mybir.dt.float32r
U32 = mybir.dt.uint32
ACT = mybir.ActivationFunctionType
ALU = mybir.AluOpType
ds = bass.ds

P = 128
D = 1024
KD = D // P
TP, TS = 512, 32
T = TP + TS
HALF = T // 2
CONV = 4
PAD = CONV - 1
TC = T + PAD + 1
SC = TP + PAD
DEPTH = 2
DFF = 2816
FFN_CUTS = (8, 8, 6)
HEADS = 4
NB = TP // P
MOD_TILES = 6 * KD
EPS = 1e-6
BIG = 1e30

RET_SCALE = float(P) ** -0.5
GLA_SCALE = float(64) ** -0.5
GLA_TAU = 16.0
GELU_A, GELU_B = 0.7978845608028654, 0.044715

C_ID, C_COS, C_SIN = 0, P, P + T
C_DEC = C_SIN + T
C_QD = C_DEC + HEADS * P
C_KD = C_QD + HEADS * P
C_SD = C_KD + 2 * HEADS
C_NEG = C_SD + 2 * HEADS
C_MASK = C_NEG + P
C_ALL = C_MASK + P
EARLY_BUFS = 5
AREA_ALL = 16168

R1 = {}
R2 = {}
_n = 0
for _name, _k in (("norm_mix_g", 16), ("norm_ffn_g", 16), ("final_norm_g", 8), ("lru_conv_w", 16),
                  ("lru_conv_b", 4), ("lru_gate_b", 8), ("lru_lambda", 4), ("ret_gn_g", 4),
                  ("state_lru_h", 4), ("state_lru_conv", 12), ("c_prompt", 8), ("c_sample", 8)):
    R1[_name] = _n
    _n += _k
R1_ALL = _n
_n = 0
for _name, _k in (("gla_b_gate", 2), ("gla_gn_g", 4), ("mlstm_conv_w", 16), ("mlstm_conv_b", 4),
                  ("mlstm_gn_g", 4), ("state_mlstm_conv", 12), ("state_mlstm_n", 4)):
    R2[_name] = _n
    _n += _k
R2_ALL = _n
MOD_ROWS = DEPTH * MOD_TILES

A_ORDER = (("k", 1536), ("q", 1024), ("v", 2048), ("xb", 0), ("g", 2560), ("gb", 512))


def constants():
    c = np.zeros((P, C_ALL), np.float32)
    c[:, C_ID:C_ID + P] = np.eye(P)
    half = P // 2
    inv = np.float32(10000.0) ** (-np.arange(half, dtype=np.float32) / np.float32(half))
    pos = np.concatenate([np.arange(TP), 256 + np.arange(TS)]).astype(np.float32)
    ang = (pos[None, :] * inv.astype(np.float32)[:, None]).astype(np.float32).astype(np.float64)
    c[:half, C_COS:C_COS + T] = c[half:, C_COS:C_COS + T] = np.cos(ang)
    c[:half, C_SIN:C_SIN + T] = np.sin(ang)
    c[half:, C_SIN:C_SIN + T] = -np.sin(ang)
    lg = np.log1p(-np.exp2(-5.0 - np.arange(HEADS))).astype(np.float32).astype(np.float64)
    s, l = np.arange(P)[:, None], np.arange(P)[None, :]
    for h in range(HEADS):
        c[:, C_DEC + h * P:C_DEC + (h + 1) * P] = np.where(l >= s, np.exp((l - s) * lg[h]), 0) * RET_SCALE
        c[:, C_QD + h * P:C_QD + (h + 1) * P] = np.exp((l + 1) * lg[h])
        c[:, C_KD + 2 * h] = np.exp((P - 1 - np.arange(P)) * lg[h]) * RET_SCALE
        c[:TS, C_KD + 2 * h + 1] = np.exp((TS - 1 - np.arange(TS)) * lg[h]) * RET_SCALE
        c[:, C_SD + 2 * h] = np.exp(P * lg[h])
        c[:, C_SD + 2 * h + 1] = np.exp(TS * lg[h])
    c[:, C_NEG:C_NEG + P] = np.where(l >= s, 0.0, -BIG)
    c[:, C_MASK:C_MASK + P] = (l >= s) & (l // 64 == s // 64)
    return c


def selectors():
    s = np.zeros((HEADS, HEADS, P), np.float32)
    for h in range(HEADS):
        s[h, h] = 1.0
    return s


ACT_HEAD, DVE_HEAD, ACT_PAIR, DVE_PAIR, ACT_ML, DVE_ML = 11, 29, 12, 41, 14, 26 


class Turn:

    def __init__(self, base, j=0, per=0, i=0):
        self.slot = (base + j) % 2
        self.before = (base + j) // 2 + (per // 2) * i
        self.index = base + j + per * i


class Steps:

    def __init__(self, eng, sem):
        self.eng, self.sem, self.n, self.i, self.per = eng, sem, 0, 0, 0

    def loop(self, i, per):
        self.i, self.per, self.start = i, per, self.n

    def end(self, count):
        assert self.n - self.start == self.per, self.n - self.start
        self.n, self.i, self.per = self.start + self.per * count, 0, 0

    def add(self, ins):
        ins.then_inc(self.sem, 1)
        self.n += 1

    def wait(self):
        self.eng.wait_ge(self.sem, self.n + self.per * self.i if self.per else self.n)

    def done(self, ins):
        self.add(ins)
        self.wait()


def encoder(nc, t, out):
    with ExitStack() as ctx:
        def sb(name, shape, dt=F32):
            return ctx.enter_context(nc.sbuf_tensor(name, shape, dt))

        def sem(name):
            return ctx.enter_context(nc.semaphore(name))

        CST = sb("constants", [P, C_ALL])
        IDENT = CST[:, C_ID:C_ID + P]
        COS, SIN = CST[:, C_COS:C_COS + T], CST[:, C_SIN:C_SIN + T]
        DECAY = CST[:, C_DEC:C_DEC + HEADS * P].rearrange("p (h l) -> p h l", h=HEADS)
        QDEC = CST[:, C_QD:C_QD + HEADS * P].rearrange("p (h l) -> p h l", h=HEADS)
        NEG = CST[:, C_NEG:C_NEG + P]
        CHUNK_MASK = CST[:, C_MASK:C_MASK + P].bitcast(U32)
        ONES = sb("ones", [P, P])
        MEAN = sb("mean_matrix", [P, P])
        EPSC = sb("eps_column", [P, 1])
        ROWS = sb("param_rows", [P, 4, P])
        ACC = ROWS[:, :, :].rearrange("p (c m) n -> p c (m n)", c=2)
        COLS = sb("param_columns", [P, MOD_ROWS + R1_ALL + R2_ALL])
        BMOD = COLS[:, 0:MOD_ROWS]
        IF_BIAS = sb("if_bias", [HEADS, 2])
        M0 = sb("m_state", [HEADS, 1])

        def col1(name, k, n=1):
            a = MOD_ROWS + R1[name] + k
            return COLS[:, ds(a, n)]

        def cols1(name, n):
            a = MOD_ROWS + R1[name]
            return COLS[:, a:a + n]

        def cols2(name, n):
            a = MOD_ROWS + R1_ALL + R2[name]
            return COLS[:, a:a + n]

        def col2(name, k, n=1):
            a = MOD_ROWS + R1_ALL + R2[name] + k
            return COLS[:, ds(a, n)]

        CS = sb("silu_c", [P, 2, KD])
        CTMP = sb("silu_c_tanh", [P, 2, KD])
        MOD = sb("modulation", [P, DEPTH * MOD_TILES, 2])
        GAIN = sb("norm_gain", [P, KD, 2])
        X = sb("residual", [P, KD, T])
        HNH = sb("normed_high", [P, KD, T], F32R)
        HNL = sb("normed_low", [P, KD, T], F32R)
        GH = sb("mixed_high", [P, KD, T], F32R)
        GL = sb("mixed_low", [P, KD, T], F32R)
        RAW = [sb(f"weight_raw{s}", [P, KD, P]) for s in range(2)]
        WH = [sb(f"weight_high{s}", [P, KD, P], F32R) for s in range(2)]
        WL = [sb(f"weight_low{s}", [P, KD, P], F32R) for s in range(2)]
        MW = sb("mod_weight", [P, KD, 2 * P])
        SP = sb("softplus", [P, 6, 4])
        BRH = sb("half_gate_bias", [P, 8])
        HGAIN = sb("half_head_gains", [P, 12])
        OV = sb("vector_outputs", [P, DEPTH, 32])
        NV = sb("norm_value", [P, T])
        NR = sb("norm_rstd", [P, T])
        NT = sb("norm_step", [P, T])
        TMP = sb("norm_temp", [P, 2, T])
        AREA = sb("mixer_area", [P, AREA_ALL])
        mark = [0]

        def area(*shape):
            n = int(np.prod(shape))
            a = AREA[:, mark[0]:mark[0] + n]
            mark[0] += n
            assert mark[0] <= AREA_ALL, mark[0]
            return a.rearrange("p (a b) -> p a b", a=shape[0]) if len(shape) == 2 else a

        OT, OC, OSQ, OB = area(T), area(T), area(T), area(T)
        THG, SG = area(T), area(T)
        common = mark[0]
        ROTA, ROTB = area(T), area(T)
        KT, QT, VT, QD = area(T), area(T), area(T), area(T)
        KDT = area(NB + 1, P)
        VTOK = area(NB + 1, P)
        ATT = area(NB + 1, P)
        ST = area(NB, P)
        S0, SN = area(P), area(P)
        XB = area(TC + PAD)
        XC, TR, TI = area(TC), area(TC), area(TC)
        LA, LTH, LA2, LB, LS = area(TC), area(TC), area(TC), area(TC), area(TC)
        HS = LA2
        GX2, GT, OA = area(T), area(T), area(T)
        GW = [area(P), area(P)]
        mark[0] = common
        CUM = area(2, T)
        RI, RF, RM, RB, RA = area(T), area(T), area(T), area(T), area(T)
        GTOK = area(NB + 1, HEADS)
        layer1 = mark[0]
        CR, LC = OT, OC
        EQ1, EK1, EQ3, EK4 = area(T), area(T), area(T), area(T)
        Q1, Q3 = [area(T), area(T)], [area(T), area(T)]
        EL = area(16)
        VG = area(T)
        K4T, VTG, AG = area(NB + 1, P), area(NB + 1, P), area(NB + 1, P)
        SG8 = area(8, P)
        SG0, SGN, SGF = area(P), area(P), area(P)
        mark[0] = layer1
        WGATE, GLR = area(2 * P), area(T)
        MASK64, MASKR = area(T), area(T)
        GA, GX = area(T), area(T)
        mark[0] = layer1
        UP, UC, UT = area(TC + PAD), area(TC), area(TC)
        QM, KM, QI = area(T), area(T), area(T)
        VO = area(NB + 1, 2 * P)
        CN = area(NB, 2 * P)
        CN0, CNS = area(2 * P), area(2 * P)
        EW, AM, KW = area(NB + 1, P), area(NB + 1, P), area(NB + 1, P)
        WB = area(T)
        ENB, DD = CUM[:, 0, :], CUM[:, 1, :]
        WQK, WV = area(2 * P), area(P)
        SEL = area(P)
        mark[0] = 0
        Y = area(KD, T)
        YR = [area(D), area(D)]
        OVR = area(DEPTH, P)[0:32]
        XROW = AREA[:, 0:NB * D].rearrange("p (b d) -> p b d", b=NB)
        XSROW = AREA[:, NB * D:(NB + 1) * D]
        mark[0] = (NB + 1) * D
        EARLY = [area(KD, 2 * P) for _ in range(EARLY_BUFS)]

        PS = [ctx.enter_context(nc.psum_tensor(f"ring{s}", [P, 2, 512], F32)) for s in range(2)]
        K = ctx.enter_context(nc.psum_tensor("core_k", [P, 2, 512], F32))
        J = ctx.enter_context(nc.psum_tensor("core_j", [P, 2, 512], F32))
        MODPS = J[:, 1, 256:260]
        NORM_BUF = [TMP[:, 0, :], TMP[:, 1, :], NV[:, :], NT[:, :]]

        s_id, s_cst, s_rows, s_small, s_x = sem("identity_in"), sem("constants_in"), sem("rows_in"), sem("small_in"), sem("x_in")
        s_init, s_clear = sem("memory_set"), sem("pads_cleared")
        s_raw = [sem(f"weight_in{s}") for s in range(2)]
        s_mw = sem("mod_weight_in")
        s_mwh = [sem(f"mod_half_in{s}") for s in range(2)]
        s_early = [sem(f"early_mod_weight_in{s}") for s in range(EARLY_BUFS)]
        s_hi, s_lo, s_used = sem("weight_high"), sem("weight_low"), sem("product_done")
        s_free = [sem(f"ring_free{s}") for s in range(2)]
        s_modu, s_mod, s_direct = sem("mod_product"), sem("mod_ready"), sem("direct_mod_product")
        s_dparts = sem("early_mod_parts")
        s_part, s_half, s_glf = sem("mod_part_step"), sem("mod_wait"), sem("hidden_low_done")
        s_tr = sem("transposed")
        s_cols, s_cs, s_cth = sem("columns_ready"), sem("silu_c_ready"), sem("silu_c_tanh_ready")
        s_sq, s_add, s_squ = sem("squared"), sem("square_added"), sem("squares_summed")
        s_ln, s_hln = sem("norm_log"), sem("head_norm_log")
        s_r0, s_hf, s_hnh, s_hnl = sem("rstd_start"), sem("normed"), sem("normed_high"), sem("normed_low")
        s_dve, s_act = sem("vector_step"), sem("scalar_step")
        s_kt, s_qt, s_qd = sem("k_rotated"), sem("q_rotated"), sem("q_decayed")
        s_ktr, s_kd, s_sc, s_att = sem("k_transposed"), sem("k_by_token"), sem("scores"), sem("attention")
        s_vtr, s_vtok, s_kv, s_st = sem("v_transposed"), sem("v_by_token"), sem("kv"), sem("states")
        s_ot, s_o, s_mean, s_oc = sem("head_out"), sem("head_out_copied"), sem("head_mean"), sem("centered")
        s_osq, s_var, s_hr0, s_ob = sem("centered_squared"), sem("head_var"), sem("head_rstd_start"), sem("head_done")
        s_thg = sem("gate_tanh")
        s_xb, s_xc, s_gw, s_s0, s_sout = sem("xb_ready"), sem("conv_done"), sem("gate_weights_in"), sem("state_in"), sem("state_out")
        s_gr, s_gi, s_la, s_lq, s_ls = sem("r_gate"), sem("i_gate"), sem("decay_ready"), sem("one_minus_a2"), sem("root_ready")
        s_gx2, s_gt2, s_gth, s_oa = sem("gelu_square"), sem("gelu_inner"), sem("gelu_tanh"), sem("lru_done")
        s_gah, s_ov, s_ovt, s_out = sem("mixed_high_done"), sem("vectors_ready"), sem("vectors_transposed"), sem("output_written")
        s_glo = sem("mixed_low_done")
        s_seen, s_asked = sem("scores_seen"), sem("weight_asked")
        s_yout = [sem(f"y_written{b}") for b in range(2)]
        s_fth = sem("ffn_tanh")
        s_area, s_smw, s_wg = sem("area_cleared"), sem("small_weights_in"), sem("decay_weights_in")
        s_rows1, s_rabs, s_rln, s_rwin = sem("gate_rows"), sem("gate_rows_biased"), sem("gate_rows_log"), sem("gate_rows_in")
        s_rg, s_gt, s_gtok, s_rexp = sem("gate_rows_ready"), sem("gate_transposed"), sem("gate_by_token"), sem("gate_rows_exp")
        s_gp, s_gab, s_gln, s_cum = sem("decay_product"), sem("decay_abs"), sem("decay_log"), sem("decay_sums")
        s_cr, s_ef, s_k4, s_q3 = sem("decay_centered"), sem("decay_factors"), sem("gla_keys"), sem("gla_queries")
        s_k4t, s_k4tok = sem("gla_keys_transposed"), sem("gla_keys_by_token")
        s_gsc, s_gatt, s_gvt, s_gvtok = sem("gla_scores"), sem("gla_attention"), sem("gla_v_transposed"), sem("gla_v_by_token")
        s_gkv, s_gst, s_got, s_gs0, s_gsout = sem("gla_kv"), sem("gla_states"), sem("gla_out"), sem("gla_state_in"), sem("gla_state_out")
        s_mw2, s_c0, s_cout, s_uc, s_uct, s_ucs = (sem("mlstm_weights_in"), sem("mlstm_state_in"), sem("mlstm_state_out"),
                                                   sem("mlstm_conv"), sem("mlstm_conv_tanh"), sem("mlstm_conv_silu"))
        s_ba, s_ex, s_ew, s_mv, s_vo, s_bw, s_wb = (sem("gate_spread"), sem("exponent"), sem("weights_exp"), sem("mlstm_v"),
                                                    sem("mlstm_v_ready"), sem("win_spread"), sem("win_ready"))
        s_mq, s_mk, s_qm, s_km, s_qi = (sem("mlstm_q"), sem("mlstm_k"), sem("mlstm_q_ready"), sem("mlstm_k_ready"),
                                        sem("mlstm_q_weighted"))
        s_msc, s_am, s_mkt, s_kw, s_be, s_enb = (sem("mlstm_scores"), sem("mlstm_attention"), sem("mlstm_k_tokens"),
                                                 sem("mlstm_k_weighted"), sem("floor_spread"), sem("floor_ready"))
        s_cu, s_cn, s_cn0, s_nd, s_dabs, s_dmax, s_d2, s_nv = (
            sem("mlstm_update"), sem("mlstm_states"), sem("mlstm_n_spread"), sem("mlstm_out"), sem("den_abs"),
            sem("den_floored"), sem("den_squared"), sem("variance_plus"))
        s_hmo, s_y, s_yt, s_yr = sem("mlstm_gate"), sem("y_ready"), sem("y_transposed"), sem("y_rows")

        W_HEAD, W_OUT0, W_FFN0 = 0, 24, 32
        psn = [0]

        steps = {}


        def take(n):
            psn[0] += n
            return psn[0] - n

        R_PAR, R_X, R_N0 = take(1), take(KD), take(1)
        R_HEAD, R_OUT0 = take(HEADS * 8), take(KD)
        R_N1 = take(1)
        R_FFN0 = take(3 * KD + 2 * sum(FFN_CUTS))
        R_N2, R_SM, R_G = take(1), take(1), take(2)
        R_GLA = take(2 * 6)
        R_ML = take(HEADS * 4)
        R_OUT1, R_N3 = take(KD), take(1)
        R_FFN1 = take(3 * KD + 2 * sum(FFN_CUTS))
        R_N4, R_Y = take(1), take(NB + 1)
        W1 = W_FFN0 + 3 * KD + 2 * sum(FFN_CUTS)
        W_SM, W_GLA, W_ML = W1, W1 + 1, W1 + 13
        W_OUT1, W_FFN1 = W_ML + 2 * HEADS, W_ML + 2 * HEADS + KD
        MG_NORM, MG_DIRECT = 8, 6
        MG_PE = 3
        DACC = [AREA[:, j * 4 * P:(j + 1) * 4 * P].rearrange("p (c m) -> p c m", c=2)
                for j in range(MG_DIRECT - MG_PE)]

        def pair(a):
            return a[:, :T].rearrange("p (a b) -> p a b", a=2)

        def ring(p, n=HALF):
            return PS[p.slot][:, :, 0:n]

        def ring_done(eng, p):
            eng.wait_ge(s_free[p.slot], p.before + 1)

        def hi_of(act, n):
            if isinstance(n.index, int) and n.index == W_SM:
                act.wait_ge(s_smw, 32)
            act.wait_ge(s_raw[n.slot], 16 * (n.before + 1))
            act.wait_ge(s_used, n.index - 1 if not isinstance(n.index, int) else max(n.index - 1, 0))
            act.activation(WH[n.slot][:], RAW[n.slot][:], ACT.Copy).then_inc(s_hi, 1)

        def lo_of(dve, n):
            dve.wait_ge(s_hi, n.index + 1)
            dve.tensor_tensor(WL[n.slot][:], RAW[n.slot][:], WH[n.slot][:].bitcast(F32),
                              ALU.subtract).then_inc(s_lo, 1)

        def load_weight(q, n, src, a):
            q.wait_ge(s_lo, n.index)
            q.sem_inc(s_asked, 1)
            src = src[:, :, ds(a(), P)]
            q.dma_start(RAW[n.slot][:, 0:src.shape[1], :], src).then_inc(s_raw[n.slot], 16)

        def mod_source(l, a0):
            return t["w_mod"][l].rearrange("(k p) m -> p k m", p=P)[:, :, ds(a0, 2 * P)]

        def load_early(q, g):
            if g >= EARLY_BUFS:
                q.wait_ge(s_direct, g - EARLY_BUFS + 1)
            q.dma_start(EARLY[g % EARLY_BUFS], mod_source(0, g * 2 * P)).then_inc(s_early[g % EARLY_BUFS], 16)

        def mod_direct(pe, w, dst):
            for s in range(2):
                for k in range(KD):
                    mm = pe.matmul(dst[:, 2 * s:2 * s + 2], w[:, k, s * P:(s + 1) * P], CS[:, :, k],
                                   start=(k == 0), stop=(k == KD - 1))
            return mm

        def mod_early(pe, g):
            pe.wait_ge(s_early[g % EARLY_BUFS], 16 * (g // EARLY_BUFS + 1))
            mod_direct(pe, EARLY[g % EARLY_BUFS], J[:, 1, 4 * g:4 * g + 4]).then_inc(s_direct, 1)

        def load_mod(pool, l, g):
            pool.dma_start(MW[:, :, :], t["w_mod"][l].rearrange("(k p) m -> p k m", p=P)[:, :, ds(g() * 2 * P, 2 * P)]
                           ).then_inc(s_mw, 16)

        def load_half(pool, g, half):
            pool.dma_start(MW[:, 4 * half:4 * half + 4, :],
                           t["w_mod"][1].rearrange("(k p) m -> p k m", p=P)[:, 4 * half:4 * half + 4, ds(g() * 2 * P, 2 * P)]
                           ).then_inc(s_mwh[half], 16)

        def mod_parts(dve, g, piece):
            n = g - MOD_TILES // 2
            if piece == 0:
                dve.wait_ge(s_mod, g)
            if piece % 2 == 0:
                dve.wait_ge(s_mwh[piece // 2], 16 * n + 16)
            for k in (2 * piece, 2 * piece + 1):
                for c in range(2):
                    w, x = MW[:, k, :], CS[:, c, k:k + 1]
                    if k == 0:
                        ins = dve.tensor_scalar(ACC[:, c, :], w, x, None, ALU.mult)
                    else:
                        dve.wait_ge(s_part, n * 16 + (2 * k + c - 1))
                        ins = dve.scalar_tensor_tensor(out=ACC[:, c, :], in0=w, scalar=x, in1=ACC[:, c, :],
                                                       op0=ALU.mult, op1=ALU.add)
                    ins.then_inc(s_part, 1)

        def early_parts(dve, g):
            st, acc = steps["dve"], DACC[g - MG_PE]
            dve.wait_ge(s_early[g % EARLY_BUFS], 16 * (g // EARLY_BUFS + 1))
            for k in range(KD):
                for c in range(2):
                    w, x = EARLY[g % EARLY_BUFS][:, k, :], CS[:, c, k:k + 1]
                    if k == 0:
                        st.add(dve.tensor_scalar(acc[:, c, :], w, x, None, ALU.mult))
                        continue
                    dve.wait_ge(s_dve, st.n - 1)
                    ins = dve.scalar_tensor_tensor(out=acc[:, c, :], in0=w, scalar=x, in1=acc[:, c, :],
                                                   op0=ALU.mult, op1=ALU.add)
                    if k < KD - 1 or c == 0:
                        st.add(ins)
            ins.then_inc(s_dparts, 1)

        def sum_parts(pe, acc, dst):
            for s in range(2):
                for c in range(2):
                    mm = pe.matmul(dst[:, 2 * s + c:2 * s + c + 1], acc[:, c, s * P:(s + 1) * P], ONES[:, 0:1],
                                   start=True, stop=True)
            return mm

        def mod_next(pe, g, dst):
            pe.wait_ge(s_mw, g * 16 + 16 * (1 - MG_DIRECT))
            mod_direct(pe, MW, dst).then_inc(s_modu, 1)

        def mod_group(pe, g, parts=False):
            pe.wait_ge(s_mod, g)
            if parts:
                pe.wait_ge(s_part, g * 16 + 16 * (1 - MOD_TILES // 2))
                sum_parts(pe, ACC, MODPS).then_inc(s_modu, 1)
            else:
                mod_next(pe, g, MODPS)

        def mod_add(dve, src, g, n):
            return dve.tensor_tensor(MOD[:, ds(2 * g, 2 * n), :], src.rearrange("p (a b) -> p a b", a=2 * n),
                                     BMOD[:, ds(2 * g, 2 * n)].unsqueeze(2).to_broadcast([P, 2 * n, 2]), ALU.add)

        def mod_read(dve, g):
            dve.wait_ge(s_modu, g - MG_DIRECT + 1)
            mod_add(dve, MODPS, g, 1).then_inc(s_mod, 1)

        def project(pe, n, p, kt=KD, moving=(HNH, HNL), normed=None):
            pe.wait_ge(s_lo, n.index + 2)
            pe.wait_ge(s_free[p.slot], p.before)
            for k in range(kt):
                if normed is not None:
                    pe.wait_ge(s_hnl, normed + k + 1)
                last = product(pe, n, p, k, kt, moving)
            last.then_inc(s_used, 1)

        def project_two(pe, n, p, normed):
            for j in range(2):
                pe.wait_ge(s_lo, n + j + 2)
                pe.wait_ge(s_free[Turn(p, j).slot], Turn(p, j).before)
            for k in range(KD):
                pe.wait_ge(s_hnl, normed + k + 1)
                for j in range(2):
                    last = product(pe, Turn(n, j), Turn(p, j), k, KD, (HNH, HNL))
                    if k == KD - 1:
                        last.then_inc(s_used, 1)

        def product(pe, n, p, k, kt, moving):
            h, l = moving
            for w, x in ((WH, h), (WH, l), (WL, h)):
                for half in range(2):
                    last = pe.matmul(PS[p.slot][:, half, 0:HALF], w[n.slot][:, k, :],
                                     x[:, k, half * HALF:(half + 1) * HALF],
                                     start=(k == 0 and w is WH and x is h),
                                     stop=(k == kt - 1 and w is WL))
            return last
        def newton(dve, st, v, y, tmp):
            st.done(dve.tensor_tensor(tmp, y, y, ALU.mult))
            st.done(dve.tensor_tensor(tmp, tmp, v, ALU.mult))
            st.done(dve.tensor_scalar(tmp, tmp, -0.5, 1.5, ALU.mult, ALU.add))
            st.done(dve.tensor_tensor(y, y, tmp, ALU.mult))

        def norm_pe(pe, q, p):
            pe.wait_ge(s_free[p.slot], p.before)
            pe.wait_ge(s_add, KD * (q + 1))
            for half in range(2):
                mm = pe.matmul(PS[p.slot][:, half, 0:HALF], ONES[:, :], NR[:, half * HALF:(half + 1) * HALF],
                               start=True, stop=True)
            mm.then_inc(s_squ, 1)

        def square(act, q, k, p, j):
            if q or k >= 2:
                act.wait_ge(s_add, k + (KD * q - 1))
            ring_done(act, p)
            act.activation(TMP[:, j, :], X[:, k, :], ACT.Square).then_inc(s_sq, 1)

        def clear_sum(dve):
            st = steps["dve"]
            st.done(dve.memset(NR[:, :], 0.0))

        def add_square(dve, q, k, j):
            dve.wait_ge(s_sq, k + (KD * q + 1))
            if q or k:
                dve.wait_ge(s_add, k + KD * q)
            dve.tensor_tensor(NR[:, :], NR[:, :], TMP[:, j, :], ALU.add).then_inc(s_add, 1)

        def norm_act(act, q, p):
            act.preload_act_table(ACT.Ln)
            act.wait_ge(s_squ, q + 1)
            act.activation(pair(NR), ring(p), ACT.Ln, bias=EPSC[:, 0:1], scale=1.0 / D).then_inc(s_ln, 1)
            act.wait_ge(s_ln, q + 1)
            act.activation(NR[:, :], NR[:, :], ACT.Exp, scale=-0.5).then_inc(s_r0, 1)

        def norm_high(act, q, shift):
            for k in range(KD):
                act.wait_ge(s_hf, KD * q + k + 1)
                src = NORM_BUF[k % 4]
                act.activation(HNH[:, k, 0:TP], src[:, 0:TP], ACT.Identity, bias=MOD[:, shift + k, 0:1])
                act.activation(HNH[:, k, TP:T], src[:, TP:T], ACT.Identity,
                               bias=MOD[:, shift + k, 1:2]).then_inc(s_hnh, 1)

        def norm_dve(dve, q, p, shift, scale, gain, rstd=True):
            st = steps["dve"]
            st.done(dve.scalar_tensor_tensor(out=GAIN[:, :, :], in0=MOD[:, scale:scale + KD, :], scalar=1.0,
                                             in1=gain.unsqueeze(2).to_broadcast([P, KD, 2]),
                                             op0=ALU.add, op1=ALU.mult))
            if rstd:
                norm_rstd(dve, q, p)
            for k in range(KD):
                if KD * q + k >= 4:
                    dve.wait_ge(s_hnh, KD * q + k - 3)
                    dve.wait_ge(s_hnl, KD * q + k - 3)
                dst = NORM_BUF[k % 4]
                st.add(dve.scalar_tensor_tensor(out=dst[:, 0:TP], in0=X[:, k, 0:TP], scalar=GAIN[:, k, 0:1],
                                                in1=NR[:, 0:TP], op0=ALU.mult, op1=ALU.mult))
                dve.scalar_tensor_tensor(out=dst[:, TP:T], in0=X[:, k, TP:T], scalar=GAIN[:, k, 1:2],
                                         in1=NR[:, TP:T], op0=ALU.mult, op1=ALU.mult).then_inc(s_hf, 1)
                if k:
                    low_of_norm(dve, q, k - 1, shift)
            low_of_norm(dve, q, KD - 1, shift)

        def norm_rstd(dve, q, p):
            st = steps["dve"]
            dve.wait_ge(s_ln, q + 1)
            st.done(dve.tensor_scalar(pair(NV), ring(p), 1.0 / D, EPS, ALU.mult, ALU.add))
            dve.wait_ge(s_r0, q + 1)
            dve.tensor_tensor(NT[:, :], NR[:, :], NR[:, :], ALU.mult).then_inc(s_free[p.slot], 1)
            ring_done(dve, p)
            st.done(dve.tensor_tensor(NT[:, :], NT[:, :], NV[:, :], ALU.mult))
            st.done(dve.tensor_scalar(NT[:, :], NT[:, :], -0.5, 1.5, ALU.mult, ALU.add))
            st.done(dve.tensor_tensor(NR[:, :], NR[:, :], NT[:, :], ALU.mult))

        def low_of_norm(dve, q, k, shift):
            dve.wait_ge(s_hf, KD * q + k + 1)
            dve.wait_ge(s_hnh, KD * q + k + 1)
            src = NORM_BUF[k % 4]
            for a, b, g in ((0, TP, 0), (TP, T, 1)):
                ins = dve.scalar_tensor_tensor(out=HNL[:, k, a:b], in0=src[:, a:b],
                                               scalar=MOD[:, shift + k, g:g + 1],
                                               in1=HNH[:, k, a:b].bitcast(F32), op0=ALU.add, op1=ALU.subtract)
            ins.then_inc(s_hnl, 1)

        def residual_dve(dve, n, p, gate, m):
            dve.wait_ge(s_used, n.index + 1)
            for lo, hi, half, g in ((0, HALF, 0, 0), (HALF, TP, 1, 0), (TP, T, 1, 1)):
                a = lo - half * HALF
                ins = dve.scalar_tensor_tensor(
                    out=X[:, m, lo:hi],
                    in0=PS[p.slot][:, half, a:a + hi - lo],
                    scalar=MOD[:, gate + m, g:g + 1],
                    in1=X[:, m, lo:hi],
                    op0=ALU.mult, op1=ALU.add)
                if hi == T:
                    ins.then_inc(s_free[p.slot], 1)

        def row_loads():
            yield ROWS[0:MOD_ROWS, 0, :], t["b_mod"].rearrange("l (m p) -> (l m) p", p=P)
            for name in ("norm_mix_g", "norm_ffn_g", "lru_lambda", "ret_gn_g", "lru_conv_b", "c_prompt", "c_sample"):
                n = t[name].shape[0] * t[name].shape[1] // P
                yield ROWS[R1[name]:R1[name] + n, 1, :], t[name].rearrange("a (k p) -> (a k) p", p=P)
            yield (ROWS[R1["final_norm_g"]:R1["final_norm_g"] + KD, 1, :],
                   t["final_norm_g"].rearrange("(k p) -> k p", p=P))
            yield (ROWS[R1["lru_conv_w"]:R1["lru_conv_w"] + 16, 1, :],
                   t["lru_conv_w"][0].rearrange("t (k p) -> (t k) p", p=P))
            yield (ROWS[R1["state_lru_conv"]:R1["state_lru_conv"] + 12, 1, :],
                   t["state_lru_conv"][0, 0].rearrange("t (k p) -> (t k) p", p=P))
            yield (ROWS[R1["state_lru_h"]:R1["state_lru_h"] + 4, 1, :],
                   t["state_lru_h"][0].rearrange("a (k p) -> (a k) p", p=P))
            for part in range(2):
                r = R1["lru_gate_b"] + 4 * part
                yield (ROWS[r:r + 4, 1, :].rearrange("r (two j) -> r two j", two=2),
                       t["lru_gate_b"][0].rearrange("(r two) j -> r two j", two=2)[:, :, 64 * part:64 * part + 64])
            for name in ("gla_b_gate", "gla_gn_g", "mlstm_conv_b", "mlstm_gn_g"):
                n = t[name].shape[1] // P
                yield ROWS[R2[name]:R2[name] + n, 2, :], t[name].rearrange("a (k p) -> (a k) p", p=P)
            yield (ROWS[R2["mlstm_conv_w"]:R2["mlstm_conv_w"] + 16, 2, :],
                   t["mlstm_conv_w"][0].rearrange("t (k p) -> (t k) p", p=P))
            yield (ROWS[R2["state_mlstm_conv"]:R2["state_mlstm_conv"] + 12, 2, :],
                   t["state_mlstm_conv"][0, 0].rearrange("t (k p) -> (t k) p", p=P))
            yield ROWS[R2["state_mlstm_n"]:R2["state_mlstm_n"] + 4, 2, :], t["state_mlstm_n"][0, 0]

        def ffn_parts(w, p, g):
            a = 0
            for n in FFN_CUTS:
                yield a, n, w, p, g
                g += n + (2 if a == 0 else 0)
                a, w, p = a + n, w + 2 * n + KD, p + 2 * n + KD

        def out_loads(sp, w, src):
            with sp.Fori(0, KD // 2) as i:
                for j in range(2):
                    load_weight(sp, Turn(w, j, 2, i), src.rearrange("(k p) m -> p k m", p=P),
                                lambda: i * 2 * P + j * P)

        def ffn_loads(sp, l, w0):
            for a, n, w, _, _ in ffn_parts(w0, 0, 0):
                with sp.Fori(0, n) as i:
                    for j in range(2):
                        load_weight(sp, Turn(w, j, 2, i), t["w_ffn_in"][l].rearrange("(k p) m -> p k m", p=P),
                                    lambda: i * P + j * DFF + a * P)
                out_loads(sp, w + 2 * n, t["w_ffn_out"][l][a * P:(a + n) * P, :])

        def transpose_blocks(pe, src, dst, dst_s):
            for b in range(NB):
                pe.transpose(dst[:, b * P:(b + 1) * P], src[:, b * P:(b + 1) * P], IDENT)
            return pe.transpose(dst_s, src[:, TP:T], IDENT)

        def out_pe(pe, w, p, kt, group=None, step=2):
            with pe.Fori(0, KD // step) as i:
                for j in range(step):
                    project(pe, Turn(w, j, step, i), Turn(p, j, step, i), kt, (GH, GL))
                if group is not None:
                    mod_group(pe, group + i, step == 4)

        def ffn_pe(pe, w0, p0, glo, group, q):
            for a, n, w, p, g in ffn_parts(w0, p0, group or 0):
                if a == 0:
                    project_two(pe, w, p, KD * q)
                else:
                    for j in range(2):
                        project(pe, Turn(w, j), Turn(p, j))
                with pe.Fori(1, n) as i:
                    project(pe, Turn(w, 0, 2, i), Turn(p, 0, 2, i))
                    if group is not None:
                        mod_group(pe, i + (g - 1), True)
                    project(pe, Turn(w, 1, 2, i), Turn(p, 1, 2, i))
                if group is not None:
                    mod_group(pe, g + n - 1, True)
                pe.wait_ge(s_glf, glo + a + n)
                more = a == 0 and group is not None
                out_pe(pe, w + 2 * n, p + 2 * n, n, g + n if more else None, 4 if more else 2)

        def head_mean(pe, src, ready, h):
            pe.wait_ge(ready, h + 1)
            pe.matmul(J[:, 0, :], MEAN[:, :], src[:, 0:TP], start=True, stop=True)
            pe.matmul(J[:, 1, 0:TS], MEAN[:, :], src[:, TP:T], start=True, stop=True).then_inc(s_mean, 1)

        def head_var(pe, src, ready, h):
            pe.wait_ge(ready, h + 1)
            pe.matmul(K[:, 0, :], MEAN[:, :], src[:, 0:TP], start=True, stop=True)
            pe.matmul(K[:, 1, 0:TS], MEAN[:, :], src[:, TP:T], start=True, stop=True).then_inc(s_var, 1)

        def out_act(act, w, p=0, q=None, last=False):
            n = KD // 2 - (1 if last else 0)

            def step(i, end):
                for j in range(2):
                    if not (end and j):
                        hi_of(act, Turn(w, j + 1, 2, i))
                    if q is not None:
                        square(act, q, 2 * i + j, Turn(p, j, 2, i), j)

            with act.Fori(0, n) as i:
                step(i, False)
            if last:
                step(n, True)

        def ffn_act(act, w0, p0, q, last=False):
            parts = list(ffn_parts(w0, p0, 0))
            for a, n, w, p, _ in parts:
                act.preload_act_table(ACT.Tanh)

                def step(i, first=False):
                    if not first:
                        hi_of(act, Turn(w, 1, 2, i))
                    act.wait_ge(s_used, Turn(w, 0, 2, i).index + 1)
                    act.activation(pair(TMP[:, 0, :]), ring(Turn(p, 0, 2, i)), ACT.Tanh, scale=0.5).then_inc(s_fth, 1)
                    hi_of(act, Turn(w, 2, 2, i))
                    ring_done(act, Turn(p, 1, 2, i))
                    act.activation(GH[:, i, :], TMP[:, 1, :], ACT.Copy).then_inc(s_gah, 1)

                if a == 0:
                    step(0, True)
                with act.Fori(1 if a == 0 else 0, n) as i:
                    step(i)
                end = a == parts[-1][0]
                out_act(act, w + 2 * n, p + 2 * n, q if end else None, last and end)

        def fill_padded(act, st, dst, p):
            st.add(act.activation(dst[:, PAD:PAD + HALF], PS[p.slot][:, 0, 0:HALF], ACT.Copy))
            st.add(act.activation(dst[:, PAD + HALF:PAD + TP], PS[p.slot][:, 1, 0:TP - HALF], ACT.Copy))
            act.activation(dst[:, SC + PAD:SC + PAD + TS], PS[p.slot][:, 1, TP - HALF:HALF],
                           ACT.Copy).then_inc(s_free[p.slot], 1)
            ring_done(act, p)

        def conv_columns(act, st, src, l, h):
            for o, a in ((8, TP), (20, SC + TS)):
                st.add(act.activation(OV[:, l, o:o + 12].rearrange("p (t k) -> p t k", k=4)[:, :, h],
                                      src[:, a:a + PAD], ACT.Copy))

        def copy_head(act, st, ready, h, count):
            act.wait_ge(ready, count)
            act.wait_ge(s_oc, h)
            st.add(act.activation(OT[:, 0:TP], K[:, 0, :], ACT.Copy))
            act.activation(OT[:, TP:T], K[:, 1, P:P + TS], ACT.Copy).then_inc(s_o, 1)

        def head_rstd(act, st, h):
            act.wait_ge(s_var, h + 1)
            st.add(act.activation(NR[:, 0:TP], K[:, 0, :], ACT.Ln, bias=EPSC[:, 0:1]))
            act.activation(NR[:, TP:T], K[:, 1, 0:TS], ACT.Ln, bias=EPSC[:, 0:1]).then_inc(s_hln, 1)
            act.wait_ge(s_hln, h + 1)
            act.activation(NR[:, :], NR[:, :], ACT.Exp, scale=-0.5).then_inc(s_hr0, 1)

        def gate_dve(dve, n, p, h):
            dve.wait_ge(s_thg, h + 1)
            dve.scalar_tensor_tensor(out=pair(SG), in0=pair(THG), scalar=1.0, in1=ring(p), op0=ALU.add,
                                     op1=ALU.mult).then_inc(s_free[p.slot], 1)

        def center(dve, st, h):
            dve.wait_ge(s_mean, h + 1)
            dve.wait_ge(s_osq, h)
            st.add(dve.tensor_tensor(OC[:, 0:TP], OT[:, 0:TP], J[:, 0, :], ALU.subtract))
            dve.tensor_tensor(OC[:, TP:T], OT[:, TP:T], J[:, 1, 0:TS], ALU.subtract).then_inc(s_oc, 1)

        def low_tile(pool, i, before):
            pool.wait_ge(s_gah, before + 1)
            pool.sem_inc(s_half, 1)
            pool.tensor_tensor(GL[:, i, :], TMP[:, 1, :], GH[:, i, :].bitcast(F32), ALU.subtract).then_inc(s_glf, 1)

        def load_next(pool, n, half):
            pool.wait_ge(s_part, n * 16 + 8 * (half + 1))
            pool.sem_inc(s_half, 1)
            load_half(pool, lambda: n + 1, half)

        def ffn_pool(pool, gah, mods):
            parts = list(ffn_parts(0, 0, 0))
            for a, n, _, _, g in parts:
                end = mods and a == parts[-1][0]
                with pool.Fori(0, n - 1 if end else n) as i:
                    if mods:
                        load_next(pool, i + g, 0)
                    low_tile(pool, i, i + gah + a)
                    if mods:
                        load_next(pool, i + g, 1)
                if mods and a == 0:
                    with pool.Fori(0, 2) as i:
                        for half in range(2):
                            load_next(pool, i + g + n, half)
                if end:
                    low_tile(pool, n - 1, gah + a + n - 1)

        def finish_head(dve, st, h, gain):
            dve.wait_ge(s_hln, h + 1)
            st.add(dve.tensor_scalar(NV[:, 0:TP], K[:, 0, :], EPS, None, ALU.add))
            st.done(dve.tensor_scalar(NV[:, TP:T], K[:, 1, 0:TS], EPS, None, ALU.add))
            finish_rstd(dve, st, h, gain)

        def finish_rstd(dve, st, h, gain):
            dve.wait_ge(s_hr0, h + 1)
            newton(dve, st, NV[:, :], NR[:, :], NT[:, :])
            st.done(dve.tensor_tensor(NT[:, :], OC, NR[:, :], ALU.mult))
            dve.scalar_tensor_tensor(out=OB, in0=NT[:, :], scalar=gain, in1=SG, op0=ALU.mult,
                                     op1=ALU.mult).then_inc(s_ob, 1)
            dve.wait_ge(s_ob, h + 1)

        def convolve(dve, st, src, dst, w, b, h, ready, free):
            dve.wait_ge(*free)
            st.done(dve.tensor_scalar(dst, src[:, PAD:PAD + TC], w[:, PAD, ds(h, 1)], b[:, ds(h, 1)],
                                      ALU.mult, ALU.add))
            for tap in (2, 1, 0):
                ins = dve.scalar_tensor_tensor(out=dst, in0=src[:, tap:tap + TC], scalar=w[:, tap, ds(h, 1)],
                                               in1=dst, op0=ALU.mult, op1=ALU.add)
                if tap:
                    st.done(ins)
            ins.then_inc(ready, 1)

        def out_dve(dve, w, p, gate, q=None, group=None, size=2, last=False):
            n = KD // size - (1 if last else 0)
            if q is not None:
                clear_sum(dve)

            def step(i, end):
                for j in range(size):
                    if not (end and j == size - 1):
                        lo_of(dve, Turn(w, j + 1, size, i))
                    residual_dve(dve, Turn(w, j, size, i), Turn(p, j, size, i), gate, i * size + j)
                    if q is not None:
                        add_square(dve, q, i * size + j, j % 2)
                    if size == 4:
                        mod_parts(dve, group + i, j)
                if group is not None:
                    mod_read(dve, group + i)

            with dve.Fori(0, n) as i:
                step(i, False)
            if last:
                step(n, True)

        def ffn_dve(dve, w0, p0, done, gate, q, group, last=False):
            mods = group is not None
            parts = list(ffn_parts(w0, p0, group or 0))
            for a, n, w, p, g in parts:
                def step(i, first=False):
                    gi, ui = Turn(p, 0, 2, i), Turn(p, 1, 2, i)
                    if a or not first:
                        lo_of(dve, Turn(w, 1, 2, i))
                    if mods and not first:
                        mod_parts(dve, i + (g - 1), 3)
                    dve.wait_ge(s_fth, i + done + a + 1)
                    dve.scalar_tensor_tensor(out=pair(NV), in0=pair(TMP[:, 0, :]), scalar=1.0, in1=ring(gi),
                                             op0=ALU.add, op1=ALU.mult).then_inc(s_free[gi.slot], 1)
                    if mods and not first:
                        mod_read(dve, i + (g - 1))
                    if mods:
                        mod_parts(dve, i + g, 0)
                    lo_of(dve, Turn(w, 2, 2, i))
                    if mods:
                        mod_parts(dve, i + g, 1)
                    ring_done(dve, gi)
                    dve.wait_ge(s_glf, i + done + a)
                    dve.wait_ge(s_used, Turn(w, 1, 2, i).index + 1)
                    dve.scalar_tensor_tensor(out=pair(TMP[:, 1, :]), in0=pair(NV), scalar=0.5, in1=ring(ui),
                                             op0=ALU.mult, op1=ALU.mult).then_inc(s_free[ui.slot], 1)
                    if mods:
                        mod_parts(dve, i + g, 2)

                step(0, True)
                with dve.Fori(1, n) as i:
                    step(i)
                if mods:
                    mod_parts(dve, g + n - 1, 3)
                    mod_read(dve, g + n - 1)
                end = a == parts[-1][0]
                more = a == 0 and group is not None
                out_dve(dve, w + 2 * n, p + 2 * n, gate, q if end else None, g + n if more else None,
                        4 if more else 2, last and end)

        CW = t["c_w_in"][0].rearrange("(k p) m -> p k m", p=P)
        C_GQ, C_GK, C_GV, C_GLR, C_GR, C_U, C_O, C_I, C_F = 0, 256, 512, 1024, 1040, 1552, 2064, 2576, 2580

        def pair_items(i):
            return [lambda: i * P + C_GK, lambda: i * P + C_GQ, lambda: i * 2 * P + C_GV, lambda: i * 2 * P + C_GR,
                    lambda: i * 2 * P + C_GV + P, lambda: i * 2 * P + C_GR + P]

        def layer1_sync(sp):
            sp.wait_ge(s_lo, W_SM)
            raw = RAW[Turn(W_SM).slot]
            sp.dma_start(raw[:, :, 32:32 + HEADS], CW[:, :, C_I:C_I + HEADS], allow_slow_non_contiguous=True).then_inc(s_smw, 16)
            sp.dma_start(raw[:, :, 64:64 + HEADS], CW[:, :, C_F:C_F + HEADS], allow_slow_non_contiguous=True).then_inc(s_smw, 16)
            sp.dma_start(raw[:, :, 0:16], CW[:, :, C_GLR:C_GLR + 16], allow_slow_non_contiguous=True).then_inc(s_raw[Turn(W_SM).slot], 16)
            sp.wait_ge(s_sout, 32 * HEADS)
            with sp.Fori(0, 2) as i:
                for j, a in enumerate(pair_items(i)):
                    load_weight(sp, Turn(W_GLA, j, 6, i), CW, a)
                    if j == 1:
                        sp.wait_ge(s_gtok, 1)
                        sp.wait_ge(s_cum, 2)
                        sp.wait_ge(s_got, 2 * i)
                        sp.dma_start(SG0, t["state_gla"][0, 0, ds(2 * i, 2)].rearrange("h d e -> (h d) e")
                                     ).then_inc(s_gs0, 16)
            with sp.Fori(0, HEADS) as h:
                load_weight(sp, Turn(W_ML, 0, 2, h), CW, lambda: h * P + C_U)
                sp.wait_ge(s_gsout, 64)
                sp.wait_ge(s_got, HEADS)
                sp.wait_ge(s_nd, h)
                sp.dma_start(WQK, t["mlstm_w_qk"][0, h]).then_inc(s_mw2, 16)
                sp.dma_start(WV, t["mlstm_w_v"][0, h]).then_inc(s_mw2, 16)
                sp.dma_start(SEL[0:HEADS, :], t["selectors"][h]).then_inc(s_mw2, 16)
                sp.dma_start(CN0[:, 0:P], t["state_mlstm_C"][0, 0, h]).then_inc(s_c0, 16)
                load_weight(sp, Turn(W_ML, 1, 2, h), CW, lambda: h * P + C_O)
            sp.wait_ge(s_rg, 1)
            sp.dma_start(out["m_p"][0].rearrange("a h -> h a"), RM[0:HEADS, TP - 1:TP],
                         allow_slow_non_contiguous=True).then_inc(s_out, 16)
            sp.dma_start(out["m_s"][0].rearrange("a h -> h a"), RM[0:HEADS, T - 1:T],
                         allow_slow_non_contiguous=True).then_inc(s_out, 16)
            out_loads(sp, W_OUT1, t["c_w_out"][0])
            ffn_loads(sp, 1, W_FFN1)
            sp.wait_ge(s_ov, 1)
            n = 2
            for l, (first, second) in enumerate((("lru_h", "lru_conv"), ("n", "conv"))):
                for g, group in enumerate(("_p", "_s")):
                    dst = out[first + group]
                    dst = dst[0, 0] if l else dst[0].rearrange("a (k p) -> (a k) p", p=P)
                    sp.dma_start(dst, OVR[4 * g:4 * g + 4, l, :]).then_inc(s_out, 16)
                    sp.dma_start(out[second + group][0, 0].rearrange("t (k p) -> (t k) p", p=P),
                                 OVR[8 + 12 * g:20 + 12 * g, l, :]).then_inc(s_out, 16)
                    n += 2
            for b in range(NB + 1):
                sp.wait_ge(s_yr, b + 1)
                dst = out["y_p"][0, b * P:(b + 1) * P, :] if b < NB else out["y_s"][0]
                sp.dma_start(dst, YR[b % 2][0:P if b < NB else TS, :]).then_inc(s_yout[b % 2], 16)
            sp.wait_ge(s_out, 16 * n)
            sp.wait_ge(s_yout[0], 16 * (NB // 2 + 1))
            sp.wait_ge(s_yout[1], 16 * (NB // 2))
            sp.wait_ge(s_cout, 32 * HEADS)
            sp.wait_ge(s_small, 32)

        def layer1_pool(pool):
            pool.wait_ge(s_glo, KD)
            pool.wait_ge(s_sout, 32 * HEADS)
            pool.memset(MASK64, 1.0).then_inc(s_area, 1)
            pool.memset(MASKR, 1.0).then_inc(s_area, 1)
            pool.wait_ge(s_area, 2)
            pool.memset(MASK64[:, 0:T:64], 0.0).then_inc(s_area, 1)
            pool.memset(MASKR[:, 0:T:P], 0.0).then_inc(s_area, 1)
            pool.dma_start(WGATE[0:16, :], t["gla_w_gate"][0]).then_inc(s_wg, 16)
            pool.wait_ge(s_cum, 2)
            pool.wait_ge(s_rg, 1)
            for a in (Q1[0], Q1[1], Q3[0], Q3[1], AG):
                pool.memset(a, 0.0).then_inc(s_area, 1)
            with pool.Fori(0, 2) as i:
                pool.wait_ge(s_gst, 2 * i + 2)
                for name, state in (("gla_p", SGF), ("gla_s", SGN)):
                    pool.dma_start(out[name][0, 0, ds(2 * i, 2)].rearrange("h d e -> (h d) e"),
                                   state).then_inc(s_gsout, 16)
            pool.wait_ge(s_ob, 2 * HEADS)
            pool.wait_ge(s_got, HEADS)
            pool.wait_ge(s_gsout, 64)
            for a in (UP[:, 0:PAD], UP[:, TC + PAD - 1:TC + PAD]):
                pool.memset(a, 0.0).then_inc(s_area, 1)
            pool.memset(VO[:, :, P:2 * P], 1.0).then_inc(s_area, 1)
            with pool.Fori(0, HEADS) as h:
                pool.wait_ge(s_cn, h + 1)
                pool.dma_start(out["C_p"][0, 0, h], CN[:, NB - 1, 0:P]).then_inc(s_cout, 16)
                pool.dma_start(out["C_s"][0, 0, h], CNS[:, 0:P]).then_inc(s_cout, 16)
            ffn_pool(pool, 2 * KD + DONE0, False)

        AREA_SMALL, AREA_GLA, AREA_ML = 4, 9, 12

        def small_pe(pe):
            project(pe, Turn(W_SM), Turn(R_SM), normed=2 * KD)
            pe.wait_ge(s_wg, 16)
            pe.wait_ge(s_rows1, 1)
            for i in range(2):
                p = Turn(R_G, i)
                pe.wait_ge(s_free[p.slot], p.before)
                for half in range(2):
                    mm = pe.matmul(PS[p.slot][:, half, 0:HALF], WGATE[0:16, i * P:(i + 1) * P],
                                   GLR[0:16, half * HALF:(half + 1) * HALF], start=True, stop=True)
                mm.then_inc(s_gp, 1)
            pe.wait_ge(s_rg, 1)
            for b in range(NB):
                pe.transpose(K[:, 0, 4 * b:4 * b + 4], RB[0:HEADS, b * P:(b + 1) * P], IDENT[0:HEADS, 0:HEADS])
            pe.transpose(K[0:TS, 0, 16:20], RB[0:HEADS, TP:T], IDENT[0:HEADS, 0:HEADS]).then_inc(s_gt, 1)

        def gla_head_pe(pe, i, j):
            n = 2 * i + j
            pe.wait_ge(s_q3, i + 1)
            for b in range(NB):
                pe.matmul(J[:, 0, b * P:(b + 1) * P], EK1[:, b * P:(b + 1) * P], Q1[j][:, b * P:(b + 1) * P],
                          start=True, stop=True)
            pe.matmul(J[0:TS, 1, 0:TS], EK1[:, TP:T], Q1[j][:, TP:T], start=True, stop=True).then_inc(s_gsc, 1)

        def gla_values_pe(pe, i, j, p):
            ring_done(pe, p)
            transpose_blocks(pe, VG, K[:, 0, :], K[0:TS, 1, 0:P]).then_inc(s_gvt, 1)

        def gla_out_pe(pe, i, j):
            n = 2 * i + j
            pe.wait_ge(s_gvtok, n + 1)
            pe.wait_ge(s_gatt, n + 1)
            for c in range(2 * NB):
                r = slice(64 * (c % 2), 64 * (c % 2) + 64)
                dst = (K, J)[c % 2][:, 0, (c // 2) * P:(c // 2 + 1) * P]
                pe.matmul(dst, K4T[r, c // 2, :], VTG[r, c // 2, :], start=True, stop=True)
            pe.matmul(K[:, 1, 0:P], K4T[0:TS, NB, :], VTG[0:TS, NB, :], start=True, stop=True).then_inc(s_gkv, 1)
            pe.wait_ge(s_gst, n + 1)
            pe.wait_ge(s_gs0, 16 * i + 16)
            for c in range(2 * NB):
                cols = slice(64 * c, 64 * c + 64)
                pe.matmul(K[:, 0, cols], VTG[:, c // 2, :], AG[:, c // 2, 64 * (c % 2):64 * (c % 2) + 64],
                          start=True, stop=(c == 0))
                if c:
                    pe.matmul(K[:, 0, cols], SG8[:, c - 1, :], Q3[j][:, cols], start=False, stop=True)
            pe.matmul(K[:, 1, P:P + TS], VTG[0:TS, NB, :], AG[0:TS, NB, 0:TS], start=True, stop=False)
            pe.matmul(K[:, 1, P:P + TS], SG0, Q3[j][:, TP:T], start=False, stop=True).then_inc(s_got, 1)

        def gla_pe(pe):
            pe.wait_ge(s_gtok, 1)
            with pe.Fori(0, 2) as i:
                def item(j):
                    project(pe, Turn(W_GLA, j, 6, i), Turn(R_GLA, j, 6, i))

                item(0)
                item(1)
                item(2)
                pe.wait_ge(s_k4, i + 1)
                pe.wait_ge(s_ob, 2 * i + HEADS)
                transpose_blocks(pe, EK4, K[:, 0, :], K[0:TS, 1, 0:P]).then_inc(s_k4t, 1)
                pe.wait_ge(s_oc, 2 * i + HEADS)
                gla_head_pe(pe, i, 0)
                item(3)
                pe.wait_ge(s_k4tok, i + 1)
                gla_values_pe(pe, i, 0, Turn(R_GLA, 2, 6, i))
                item(4)
                gla_out_pe(pe, i, 0)
                item(5)
                head_mean(pe, OT, s_o, 2 * i + HEADS)
                head_var(pe, OSQ, s_osq, 2 * i + HEADS)
                gla_head_pe(pe, i, 1)
                pe.wait_ge(s_ob, 2 * i + HEADS + 1)
                gla_values_pe(pe, i, 1, Turn(R_GLA, 4, 6, i))
                gla_out_pe(pe, i, 1)
                head_mean(pe, OT, s_o, 2 * i + HEADS + 1)
                head_var(pe, OSQ, s_osq, 2 * i + HEADS + 1)

        def mlstm_pe(pe):
            with pe.Fori(0, HEADS) as h:
                def r(j):
                    return Turn(R_ML, j, 4, h)

                def spread(row, dst):
                    pe.matmul(dst[:, 0, :], SEL[0:HEADS, :], row[0:HEADS, 0:TP], start=True, stop=True)
                    return pe.matmul(dst[:, 1, 0:TS], SEL[0:HEADS, :], row[0:HEADS, TP:T], start=True, stop=True)

                project(pe, Turn(W_ML, 0, 2, h), r(0))
                pe.wait_ge(s_mw2, 48 * h + 48)
                pe.wait_ge(s_rexp, 2)
                pe.wait_ge(s_ob, h + 2 * HEADS)
                spread(RA, K).then_inc(s_ba, 1)
                project(pe, Turn(W_ML, 1, 2, h), r(1))
                ring_done(pe, r(0))
                pe.wait_ge(s_oc, h + 2 * HEADS)
                for b in range(NB + 1):
                    n, a = (P, PAD + b * P) if b < NB else (TS, SC + PAD)
                    mm = pe.matmul(J[:, 0, b * P:(b + 1) * P] if b < NB else J[0:TS, 1, 0:P],
                                   UP[:, a:a + n], WV, start=True, stop=True)
                mm.then_inc(s_mv, 1)
                pe.wait_ge(s_ucs, h + 1)
                for part, s_q in ((0, s_mq), (1, s_mk)):
                    p = r(2 + part)
                    pe.wait_ge(s_free[p.slot], p.before)
                    pe.matmul(PS[p.slot][:, 0, :], WQK[:, part * P:(part + 1) * P], UC[:, 0:TP], start=True, stop=True)
                    pe.matmul(PS[p.slot][:, 1, 0:TS], WQK[:, part * P:(part + 1) * P], UC[:, SC:SC + TS],
                              start=True, stop=True).then_inc(s_q, 1)
                pe.wait_ge(s_vo, h + 1)
                spread(RI, J).then_inc(s_bw, 1)
                pe.wait_ge(s_qm, h + 1)
                pe.wait_ge(s_km, h + 1)
                pe.wait_ge(s_ex, h + 1)
                for b in range(NB):
                    pe.matmul(K[:, 0, b * P:(b + 1) * P], KM[:, b * P:(b + 1) * P], QM[:, b * P:(b + 1) * P],
                              start=True, stop=True)
                pe.matmul(K[0:TS, 1, 0:TS], KM[:, TP:T], QM[:, TP:T], start=True, stop=True).then_inc(s_msc, 1)
                pe.wait_ge(s_wb, h + 1)
                for b in range(NB + 1):
                    n, a = (P, b * P) if b < NB else (TS, SC)
                    mm = pe.matmul(J[:, 0, b * P:(b + 1) * P] if b < NB else J[0:TS, 1, 0:P],
                                   UC[:, a:a + n], WQK[:, P:2 * P], start=True, stop=True)
                mm.then_inc(s_mkt, 1)
                pe.wait_ge(s_am, h + 1)
                spread(RF, K).then_inc(s_be, 1)
                pe.wait_ge(s_kw, h + 1)
                pe.wait_ge(s_enb, h + 1)
                for b in range(NB):
                    pe.matmul(K[:, b // 2, (b % 2) * 256:(b % 2) * 256 + 256], KW[:, b, :], VO[:, b, :],
                              start=True, stop=True)
                pe.matmul(J[:, 1, 0:256], KW[0:TS, NB, :], VO[0:TS, NB, :], start=True, stop=True).then_inc(s_cu, 1)
                pe.wait_ge(s_cn, h + 1)
                pe.wait_ge(s_qi, h + 1)
                for b in range(NB):
                    cols = slice(b * P, (b + 1) * P)
                    for part, dst in ((0, K), (1, J)):
                        c = slice(part * P, (part + 1) * P)
                        pe.matmul(dst[:, 0, cols], VO[:, b, c], AM[:, b, :], start=True, stop=(b == 0))
                        if b:
                            pe.matmul(dst[:, 0, cols], CN[:, b - 1, c], QI[:, cols], start=False, stop=True)
                for part, dst in ((0, K[:, 1, P:P + TS]), (1, J[:, 1, 0:TS])):
                    c = slice(part * P, (part + 1) * P)
                    pe.matmul(dst, VO[0:TS, NB, c], AM[0:TS, NB, 0:TS], start=True, stop=False)
                    mm = pe.matmul(dst, CN0[:, c], QI[:, TP:T], start=False, stop=True)
                mm.then_inc(s_nd, 1)
                pe.wait_ge(s_dabs, h + 1)
                head_mean(pe, OT, s_o, h + 2 * HEADS)
                head_var(pe, OSQ, s_osq, h + 2 * HEADS)

        def layer1_pe(pe):
            norm_pe(pe, 2, Turn(R_N2))
            small_pe(pe)
            gla_pe(pe)
            mlstm_pe(pe)
            pe.wait_ge(s_glo, 2 * KD)
            out_pe(pe, W_OUT1, R_OUT1, KD)
            norm_pe(pe, 3, Turn(R_N3))
            ffn_pe(pe, W_FFN1, R_FFN1, DONE0, None, 3)
            norm_pe(pe, 4, Turn(R_N4))
            for l in range(DEPTH):
                pe.transpose(K[0:32, 0, l * P:(l + 1) * P], OV[:, l, :], IDENT).then_inc(s_ovt, 1)
            for b in range(NB + 1):
                n = P if b < NB else TS
                p = Turn(R_Y, b)
                pe.wait_ge(s_free[p.slot], p.before)
                pe.wait_ge(s_y, KD)
                for k in range(KD):
                    mm = pe.transpose(PS[p.slot][0:n, k // 4, (k % 4) * P:(k % 4 + 1) * P],
                                      Y[:, k, b * P:b * P + n], IDENT)
                mm.then_inc(s_yt, 1)

        def small_act(act, st):
            hi_of(act, Turn(W_GLA))
            act.wait_ge(s_used, W_SM + 1)
            act.wait_ge(s_area, AREA_SMALL)
            small = ring(Turn(R_SM))
            st.add(act.activation(pair(GLR)[0:16], small[0:16], ACT.Copy))
            st.add(act.activation(pair(RI)[0:HEADS], small[32:36], ACT.Copy))
            act.activation(pair(RF)[0:HEADS], small[64:68], ACT.Copy).then_inc(s_free[Turn(R_SM).slot], 1)
            ring_done(act, Turn(R_SM))
            act.sem_inc(s_rows1, 1)
            act.wait_ge(s_rabs, 1)
            act.preload_act_table_set("natural_log_exp_and_others")
            st.done(act.activation(RA[0:HEADS], RF[0:HEADS], ACT.Abs))
            st.done(act.activation(RA[0:HEADS], RA[0:HEADS], ACT.Exp, scale=-1.0))
            act.activation(RA[0:HEADS], RA[0:HEADS], ACT.Ln, bias=ONES[0:HEADS, 0:1]).then_inc(s_rln, 1)
            for i in range(2):
                act.wait_ge(s_gp, i + 1)
                act.wait_ge(s_cum, i)
                act.activation(pair(GA), ring(Turn(R_G, i)), ACT.Abs, bias=col2("gla_b_gate", i)).then_inc(s_gab, 1)
                act.wait_ge(s_gab, i + 1)
                st.done(act.activation(GA, GA, ACT.Exp, scale=-1.0))
                act.activation(GA, GA, ACT.Ln, bias=ONES[:, 0:1]).then_inc(s_gln, 1)
            act.wait_ge(s_rwin, 1)
            act.activation(RI[0:HEADS], RI[0:HEADS], ACT.Exp).then_inc(s_rexp, 1)
            act.activation(RF[0:HEADS], RM[0:HEADS], ACT.Exp, scale=-1.0).then_inc(s_rexp, 1)
            act.wait_ge(s_gt, 1)
            st.add(act.activation(GTOK[:, 0:NB, :], K[:, 0, 0:16].rearrange("p (b h) -> p b h", b=NB), ACT.Copy))
            act.activation(GTOK[0:TS, NB, :], K[0:TS, 0, 16:20], ACT.Copy).then_inc(s_gtok, 1)

        def mixed_high(act, n, dst):
            act.wait_ge(s_ob, n + 1)
            act.activation(GH[:, dst, :], OB, ACT.Copy).then_inc(s_gah, 1)

        def gla_act(act, st):
            act.wait_ge(s_area, AREA_GLA)
            with act.Fori(0, 2) as i:
                st.loop(i, ACT_PAIR)

                def w(j):
                    return Turn(W_GLA, j, 6, i)

                def r(j):
                    return Turn(R_GLA, j, 6, i)

                act.wait_ge(s_cr, i + 1)
                act.wait_ge(s_gsc, 2 * i)
                act.wait_ge(s_k4t, i)
                st.add(act.activation(EK1, CR, ACT.Exp, scale=-1.0 / GLA_TAU))
                st.add(act.activation(EK4, LC, ACT.Exp, scale=1.0 / GLA_TAU))
                st.add(act.activation(EQ1, CR, ACT.Exp, scale=1.0 / GLA_TAU))
                st.add(act.activation(EL[:, 0:8], CUM[:, i, 63:TP:64], ACT.Exp, scale=1.0 / GLA_TAU))
                st.add(act.activation(EL[:, 8:9], CUM[:, i, T - 1:T], ACT.Exp, scale=1.0 / GLA_TAU))
                act.activation(EQ3, CUM[:, i, :], ACT.Exp, scale=1.0 / GLA_TAU).then_inc(s_ef, 1)
                hi_of(act, w(1))
                hi_of(act, w(2))
                hi_of(act, w(3))
                act.wait_ge(s_k4t, i + 1)
                act.wait_ge(s_gkv, 2 * i)
                st.add(act.activation(K4T[:, 0:NB, :], K[:, 0, :].rearrange("p (b c) -> p b c", b=NB), ACT.Copy))
                act.activation(K4T[0:TS, NB, :], K[0:TS, 1, 0:P], ACT.Copy).then_inc(s_k4tok, 1)
                for j in range(2):
                    n = 2 * i + j
                    v, g = r(2 + 2 * j), r(3 + 2 * j)
                    act.wait_ge(s_used, w(2 + 2 * j).index + 1)
                    act.wait_ge(s_gvt, n)
                    act.activation(pair(VG), ring(v), ACT.Copy).then_inc(s_free[v.slot], 1)
                    hi_of(act, w(6 if j else 4))
                    gla_values_act(act, st, i, j)
                    gla_gate_act(act, w(3 + 2 * j), g, n)
                    if not j:
                        hi_of(act, w(5))
                    copy_head(act, st, s_got, n + HEADS, n + 1)
                    gla_square(act, n)
                    head_rstd(act, st, n + HEADS)
                    mixed_high(act, n + HEADS, n)
            st.end(2)

        def gla_square(act, n):
            act.wait_ge(s_oc, n + HEADS + 1)
            act.activation(OSQ, OC, ACT.Square).then_inc(s_osq, 1)

        def gla_values_act(act, st, i, j):
            n = 2 * i + j
            act.wait_ge(s_gvt, n + 1)
            act.wait_ge(s_got, n)
            st.add(act.activation(VTG[:, 0:NB, :], K[:, 0, :].rearrange("p (b c) -> p b c", b=NB), ACT.Copy))
            act.activation(VTG[0:TS, NB, :], K[0:TS, 1, 0:P], ACT.Copy).then_inc(s_gvtok, 1)

        def gla_gate_act(act, w, g, n):
            act.wait_ge(s_used, w.index + 1)
            act.wait_ge(s_ob, n + HEADS)
            act.activation(pair(THG), ring(g), ACT.Tanh, scale=0.5).then_inc(s_thg, 1)

        def mlstm_act(act, st):
            act.wait_ge(s_area, AREA_ML)
            with act.Fori(0, HEADS) as h:
                st.loop(h, ACT_ML)

                def w(j):
                    return Turn(W_ML, j, 2, h)

                def r(j):
                    return Turn(R_ML, j, 4, h)

                hi_of(act, w(1))
                act.wait_ge(s_used, w(0).index + 1)
                act.wait_ge(s_uc, h)
                act.wait_ge(s_mv, h)
                st.done(act.activation(UP[:, SC:SC + PAD], cols2("state_mlstm_conv", 12).rearrange(
                    "p (t k) -> p t k", k=4)[:, :, h], ACT.Copy))
                fill_padded(act, st, UP, r(0))
                conv_columns(act, st, UP, 1, h)
                act.wait_ge(s_ex, h + 1)
                act.wait_ge(s_am, h)
                act.wait_ge(s_kw, h)
                st.add(act.activation(EW[:, 0:NB, :], EW[:, 0:NB, :], ACT.Exp))
                act.activation(EW[0:TS, NB, 0:TS], EW[0:TS, NB, 0:TS], ACT.Exp).then_inc(s_ew, 1)
                hi_of(act, w(2))
                act.wait_ge(s_uc, h + 1)
                act.activation(UT, UC, ACT.Tanh, scale=0.5).then_inc(s_uct, 1)
                act.wait_ge(s_mv, h + 1)
                act.wait_ge(s_nd, h)
                st.add(act.activation(VO[:, 0:NB, 0:P], J[:, 0, :].rearrange("p (b c) -> p b c", b=NB), ACT.Copy))
                act.activation(VO[0:TS, NB, 0:P], J[0:TS, 1, 0:P], ACT.Copy).then_inc(s_vo, 1)
                act.wait_ge(s_used, w(1).index + 1)
                act.wait_ge(s_ob, h + 2 * HEADS)
                act.activation(pair(THG), ring(r(1)), ACT.Tanh, scale=0.5).then_inc(s_free[r(1).slot], 1)
                for part, s_q, dst, sc, ready in ((0, s_mq, QM, 0.5, s_qm), (1, s_mk, KM, 0.5 * RET_SCALE, s_km)):
                    p = r(2 + part)
                    act.wait_ge(s_q, h + 1)
                    act.wait_ge(s_msc, h)
                    st.add(act.activation(dst[:, 0:TP], PS[p.slot][:, 0, :], ACT.Copy, scale=sc))
                    act.activation(dst[:, TP:T], PS[p.slot][:, 1, 0:TS], ACT.Copy,
                                   scale=sc).then_inc(s_free[p.slot], 1)
                    ring_done(act, p)
                    act.sem_inc(ready, 1)
                act.wait_ge(s_bw, h + 1)
                act.wait_ge(s_cn, h)
                st.add(act.activation(WB[:, 0:TP], J[:, 0, :], ACT.Copy))
                act.activation(WB[:, TP:T], J[:, 1, 0:TS], ACT.Copy).then_inc(s_wb, 1)
                act.wait_ge(s_be, h + 1)
                act.wait_ge(s_dmax, h)
                st.add(act.activation(ENB[:, 0:TP], K[:, 0, :], ACT.Copy))
                act.activation(ENB[:, TP:T], K[:, 1, 0:TS], ACT.Copy).then_inc(s_enb, 1)
                copy_head(act, st, s_nd, h + 2 * HEADS, h + 1)
                st.add(act.activation(DD[:, 0:TP], J[:, 0, :], ACT.Abs))
                act.activation(DD[:, TP:T], J[:, 1, 0:TS], ACT.Abs).then_inc(s_dabs, 1)
                act.wait_ge(s_dmax, h + 1)
                act.activation(DD, DD, ACT.Square, scale=float(EPS) ** 0.5).then_inc(s_d2, 1)
                act.wait_ge(s_oc, h + 2 * HEADS + 1)
                act.activation(OSQ, OC, ACT.Square).then_inc(s_osq, 1)
                act.wait_ge(s_nv, h + 1)
                st.done(act.activation(NR[:, :], NV[:, :], ACT.Ln))
                act.activation(NR[:, :], NR[:, :], ACT.Exp, scale=-0.5).then_inc(s_hr0, 1)
                mixed_high(act, h + 2 * HEADS, h + 4)
            st.end(HEADS)

        def layer1_act(act):
            st = steps["act"]
            norm_act(act, 2, Turn(R_N2))
            norm_high(act, 2, MOD_TILES)
            small_act(act, st)
            gla_act(act, st)
            mlstm_act(act, st)
            out_act(act, W_OUT1, R_OUT1, 3)
            hi_of(act, Turn(W_FFN1 + 1))
            norm_act(act, 3, Turn(R_N3))
            norm_high(act, 3, MOD_TILES + 3 * KD)
            ffn_act(act, W_FFN1, R_FFN1, 4, last=True)
            norm_act(act, 4, Turn(R_N4))
            for b in range(NB + 1):
                n = P if b < NB else TS
                p = Turn(R_Y, b)
                act.wait_ge(s_yt, b + 1)
                if b >= 2:
                    act.wait_ge(s_yout[b % 2], 16 * (b // 2))
                st.add(act.activation(YR[b % 2][0:n, 0:512], PS[p.slot][0:n, 0, :], ACT.Copy))
                act.activation(YR[b % 2][0:n, 512:D], PS[p.slot][0:n, 1, :], ACT.Copy).then_inc(s_yr, 1)
                act.wait_ge(s_yr, b + 1)
                act.sem_inc(s_free[p.slot], 1)

        def small_dve(dve, st):
            H4 = slice(0, HEADS)
            dve.wait_ge(s_area, AREA_SMALL)
            dve.wait_ge(s_rows1, 1)
            dve.wait_ge(s_small, 32)
            st.add(dve.tensor_scalar(RI[H4], RI[H4], IF_BIAS[:, 0:1], None, ALU.add))
            dve.tensor_scalar(RF[H4], RF[H4], IF_BIAS[:, 1:2], None, ALU.add).then_inc(s_rabs, 1)
            dve.wait_ge(s_rabs, 1)
            dve.wait_ge(s_rln, 1)
            st.done(dve.scalar_tensor_tensor(out=RF[H4], in0=RF[H4], scalar=0.0, in1=RA[H4], op0=ALU.min,
                                             op1=ALU.subtract))
            st.add(dve.tensor_tensor_scan(RM[H4, 0:TP], RF[H4, 0:TP], RI[H4, 0:TP], 0.0, ALU.add, ALU.max))
            st.add(dve.tensor_tensor_scan(RM[H4, TP:T], RF[H4, TP:T], RI[H4, TP:T], M0[:, 0:1], ALU.add, ALU.max))
            st.done(dve.tensor_tensor_scan(RB[H4], MASKR[H4], RF[H4], 0.0, ALU.mult, ALU.add))
            st.done(dve.tensor_tensor(RA[H4], RB[H4], RM[H4], ALU.subtract))
            dve.tensor_tensor(RB[H4], RI[H4], RB[H4], ALU.subtract).then_inc(s_rg, 1)
            dve.wait_ge(s_rg, 1)
            st.add(dve.tensor_copy(RI[H4, 0:P], RA[H4, 0:P]))
            st.add(dve.tensor_tensor(RI[H4, P:TP].rearrange("p (b c) -> p b c", c=P),
                                     RA[H4, P:TP].rearrange("p (b c) -> p b c", c=P),
                                     RM[H4, P - 1:TP - P:P].unsqueeze(2).to_broadcast([HEADS, NB - 1, P]), ALU.add))
            dve.tensor_scalar(RI[H4, TP:T], RA[H4, TP:T], M0[:, 0:1], None, ALU.add).then_inc(s_rwin, 1)
            for i in range(2):
                p = Turn(R_G, i)
                dve.wait_ge(s_gab, i + 1)
                dve.wait_ge(s_cum, i)
                dve.tensor_scalar(pair(GX), ring(p), col2("gla_b_gate", i), 0.0, ALU.add,
                                  ALU.min).then_inc(s_free[p.slot], 1)
                ring_done(dve, p)
                dve.wait_ge(s_gln, i + 1)
                st.done(dve.tensor_tensor(GX, GX, GA, ALU.subtract))
                dve.tensor_tensor_scan(CUM[:, i, :], MASK64, GX, 0.0, ALU.mult, ALU.add).then_inc(s_cum, 1)
            dve.wait_ge(s_cum, 2)

        def gla_head_dve(dve, st, i, j):
            n = 2 * i + j
            dve.wait_ge(s_gsc, n + 1)
            dve.wait_ge(s_got, n)
            dve.sem_inc(s_seen, 1)
            st.add(dve.copy_predicated(AG[:, 0:NB, :], CHUNK_MASK.unsqueeze(1).to_broadcast([P, NB, P]),
                                       J[:, 0, :].rearrange("p (b c) -> p b c", b=NB)))
            dve.copy_predicated(AG[0:TS, NB, 0:TS], CHUNK_MASK[0:TS, 0:TS], J[0:TS, 1, 0:TS]).then_inc(s_gatt, 1)

        def gla_states_dve(dve, st, i, j):
            n = 2 * i + j
            r = slice(64 * j, 64 * j + 64)
            dve.wait_ge(s_gkv, n + 1)
            st.done(dve.tensor_copy(SG8[:, 0, :], K[:, 0, 0:P]))
            for c in range(1, 2 * NB):
                last = c == 2 * NB - 1
                q = r if last else slice(0, P)
                st.done(dve.scalar_tensor_tensor(
                    out=SGF[q] if last else SG8[:, c, :], in0=SG8[q, c - 1, :], scalar=EL[q, c:c + 1],
                    in1=(K, J)[c % 2][q, 0, (c // 2) * P:(c // 2 + 1) * P], op0=ALU.mult, op1=ALU.add))
            dve.wait_ge(s_gs0, 16 * i + 16)
            dve.scalar_tensor_tensor(out=SGN[r], in0=SG0[r], scalar=EL[r, 8:9], in1=K[r, 1, 0:P],
                                     op0=ALU.mult, op1=ALU.add).then_inc(s_gst, 1)

        def low_of_head(dve, n, tile):
            dve.wait_ge(s_gah, n + 1)
            dve.tensor_tensor(GL[:, tile, :], OB, GH[:, tile, :].bitcast(F32), ALU.subtract).then_inc(s_glo, 1)

        def gla_dve(dve, st):
            dve.wait_ge(s_area, AREA_GLA)
            with dve.Fori(0, 2) as i:
                st.loop(i, DVE_PAIR)

                def w(j):
                    return Turn(W_GLA, j, 6, i)

                def r(j):
                    return Turn(R_GLA, j, 6, i)

                cum = CUM[:, i, 0:TP].rearrange("p (c l) -> p c l", l=64)
                end = CUM[:, i, 63:TP:64].unsqueeze(2).to_broadcast([P, 8, 64])
                end_s = CUM[:, i, T - 1:T].to_broadcast([P, TS])
                chunks = lambda a: a[:, 0:TP].rearrange("p (c l) -> p c l", l=64)
                dve.wait_ge(s_osq, 2 * i + HEADS)
                dve.wait_ge(s_o, 2 * i + HEADS)
                st.wait()
                st.add(dve.scalar_tensor_tensor(out=chunks(CR), in0=end, scalar=-0.5, in1=cum, op0=ALU.mult, op1=ALU.add))
                st.add(dve.scalar_tensor_tensor(out=CR[:, TP:T], in0=end_s, scalar=-0.5, in1=CUM[:, i, TP:T],
                                                op0=ALU.mult, op1=ALU.add))
                st.add(dve.tensor_tensor(chunks(LC), end, cum, ALU.subtract))
                dve.tensor_tensor(LC[:, TP:T], end_s, CUM[:, i, TP:T], ALU.subtract).then_inc(s_cr, 1)
                lo_of(dve, w(1))
                dve.wait_ge(s_ef, i + 1)
                dve.wait_ge(s_used, w(0).index + 1)
                st.add(dve.scalar_tensor_tensor(out=pair(EK4), in0=ring(r(0)), scalar=GLA_SCALE, in1=pair(EK4),
                                                op0=ALU.mult, op1=ALU.mult))
                dve.scalar_tensor_tensor(out=pair(EK1), in0=ring(r(0)), scalar=GLA_SCALE, in1=pair(EK1),
                                         op0=ALU.mult, op1=ALU.mult).then_inc(s_free[r(0).slot], 1)
                ring_done(dve, r(0))
                dve.sem_inc(s_k4, 1)
                lo_of(dve, w(2))
                dve.wait_ge(s_used, w(1).index + 1)
                dve.wait_ge(s_got, 2 * i)
                for j in range(2):
                    q = slice(64 * j, 64 * j + 64)
                    for dst, f in ((Q1[j], EQ1), (Q3[j], EQ3)):
                        ins = dve.tensor_tensor(pair(dst)[q], PS[r(1).slot][q, :, 0:HALF], pair(f)[q], ALU.mult)
                        if j and f is EQ3:
                            ins.then_inc(s_free[r(1).slot], 1)
                        else:
                            st.add(ins)
                ring_done(dve, r(1))
                dve.sem_inc(s_q3, 1)
                lo_of(dve, w(3))
                dve.wait_ge(s_gsout, 32 * i)
                gla_head_dve(dve, st, i, 0)
                lo_of(dve, w(4))
                gate_dve(dve, w(3), r(3), HEADS + 2 * i)
                lo_of(dve, w(5))
                for j in range(2):
                    n = 2 * i + j
                    gla_states_dve(dve, st, i, j)
                    if j:
                        gate_dve(dve, w(5), r(5), n + HEADS)
                    center(dve, st, n + HEADS)
                    finish_head(dve, st, n + HEADS, HGAIN[:, ds(n + 4, 1)])
                    low_of_head(dve, n + KD + DONE0, n)
                    if not j:
                        lo_of(dve, w(6))
                        gla_head_dve(dve, st, i, 1)
            st.end(2)

        def mlstm_dve(dve, st):
            dve.wait_ge(s_area, AREA_ML)
            with dve.Fori(0, HEADS) as h:
                st.loop(h, DVE_ML)

                def w(j):
                    return Turn(W_ML, j, 2, h)

                def r(j):
                    return Turn(R_ML, j, 4, h)

                lo_of(dve, w(1))
                dve.wait_ge(s_ba, h + 1)
                dve.wait_ge(s_kw, h)
                dve.wait_ge(s_am, h)
                for b in range(NB):
                    st.add(dve.scalar_tensor_tensor(out=EW[:, b, :], in0=K[:, 0, b * P:(b + 1) * P],
                                                    scalar=GTOK[:, b, ds(h, 1)], in1=NEG, op0=ALU.add, op1=ALU.add))
                dve.scalar_tensor_tensor(out=EW[0:TS, NB, 0:TS], in0=K[0:TS, 1, 0:TS],
                                         scalar=GTOK[0:TS, NB, ds(h, 1)], in1=NEG[0:TS, 0:TS], op0=ALU.add,
                                         op1=ALU.add).then_inc(s_ex, 1)
                ring_done(dve, r(0))
                convolve(dve, st, UP, UC, cols2("mlstm_conv_w", 16).rearrange("p (t k) -> p t k", k=4),
                         cols2("mlstm_conv_b", 4), h, s_uc, (s_mkt, h))
                dve.wait_ge(s_uc, h + 1)
                dve.wait_ge(s_uct, h + 1)
                dve.scalar_tensor_tensor(out=UC, in0=UT, scalar=1.0, in1=UC, op0=ALU.add,
                                         op1=ALU.mult).then_inc(s_ucs, 1)
                lo_of(dve, w(2))
                dve.wait_ge(s_nd, h)
                dve.tensor_copy(CN0[:, P:2 * P], col2("state_mlstm_n", h).to_broadcast([P, P])).then_inc(s_cn0, 1)
                dve.wait_ge(s_msc, h + 1)
                dve.wait_ge(s_ew, h + 1)
                st.add(dve.tensor_tensor(AM[:, 0:NB, :], J4(K[:, 0, :]), EW[:, 0:NB, :], ALU.mult))
                dve.tensor_tensor(AM[0:TS, NB, 0:TS], K[0:TS, 1, 0:TS], EW[0:TS, NB, 0:TS],
                                  ALU.mult).then_inc(s_am, 1)
                dve.wait_ge(s_mkt, h + 1)
                dve.wait_ge(s_cu, h)
                for b in range(NB):
                    st.add(dve.tensor_scalar(KW[:, b, :], J[:, 0, b * P:(b + 1) * P], EW[:, b, P - 1:P],
                                             0.5 * RET_SCALE, ALU.mult, ALU.mult))
                dve.tensor_scalar(KW[0:TS, NB, :], J[0:TS, 1, 0:P], EW[0:TS, NB, TS - 1:TS], 0.5 * RET_SCALE,
                                  ALU.mult, ALU.mult).then_inc(s_kw, 1)
                dve.wait_ge(s_wb, h + 1)
                dve.wait_ge(s_qm, h + 1)
                dve.tensor_tensor(QI, QM, WB, ALU.mult).then_inc(s_qi, 1)
                dve.wait_ge(s_cu, h + 1)
                dve.wait_ge(s_cout, 32 * h)
                st.done(dve.tensor_copy(CN[:, 0, :], K[:, 0, 0:256]))
                for b in range(1, NB):
                    st.done(dve.scalar_tensor_tensor(out=CN[:, b, :], in0=CN[:, b - 1, :],
                                                     scalar=WB[:, b * P + P - 1:b * P + P],
                                                     in1=K[:, b // 2, (b % 2) * 256:(b % 2) * 256 + 256],
                                                     op0=ALU.mult, op1=ALU.add))
                dve.wait_ge(s_c0, 16 * h + 16)
                dve.wait_ge(s_cn0, h + 1)
                dve.scalar_tensor_tensor(out=CNS, in0=CN0, scalar=WB[:, T - 1:T], in1=J[:, 1, 0:256],
                                         op0=ALU.mult, op1=ALU.add).then_inc(s_cn, 1)
                dve.wait_ge(s_cn, h + 1)
                st.add(dve.tensor_copy(OV[:, 1, ds(h, 1)], CN[:, NB - 1, P:P + 1]))
                st.add(dve.tensor_copy(OV[:, 1, ds(h + 4, 1)], CNS[:, P:P + 1]))
                ring_done(dve, r(1))
                dve.wait_ge(s_ob, h + 2 * HEADS)
                st.done(dve.tensor_scalar(SG, THG, 1.0, None, ALU.add))
                dve.wait_ge(s_dabs, h + 1)
                dve.tensor_tensor(DD, DD, ENB, ALU.max).then_inc(s_dmax, 1)
                center(dve, st, h + 2 * HEADS)
                dve.wait_ge(s_var, h + 2 * HEADS + 1)
                dve.wait_ge(s_d2, h + 1)
                st.add(dve.tensor_tensor(NV[:, 0:TP], K[:, 0, :], DD[:, 0:TP], ALU.add))
                dve.tensor_tensor(NV[:, TP:T], K[:, 1, 0:TS], DD[:, TP:T], ALU.add).then_inc(s_nv, 1)
                dve.wait_ge(s_nv, h + 1)
                finish_rstd(dve, st, h + 2 * HEADS, HGAIN[:, ds(h + 8, 1)])
                low_of_head(dve, h + KD + HEADS + DONE0, h + 4)
            st.end(HEADS)

        def J4(a):
            return a.rearrange("p (b c) -> p b c", b=NB)

        def layer1_dve(dve):
            st = steps["dve"]
            norm_dve(dve, 2, Turn(R_N2), MOD_TILES, MOD_TILES + KD, col1("norm_mix_g", KD, KD))
            lo_of(dve, Turn(W_GLA))
            small_dve(dve, st)
            gla_dve(dve, st)
            mlstm_dve(dve, st)
            out_dve(dve, W_OUT1, R_OUT1, MOD_TILES + 2 * KD, 3)
            lo_of(dve, Turn(W_FFN1 + 1))
            norm_dve(dve, 3, Turn(R_N3), MOD_TILES + 3 * KD, MOD_TILES + 4 * KD, col1("norm_ffn_g", KD, KD))
            ffn_dve(dve, W_FFN1, R_FFN1, DONE0, MOD_TILES + 5 * KD, 4, None, last=True)
            norm_rstd(dve, 4, Turn(R_N4))
            for k in range(KD):
                dve.scalar_tensor_tensor(out=Y[:, k, :], in0=X[:, k, :], scalar=col1("final_norm_g", k),
                                         in1=NR[:, :], op0=ALU.mult, op1=ALU.mult).then_inc(s_y, 1)
            dve.wait_ge(s_ovt, DEPTH)
            dve.tensor_copy(OVR[:, :, :], K[0:32, 0, 0:DEPTH * P].rearrange("p (l c) -> p l c", l=DEPTH)
                            ).then_inc(s_ov, 1)

        DONE0 = sum(FFN_CUTS)
        LAST_OUT = 3 * KD + 2 * sum(FFN_CUTS) - KD

        rows, ACT_ROWS = list(row_loads()), 11
        block = ctx.enter_context(nc.Block())

        @block.sync
        def _(sp):
            sp.dma_start(IDENT, t["constants"][:, C_ID:C_ID + P]).then_inc(s_id, 16)
            for dst, src in rows[ACT_ROWS:]:
                sp.dma_start(dst, src).then_inc(s_rows, 16)
            sp.dma_start(XROW[:, :, :], t["x_prompt"][0].rearrange("(b p) d -> p b d", p=P)).then_inc(s_x, 16)
            sp.dma_start(XSROW[0:TS, :], t["x_sample"][0]).then_inc(s_x, 16)
            for g in range(MG_DIRECT):
                load_early(sp, g)
            sp.dma_start(CST[:, C_ID + P:C_ALL], t["constants"][:, C_ID + P:C_ALL]).then_inc(s_cst, 16)
            with sp.Fori(0, HEADS) as h:
                for j, (_, a) in enumerate(A_ORDER):
                    load_weight(sp, Turn(W_HEAD, j, 6, h), t["a_w_in"][0].rearrange("(k p) m -> p k m", p=P),
                                lambda: h * P + a)
                    if j == 1:
                        sp.wait_ge(s_clear, 1)
                        sp.wait_ge(s_ot, h)
                        sp.dma_start(S0[:, :], t["state_ret"][0, 0, h]).then_inc(s_s0, 16)
                        sp.wait_ge(s_gi, h)
                        for part in range(2):
                            for head in range(2):
                                sp.dma_start(
                                    GW[part][64 * head:64 * head + 64, 64 * head:64 * head + 64],
                                    t["lru_gate_w"][0, 2 * h + head, :, 64 * part:64 * part + 64],
                                ).then_inc(s_gw, 16)
                sp.wait_ge(s_st, h + 1)
                sp.dma_start(out["ret_p"][0, 0, h], ST[:, NB - 1, :]).then_inc(s_sout, 16)
                sp.dma_start(out["ret_s"][0, 0, h], SN[:, :]).then_inc(s_sout, 16)
            out_loads(sp, W_OUT0, t["a_w_out"][0])
            ffn_loads(sp, 0, W_FFN0)
            layer1_sync(sp)

        @block.gpsimd
        def _(pool):
            for a, v in ((ONES[:, :], 1.0), (MEAN[:, :], 1.0 / P), (EPSC[:, :], EPS)):
                ins = pool.memset(a, v)
            ins.then_inc(s_init, 1)
            load_mod(pool, 0, lambda: MG_DIRECT)
            pool.dma_start(IF_BIAS[:, :], t["mlstm_b_if"].rearrange("a (two h) -> (a h) two", two=2),
                           allow_slow_non_contiguous=True).then_inc(s_small, 16)
            pool.dma_start(M0[:, :], t["state_mlstm_m"][0].rearrange("a h -> h a"),
                           allow_slow_non_contiguous=True).then_inc(s_small, 16)
            pool.wait_ge(s_modu, 1)
            load_mod(pool, 0, lambda: MG_DIRECT + 1)
            pool.wait_ge(s_direct, MG_DIRECT)
            for a in (XB[:, 0:PAD], XB[:, TC + PAD - 1:TC + PAD], GW[0], GW[1]):
                ins = pool.memset(a, 0.0)
            ins.then_inc(s_clear, 1)
            with pool.Fori(MG_NORM, MOD_TILES // 2) as g:
                pool.wait_ge(s_modu, g - MG_DIRECT)
                pool.sem_inc(s_half, 1)
                load_mod(pool, 0, lambda: g)
            pool.wait_ge(s_modu, MOD_TILES // 2 - MG_DIRECT)
            for half in range(2):
                load_half(pool, lambda: 0, half)
            ffn_pool(pool, KD, True)
            layer1_pool(pool)

        @block.tensor
        def _(pe):
            pe.wait_ge(s_id, 16)
            pe.wait_ge(s_rows, 16 * len(rows))
            o = 0
            for r, n in enumerate((MOD_ROWS, R1_ALL, R2_ALL)):
                ins = pe.transpose(PS[0][:, 0, o:o + n], ROWS[0:n, r, :], IDENT[0:n, 0:n])
                o += n
            ins.then_inc(s_tr, 1)
            pe.wait_ge(s_x, 32)
            for k in range(KD):
                p = Turn(R_X, k)
                pe.wait_ge(s_free[p.slot], p.before)
                for b in range(NB):
                    pe.transpose(PS[p.slot][:, 0, b * P:(b + 1) * P], XROW[:, b, k * P:(k + 1) * P], IDENT)
                pe.transpose(PS[p.slot][:, 1, 0:TS], XSROW[0:TS, k * P:(k + 1) * P],
                             IDENT[0:TS, 0:TS]).then_inc(s_tr, 1)
            pe.wait_ge(s_init, 1)
            pe.wait_ge(s_cs, 1)
            for g in (0, 1, 6, 2, 7, 3, 4, 5):
                if g < MG_PE:
                    mod_early(pe, g)
                elif g < MG_DIRECT:
                    pe.wait_ge(s_dparts, g - MG_PE + 1)
                    sum_parts(pe, DACC[g - MG_PE], J[:, 1, 4 * g:4 * g + 4]).then_inc(s_direct, 1)
                else:
                    mod_next(pe, g, J[:, 1, 4 * g:4 * g + 4])
                if g == 0:
                    norm_pe(pe, 0, Turn(R_N0))

            with pe.Fori(0, HEADS) as h:
                def item(j, pj, normed=None):
                    project(pe, Turn(W_HEAD, j, 6, h), Turn(R_HEAD, pj, 8, h), normed=normed)

                item(0, 0, 0)
                item(1, 1)
                pe.wait_ge(s_kt, h + 1)
                pe.wait_ge(s_ob, h)
                transpose_blocks(pe, KT, K[:, 0, :], K[0:TS, 1, 0:P]).then_inc(s_ktr, 1)
                pe.wait_ge(s_oc, h)
                mod_group(pe, 3 * h + MG_NORM)
                item(2, 2)
                pe.wait_ge(s_qt, h + 1)
                pe.wait_ge(s_mod, 3 * h + MG_NORM + 1)
                for b in range(NB):
                    pe.matmul(J[:, 0, b * P:(b + 1) * P], KT[:, b * P:(b + 1) * P], QT[:, b * P:(b + 1) * P],
                              start=True, stop=True)
                pe.matmul(J[0:TS, 1, 0:TS], KT[:, TP:T], QT[:, TP:T], start=True, stop=True).then_inc(s_sc, 1)
                item(3, 3)
                ring_done(pe, Turn(R_HEAD, 2, 8, h))
                pe.wait_ge(s_kd, h + 1)
                transpose_blocks(pe, VT, K[:, 0, :], K[0:TS, 1, 0:P]).then_inc(s_vtr, 1)
                pe.wait_ge(s_att, h + 1)
                mod_group(pe, 3 * h + MG_NORM + 1)
                item(4, 4)
                pe.wait_ge(s_vtok, h + 1)
                pe.wait_ge(s_mod, 3 * h + MG_NORM + 2)
                for b in range(NB):
                    pe.matmul(J[:, 0, b * P:(b + 1) * P], KDT[:, b, :], VTOK[:, b, :], start=True, stop=True)
                pe.matmul(J[:, 1, TS:TS + P], KDT[0:TS, NB, :], VTOK[0:TS, NB, :],
                          start=True, stop=True).then_inc(s_kv, 1)
                pe.wait_ge(s_xc, h + 1)
                pe.wait_ge(s_gw, 64 * h + 64)
                for part, s_gate in ((0, s_gr), (1, s_gi)):
                    p = Turn(R_HEAD, 5 + part, 8, h)
                    pe.wait_ge(s_free[p.slot], p.before)
                    for half in range(2):
                        ins = pe.matmul(PS[p.slot][:, half, 0:TC // 2], GW[part],
                                        XC[:, half * (TC // 2):(half + 1) * (TC // 2)], start=True, stop=True)
                    ins.then_inc(s_gate, 1)
                pe.wait_ge(s_st, h + 1)
                pe.wait_ge(s_qd, h + 1)
                for b in range(NB):
                    pe.matmul(K[:, 0, b * P:(b + 1) * P], VTOK[:, b, :], ATT[:, b, :], start=True, stop=(b == 0))
                    if b:
                        pe.matmul(K[:, 0, b * P:(b + 1) * P], ST[:, b - 1, :], QD[:, b * P:(b + 1) * P],
                                  start=False, stop=True)
                pe.wait_ge(s_s0, 16 * h + 16)
                pe.matmul(K[:, 1, P:P + TS], VTOK[0:TS, NB, :], ATT[0:TS, NB, 0:TS], start=True, stop=False)
                pe.matmul(K[:, 1, P:P + TS], S0, QD[:, TP:T], start=False, stop=True).then_inc(s_ot, 1)
                item(5, 7)
                head_mean(pe, OT, s_o, h)
                head_var(pe, OSQ, s_osq, h)
                mod_group(pe, 3 * h + MG_NORM + 2)
            pe.wait_ge(s_glo, KD)
            out_pe(pe, W_OUT0, R_OUT0, KD, 20)
            norm_pe(pe, 1, Turn(R_N1))
            ffn_pe(pe, W_FFN0, R_FFN0, 0, 24, 1)
            layer1_pe(pe)

        @block.scalar
        def _(act):
            steps["act"] = Steps(act, s_act)
            st = steps["act"]
            for dst, src in rows[:ACT_ROWS]:
                act.dma_start(dst, src).then_inc(s_rows, 16)
            act.wait_ge(s_cols, 1)
            act.activation(CTMP[:, :, :], cols1("c_prompt", 2 * KD).rearrange("p (c k) -> p c k", c=2),
                           ACT.Tanh, scale=0.5).then_inc(s_cth, 1)
            st.done(act.activation(SP[:, 0, :], cols1("lru_lambda", 4), ACT.Abs))
            act.activation(SP[:, 0, :], SP[:, 0, :], ACT.Exp, scale=-1.0).then_inc(s_cth, 1)
            for k in range(KD):
                p = Turn(R_X, k)
                act.wait_ge(s_tr, k + 2)
                st.add(act.activation(X[:, k, 0:TP], PS[p.slot][:, 0, :], ACT.Copy))
                act.activation(X[:, k, TP:T], PS[p.slot][:, 1, 0:TS], ACT.Copy).then_inc(s_free[p.slot], 1)
                square(act, 0, k, p, k % 2)
            norm_act(act, 0, Turn(R_N0))
            norm_high(act, 0, 0)
            act.wait_ge(s_cst, 16)
            hi_of(act, Turn(W_HEAD))
            with act.Fori(0, HEADS) as h:
                st.loop(h, ACT_HEAD)

                def w(j):
                    return Turn(W_HEAD, j, 6, h)

                def r(j):
                    return Turn(R_HEAD, j, 8, h)

                hi_of(act, w(1))
                hi_of(act, w(2))
                act.wait_ge(s_ktr, h + 1)
                act.wait_ge(s_kv, h)
                st.add(act.activation(KDT[:, 0:NB, :], K[:, 0, :].rearrange("p (b c) -> p b c", b=NB), ACT.Copy,
                                      scale=CST[:, ds(2 * h + C_KD, 1)]))
                act.activation(KDT[0:TS, NB, :], K[0:TS, 1, 0:P], ACT.Copy,
                               scale=CST[0:TS, ds(2 * h + C_KD + 1, 1)]).then_inc(s_kd, 1)
                hi_of(act, w(3))
                act.wait_ge(s_used, w(2).index + 1)
                act.activation(pair(VT), ring(r(2)), ACT.Copy).then_inc(s_free[r(2).slot], 1)
                hi_of(act, w(4))
                act.wait_ge(s_used, w(3).index + 1)
                act.wait_ge(s_xc, h)
                st.done(act.activation(XB[:, SC:SC + PAD], cols1("state_lru_conv", 12).rearrange(
                    "p (t k) -> p t k", k=4)[:, :, h], ACT.Copy))
                fill_padded(act, st, XB, r(3))
                act.wait_ge(s_vtr, h + 1)
                act.wait_ge(s_ot, h)
                st.add(act.activation(VTOK[:, 0:NB, :], K[:, 0, :].rearrange("p (b c) -> p b c", b=NB), ACT.Copy))
                act.activation(VTOK[0:TS, NB, :], K[0:TS, 1, 0:P], ACT.Copy).then_inc(s_vtok, 1)
                hi_of(act, w(5))
                conv_columns(act, st, XB, 0, h)
                act.wait_ge(s_used, w(4).index + 1)
                act.wait_ge(s_ob, h)
                act.activation(pair(THG), ring(r(4)), ACT.Tanh, scale=0.5).then_inc(s_thg, 1)
                act.wait_ge(s_oa, h)
                for dst, part, s_gate in ((TR, 0, s_gr), (TI, 1, s_gi)):
                    act.wait_ge(s_gate, h + 1)
                    act.activation(dst.rearrange("p (a b) -> p a b", a=2), ring(r(5 + part), TC // 2), ACT.Tanh,
                                   bias=BRH[:, ds(h + 4 * part, 1)], scale=0.5).then_inc(s_free[r(5 + part).slot], 1)
                ring_done(act, r(5))
                st.done(act.activation(LA, TR, ACT.Exp, bias=SP[:, 4, ds(h, 1)], scale=SP[:, 4, ds(h, 1)]))
                st.add(act.activation(LTH, TR, ACT.Tanh, bias=SP[:, 5, ds(h, 1)], scale=SP[:, 5, ds(h, 1)]))
                act.activation(LA2, LA, ACT.Square).then_inc(s_la, 1)
                copy_head(act, st, s_ot, h, h + 1)
                act.wait_ge(s_lq, h + 1)
                act.activation(LS, LA2, ACT.Sqrt, scale=0.25).then_inc(s_ls, 1)
                hi_of(act, w(6))
                act.wait_ge(s_used, w(5).index + 1)
                act.activation(pair(GX2), ring(r(7)), ACT.Square).then_inc(s_gx2, 1)
                act.wait_ge(s_oc, h + 1)
                act.activation(OSQ, OC, ACT.Square).then_inc(s_osq, 1)
                act.wait_ge(s_gt2, h + 1)
                act.activation(GT, GT, ACT.Tanh, scale=GELU_A).then_inc(s_gth, 1)
                act.wait_ge(s_oa, h + 1)
                act.activation(GH[:, h, :], OA, ACT.Copy).then_inc(s_gah, 1)
                head_rstd(act, st, h)
                act.wait_ge(s_ob, h + 1)
                act.activation(GH[:, 4 + h, :], OB, ACT.Copy).then_inc(s_gah, 1)
            st.end(HEADS)
            out_act(act, W_OUT0, R_OUT0, 1)
            hi_of(act, Turn(W_FFN0 + 1))
            norm_act(act, 1, Turn(R_N1))
            norm_high(act, 1, 3 * KD)
            ffn_act(act, W_FFN0, R_FFN0, 2)
            layer1_act(act)

        @block.vector
        def _(dve):
            steps["dve"] = Steps(dve, s_dve)
            st = steps["dve"]
            dve.sem_inc(s_lo, 1)
            dve.wait_ge(s_tr, 1)
            dve.tensor_copy(COLS[:, :], PS[0][:, 0, 0:MOD_ROWS + R1_ALL + R2_ALL]).then_inc(s_free[0], 1)
            ring_done(dve, Turn(R_PAR))
            dve.tensor_scalar(BRH[:, :], cols1("lru_gate_b", 8), 0.5, None, ALU.mult).then_inc(s_cols, 1)
            st.add(dve.tensor_scalar(HGAIN[:, 0:4], cols1("ret_gn_g", 4), 0.5, None, ALU.mult))
            st.add(dve.tensor_scalar(HGAIN[:, 4:8], cols2("gla_gn_g", 4), 0.5, None, ALU.mult))
            st.add(dve.tensor_scalar(HGAIN[:, 8:12], cols2("mlstm_gn_g", 4), 0.5, None, ALU.mult))
            dve.wait_ge(s_cth, 1)
            c = cols1("c_prompt", 2 * KD).rearrange("p (c k) -> p c k", c=2)
            st.done(dve.scalar_tensor_tensor(out=CS[:, :, :], in0=CTMP[:, :, :], scalar=1.0, in1=c,
                                             op0=ALU.add, op1=ALU.mult))
            dve.tensor_scalar(CS[:, :, :], CS[:, :, :], 0.5, None, ALU.mult).then_inc(s_cs, 1)
            clear_sum(dve)
            for k in range(KD):
                add_square(dve, 0, k, k % 2)
            for g in range(MG_PE, MG_DIRECT):
                early_parts(dve, g)
                if g == MG_PE:
                    norm_rstd(dve, 0, Turn(R_N0))
            dve.wait_ge(s_cth, 2)
            e, s, z, y = SP[:, 0, :], SP[:, 1, :], SP[:, 2, :], SP[:, 3, :]
            st.done(dve.tensor_scalar(z, e, 2.0, None, ALU.add))
            st.done(dve.reciprocal(z, z))
            st.done(dve.tensor_tensor(s, e, z, ALU.mult))
            st.done(dve.tensor_tensor(z, s, s, ALU.mult))
            st.done(dve.tensor_scalar(y, z, 1.0 / 19.0, None, ALU.mult))
            for k in range(8, 0, -1):
                st.done(dve.scalar_tensor_tensor(out=y, in0=y, scalar=1.0 / (2 * k + 1), in1=z,
                                                 op0=ALU.add, op1=ALU.mult))
            st.done(dve.scalar_tensor_tensor(out=y, in0=y, scalar=1.0, in1=s, op0=ALU.add, op1=ALU.mult))
            st.done(dve.tensor_scalar(z, cols1("lru_lambda", 4), -1.0, 0.0, ALU.mult, ALU.max))
            st.done(dve.scalar_tensor_tensor(out=y, in0=y, scalar=2.0, in1=z, op0=ALU.mult, op1=ALU.add))
            st.add(dve.tensor_scalar(SP[:, 4, :], y, -4.0, None, ALU.mult))
            st.done(dve.tensor_scalar(SP[:, 5, :], y, 4.0, None, ALU.mult))
            dve.wait_ge(s_direct, MG_DIRECT)
            dve.wait_ge(s_modu, MG_NORM - MG_DIRECT)
            mod_add(dve, J[:, 1, 0:4 * MG_NORM], 0, MG_NORM).then_inc(s_mod, MG_NORM)
            dve.wait_ge(s_mod, MG_NORM)
            norm_dve(dve, 0, Turn(R_N0), 0, KD, cols1("norm_mix_g", KD), rstd=False)
            dve.wait_ge(s_cst, 16)
            dve.wait_ge(s_clear, 1)
            lo_of(dve, Turn(W_HEAD))
            with dve.Fori(0, HEADS) as h:
                st.loop(h, DVE_HEAD)

                def w(j):
                    return Turn(W_HEAD, j, 6, h)

                def r(j):
                    return Turn(R_HEAD, j, 8, h)

                def rotate(j, dst, ready):
                    dve.wait_ge(s_used, w(j).index + 1)
                    dve.wait_ge(s_kt if j else s_qt, h + j)
                    p = PS[r(j).slot]
                    st.add(dve.tensor_tensor(pair(ROTA), ring(r(j)), pair(COS), ALU.mult))
                    st.add(dve.tensor_tensor(pair(ROTB)[0:64], p[64:P, :, 0:HALF], pair(SIN)[64:P], ALU.mult))
                    dve.tensor_tensor(pair(ROTB)[64:P], p[0:64, :, 0:HALF], pair(SIN)[0:64],
                                      ALU.mult).then_inc(s_free[r(j).slot], 1)
                    ring_done(dve, r(j))
                    dve.wait_ge(s_sc, h)
                    dve.tensor_tensor(dst, ROTA, ROTB, ALU.add).then_inc(ready, 1)

                lo_of(dve, w(1))
                rotate(0, KT, s_kt)
                lo_of(dve, w(2))
                rotate(1, QT, s_qt)
                dve.wait_ge(s_qt, h + 1)
                dve.wait_ge(s_ot, h)
                blk = lambda a: a[:, 0:TP].rearrange("p (b c) -> p b c", b=NB)
                st.add(dve.tensor_tensor(blk(QD), blk(QT), QDEC[:, h, :].unsqueeze(1).to_broadcast([P, NB, P]),
                                         ALU.mult))
                dve.tensor_tensor(QD[:, TP:T], QT[:, TP:T], QDEC[:, h, 0:TS], ALU.mult).then_inc(s_qd, 1)
                mod_read(dve, 3 * h + MG_NORM)
                lo_of(dve, w(3))
                dve.wait_ge(s_sc, h + 1)
                st.add(dve.tensor_tensor(ATT[:, 0:NB, :], blk(J[:, 0, :]),
                                         DECAY[:, h, :].unsqueeze(1).to_broadcast([P, NB, P]), ALU.mult))
                dve.tensor_tensor(ATT[0:TS, NB, 0:TS], J[0:TS, 1, 0:TS], DECAY[0:TS, h, 0:TS],
                                  ALU.mult).then_inc(s_att, 1)
                lo_of(dve, w(4))
                ring_done(dve, r(3))
                convolve(dve, st, XB, XC, cols1("lru_conv_w", 16).rearrange("p (t k) -> p t k", k=4),
                         cols1("lru_conv_b", 4), h, s_xc, (s_gi, h))
                mod_read(dve, 3 * h + MG_NORM + 1)
                lo_of(dve, w(5))
                dve.wait_ge(s_kv, h + 1)
                dve.wait_ge(s_ot, h)
                dve.wait_ge(s_sout, 32 * h)
                st.done(dve.tensor_copy(ST[:, 0, :], J[:, 0, 0:P]))
                for b in range(1, NB):
                    st.done(dve.scalar_tensor_tensor(out=ST[:, b, :], in0=ST[:, b - 1, :],
                                                     scalar=CST[:, ds(2 * h + C_SD, 1)],
                                                     in1=J[:, 0, b * P:(b + 1) * P], op0=ALU.mult, op1=ALU.add))
                dve.wait_ge(s_s0, 16 * h + 16)
                dve.scalar_tensor_tensor(out=SN, in0=S0, scalar=CST[:, ds(2 * h + C_SD + 1, 1)],
                                         in1=J[:, 1, TS:TS + P], op0=ALU.mult, op1=ALU.add).then_inc(s_st, 1)
                gate_dve(dve, w(4), r(4), h)
                dve.wait_ge(s_la, h + 1)
                dve.scalar_tensor_tensor(out=LA2, in0=LA2, scalar=1.0, in1=LTH, op0=ALU.add,
                                         op1=ALU.mult).then_inc(s_lq, 1)
                ring_done(dve, r(6))
                st.add(dve.scalar_tensor_tensor(out=LB, in0=TI, scalar=1.0, in1=XC, op0=ALU.add, op1=ALU.mult))
                lo_of(dve, w(6))
                dve.wait_ge(s_ls, h + 1)
                st.wait()
                st.done(dve.tensor_tensor(LB, LB, LS, ALU.mult))
                st.add(dve.tensor_tensor_scan(HS[:, 0:TP], LA[:, 0:TP], LB[:, 0:TP], 0.0, ALU.mult, ALU.add))
                st.done(dve.tensor_tensor_scan(HS[:, SC:SC + TS], LA[:, SC:SC + TS], LB[:, SC:SC + TS],
                                               col1("state_lru_h", h), ALU.mult, ALU.add))
                st.add(dve.tensor_copy(OV[:, 0, ds(h, 1)], HS[:, TP - 1:TP]))
                st.add(dve.tensor_copy(OV[:, 0, ds(h + 4, 1)], HS[:, SC + TS - 1:SC + TS]))
                dve.wait_ge(s_gx2, h + 1)
                st.done(dve.tensor_scalar(GT, GX2, GELU_B, 1.0, ALU.mult, ALU.add))
                dve.tensor_tensor(pair(GT), ring(r(7)), pair(GT), ALU.mult).then_inc(s_gt2, 1)
                center(dve, st, h)
                dve.wait_ge(s_gth, h + 1)
                dve.scalar_tensor_tensor(out=pair(GX2), in0=pair(GT), scalar=1.0, in1=ring(r(7)),
                                         op0=ALU.add, op1=ALU.mult).then_inc(s_free[r(7).slot], 1)
                ring_done(dve, r(7))
                st.add(dve.scalar_tensor_tensor(out=OA[:, 0:TP], in0=GX2[:, 0:TP], scalar=0.5, in1=HS[:, 0:TP],
                                                op0=ALU.mult, op1=ALU.mult))
                dve.scalar_tensor_tensor(out=OA[:, TP:T], in0=GX2[:, TP:T], scalar=0.5, in1=HS[:, SC:SC + TS],
                                         op0=ALU.mult, op1=ALU.mult).then_inc(s_oa, 1)
                dve.wait_ge(s_gah, 2 * h + 1)
                dve.tensor_tensor(GL[:, h, :], OA, GH[:, h, :].bitcast(F32), ALU.subtract).then_inc(s_glo, 1)
                mod_read(dve, 3 * h + MG_NORM + 2)
                finish_head(dve, st, h, HGAIN[:, ds(h, 1)])
                dve.wait_ge(s_gah, 2 * h + 2)
                dve.tensor_tensor(GL[:, 4 + h, :], OB, GH[:, 4 + h, :].bitcast(F32),
                                  ALU.subtract).then_inc(s_glo, 1)
            st.end(HEADS)
            out_dve(dve, W_OUT0, R_OUT0, 2 * KD, 1, 20)
            lo_of(dve, Turn(W_FFN0 + 1))
            norm_dve(dve, 1, Turn(R_N1), 3 * KD, 4 * KD, cols1("norm_ffn_g", KD))
            ffn_dve(dve, W_FFN0, R_FFN0, 0, 5 * KD, 2, 24)
            layer1_dve(dve)



_INS = ['x_prompt', 'x_sample', 'c_prompt', 'c_sample', 'state_lru_h', 'state_lru_conv', 'state_ret', 'state_gla',
        'state_mlstm_C', 'state_mlstm_n', 'state_mlstm_m', 'state_mlstm_conv', 'w_mod', 'b_mod', 'norm_mix_g',
        'norm_ffn_g', 'w_ffn_in', 'w_ffn_out', 'final_norm_g', 'a_w_in', 'a_w_out', 'lru_conv_w', 'lru_conv_b',
        'lru_gate_w', 'lru_gate_b', 'lru_lambda', 'ret_gn_g', 'c_w_in', 'c_w_out', 'gla_w_gate', 'gla_b_gate',
        'gla_gn_g', 'mlstm_conv_w', 'mlstm_conv_b', 'mlstm_w_qk', 'mlstm_w_v', 'mlstm_b_if', 'mlstm_gn_g']
_OUTS = [('y_p', (1, TP, D)), ('y_s', (1, TS, D))] + [
    (name + group, shape) for group in ('_p', '_s') for name, shape in (
        ('lru_h', (1, 1, 512)), ('lru_conv', (1, 1, PAD, 512)), ('ret', (1, 1, HEADS, P, P)),
        ('gla', (1, 1, HEADS, 64, P)), ('C', (1, 1, HEADS, P, P)), ('n', (1, 1, HEADS, P)), ('m', (1, 1, HEADS)),
        ('conv', (1, 1, PAD, 512)))]


def kernel(**inputs):
    import concourse.bacc as _bacc
    from concourse.bass_utils import run_bass_kernel_spmd as _run

    nc = _bacc.Bacc("TRN2", target_bir_lowering=False, num_devices=1)
    arrays, ins, outs = {}, {}, {}
    for name in _INS:
        arrays["in_" + name] = np.ascontiguousarray(inputs[name])
    arrays["in_constants"] = constants()
    arrays["in_selectors"] = selectors()
    for key, a in arrays.items():
        ins[key[3:]] = nc.dram_tensor(key, a.shape, F32, kind="ExternalInput").ap()
    for name, shape in _OUTS:
        outs[name] = nc.dram_tensor("out_" + name, shape, F32, kind="ExternalOutput").ap()
    encoder(nc, ins, outs)
    r = _run(nc, [arrays], core_ids=[0])
    return tuple(r.results[0]["out_" + name] for name, _ in _OUTS)
```
